# Optimizing a Trainium2 kernel written in Bass

```python
import math
import jax
import jax.numpy as jnp
from jax import lax
import numpy as np

D_MODEL = 1024
BATCH = 1
SEQ = 1024
DEPTH = 2

GRID_W = 64
CTX_LEN = 256
N_EVEN = (DEPTH + 1) // 2
N_ODD = DEPTH // 2
D_FF = -(-(8 * D_MODEL) // (3 * 256)) * 256
NORM_EPS = 1e-6

D_HY = D_MODEL // 2
HY_ORDER = 2
HY_SHORT = 3
HY_EMB = 33
HY_BANDS = (HY_EMB - 1) // 2
HY_FILTER_ORDER = 64
HY_FAST_DECAY = 0.3
HY_SLOW_DECAY = 1.5
HY_TARGET = 1e-2

MLA_HEADS = 8
MLA_NOPE = 64
MLA_ROPE = 32
MLA_V = 64
MLA_Q_RANK = 384
MLA_KV_RANK = 256
MLA_SCALE = (MLA_NOPE + MLA_ROPE) ** -0.5
ROPE_AXIS = MLA_ROPE // 2
ROPE_BASE = 10000.0
Q_BLOCK = 128

EVEN_IN = (HY_ORDER + 1) * D_HY + MLA_Q_RANK + MLA_KV_RANK + MLA_ROPE
EVEN_MIX = D_HY + MLA_HEADS * MLA_V

D_RNN = 1280
RG_BLOCKS = 10
RG_BW = D_RNN // RG_BLOCKS
RG_CONV = 4
RG_C = 8.0

kernel_name = 'hybrid_hyena_mla_rglru_flow_block'

def rmsnorm(x, g):
    xf = x.astype(jnp.float32)
    y = xf * lax.rsqrt(jnp.mean(xf * xf, axis=-1, keepdims=True) + NORM_EPS)
    return (y * g.astype(jnp.float32)).astype(x.dtype)

def modulate(h, shift, scale):
    return h * (1.0 + scale) + shift

def depthwise_conv(u, w, b, pad_left, pad_right):
    y = lax.conv_general_dilated(u, w[:, None, :], window_strides=(1,), padding=[(pad_left, pad_right)],
                                 dimension_numbers=('NWC', 'WIO', 'NWC'), feature_group_count=u.shape[-1])
    return y + b

def swiglu(h, w_in, w_out):
    gate, up = jnp.split(h @ w_in, 2, axis=-1)
    return (jax.nn.silu(gate) * up) @ w_out

def hyena_filters(L, w1, b1, w2, b2, w3, freq):
    f32 = jnp.float32
    k = jnp.arange(L, dtype=f32)
    t = (k / max(L - 1, 1))[:, None]
    ang = (2.0 * math.pi / L) * k[:, None] * jnp.linspace(1e-4, HY_BANDS - 1, HY_BANDS, dtype=f32)[None, :]
    z = jnp.concatenate([t, jnp.cos(ang), -jnp.sin(ang)], axis=-1)
    freq = freq.astype(f32)
    h = jnp.sin(freq * (z @ w1.astype(f32) + b1.astype(f32)))
    h = jnp.sin(freq * (h @ w2.astype(f32) + b2.astype(f32)))
    h = (h @ w3.astype(f32)).reshape(L, HY_ORDER, D_HY)
    half = L // 2
    dist = jnp.abs(k - half) / max(half, 1)
    deltas = jnp.abs(jnp.linspace(math.log(HY_TARGET) / HY_SLOW_DECAY, math.log(HY_TARGET) / HY_FAST_DECAY,
                                  D_HY, dtype=f32))
    window = jnp.exp(-dist[:, None] * deltas[None, :])
    return jnp.transpose(h * window[:, None, :], (1, 0, 2))

def centred_long_conv(z, h):
    L = z.shape[1]
    n = 2 * L
    y = jnp.fft.irfft(jnp.fft.rfft(z, n=n, axis=1) * jnp.fft.rfft(h, n=n, axis=0)[None], n=n, axis=1)
    return y[:, L // 2: L // 2 + L]

def hyena_mixer(u, short_w, short_b, filt, bias):
    L = u.shape[1]
    uc = depthwise_conv(u, short_w, short_b, HY_SHORT // 2, HY_SHORT // 2).astype(jnp.float32)
    v, x1, x2 = jnp.split(uc, 3, axis=-1)
    h = hyena_filters(L, *filt)
    bias = bias.astype(jnp.float32)
    z = v
    for n, gate in enumerate((x1, x2)):
        z = gate * (centred_long_conv(z, h[n]) + bias[n] * z)
    return z.astype(u.dtype)

def rotate(x, ang):
    n = x.shape[-1] // 2
    cos, sin = jnp.cos(ang), jnp.sin(ang)
    x1, x2 = x[..., :n], x[..., n:]
    return jnp.concatenate([x1 * cos - x2 * sin, x1 * sin + x2 * cos], axis=-1).astype(x.dtype)

def axial_rope(x, ang_row, ang_col):
    half = x.shape[-1] // 2
    return jnp.concatenate([rotate(x[..., :half], ang_row), rotate(x[..., half:], ang_col)], axis=-1)

def mla_queries(u, q_norm_g, w_uq, qk_g_q):
    B, L, _ = u.shape
    q = (rmsnorm(u, q_norm_g) @ w_uq).reshape(B, L, MLA_HEADS, MLA_NOPE + MLA_ROPE)
    return rmsnorm(q[..., :MLA_NOPE], qk_g_q[:MLA_NOPE]), rmsnorm(q[..., MLA_NOPE:], qk_g_q[MLA_NOPE:])

def mla_keys(u, kv_norm_g, w_ukv, qk_g_k):
    B, L, _ = u.shape
    c_kv, k_rope = u[..., :MLA_KV_RANK], u[..., MLA_KV_RANK:]
    kv = (rmsnorm(c_kv, kv_norm_g) @ w_ukv).reshape(B, L, MLA_HEADS, MLA_NOPE + MLA_V)
    k_nope, v = kv[..., :MLA_NOPE], kv[..., MLA_NOPE:]
    return rmsnorm(k_nope, qk_g_k[:MLA_NOPE]), rmsnorm(k_rope, qk_g_k[MLA_NOPE:]), v

def attend(q_nope, q_rope, k_nope, k_rope, v):
    s = (jnp.einsum('bqhn,bkhn->bhqk', q_nope, k_nope, preferred_element_type=jnp.float32)
         + jnp.einsum('bqhr,bkr->bhqk', q_rope, k_rope, preferred_element_type=jnp.float32))
    p = jax.nn.softmax(s * MLA_SCALE, axis=-1)
    return jnp.einsum('bhqk,bkhv->bqhv', p.astype(v.dtype), v)

def attend_blocked(q_nope, q_rope, k_nope, k_rope, v):
    B, L = q_nope.shape[:2]
    nb = L // Q_BLOCK

    def blk(t):
        return jnp.swapaxes(t.reshape((B, nb, Q_BLOCK) + t.shape[2:]), 0, 1)

    out = lax.map(lambda qs: attend(qs[0], qs[1], k_nope, k_rope, v), (blk(q_nope), blk(q_rope)))
    return jnp.swapaxes(out, 0, 1).reshape(B, L, MLA_HEADS * MLA_V)

def even_mixer(h_ctx, h_lat, ang_row, ang_col, w_in, short_w, short_b, filt, f_bias,
               q_norm_g, w_uq, kv_norm_g, w_ukv, qk_g_q, qk_g_k, w_out, need_ctx):
    i_hy = (HY_ORDER + 1) * D_HY
    i_kv = i_hy + MLA_Q_RANK
    u_ctx = h_ctx @ w_in
    u_lat = h_lat @ w_in
    kn_c, kr_c, v_c = mla_keys(u_ctx[..., i_kv:], kv_norm_g, w_ukv, qk_g_k)
    kn_l, kr_l, v_l = mla_keys(u_lat[..., i_kv:], kv_norm_g, w_ukv, qk_g_k)
    kr_l = axial_rope(kr_l, ang_row, ang_col)
    qn_l, qr_l = mla_queries(u_lat[..., i_hy:i_kv], q_norm_g, w_uq, qk_g_q)
    qr_l = axial_rope(qr_l, ang_row[:, None, :], ang_col[:, None, :])
    att_l = attend_blocked(qn_l, qr_l, jnp.concatenate([kn_c, kn_l], axis=1),
                           jnp.concatenate([kr_c, kr_l], axis=1), jnp.concatenate([v_c, v_l], axis=1))
    hy_l = hyena_mixer(u_lat[..., :i_hy], short_w, short_b, filt, f_bias)
    y_lat = jnp.concatenate([hy_l, att_l], axis=-1) @ w_out
    y_ctx = None
    if need_ctx:
        B, C = h_ctx.shape[:2]
        qn_c, qr_c = mla_queries(u_ctx[..., i_hy:i_kv], q_norm_g, w_uq, qk_g_q)
        att_c = attend(qn_c, qr_c, kn_c, kr_c, v_c).reshape(B, C, MLA_HEADS * MLA_V)
        hy_c = hyena_mixer(u_ctx[..., :i_hy], short_w, short_b, filt, f_bias)
        y_ctx = jnp.concatenate([hy_c, att_c], axis=-1) @ w_out
    return y_ctx, y_lat

def rglru_gates(x, w_a, b_a, w_x, b_x, lam):
    B, L, _ = x.shape
    f32 = jnp.float32
    xb = x.reshape(B, L, RG_BLOCKS, RG_BW)
    r = jax.nn.sigmoid(jnp.einsum('blnk,nkj->blnj', xb, w_a.astype(f32)).reshape(B, L, D_RNN) + b_a.astype(f32))
    i = jax.nn.sigmoid(jnp.einsum('blnk,nkj->blnj', xb, w_x.astype(f32)).reshape(B, L, D_RNN) + b_x.astype(f32))
    log_a = -RG_C * r * jax.nn.softplus(-lam.astype(f32))
    return jnp.exp(log_a), jnp.sqrt(-jnp.expm1(2.0 * log_a)) * (i * x)

def linear_scan(a, b, h0=None):
    def combine(left, right):
        return left[0] * right[0], right[0] * left[1] + right[1]

    a_cum, h = lax.associative_scan(combine, (a, b), axis=1)
    return h if h0 is None else h + a_cum * h0[:, None, :]

def odd_mixer(h_ctx, h_lat, w_in, conv_w, conv_b, w_a, b_a, w_x, b_x, lam, w_out, need_ctx):
    def branches(h):
        gate, xr = jnp.split(h @ w_in, 2, axis=-1)
        xr = depthwise_conv(xr, conv_w, conv_b, RG_CONV // 2, RG_CONV - 1 - RG_CONV // 2)
        return gate, xr.astype(jnp.float32)

    g_c, x_c = branches(h_ctx)
    g_l, x_l = branches(h_lat)
    a, b = rglru_gates(x_c, w_a[0], b_a[0], w_x[0], b_x[0], lam[0])
    hc_f = linear_scan(a, b)
    a, b = rglru_gates(x_l, w_a[0], b_a[0], w_x[0], b_x[0], lam[0])
    hl_f = linear_scan(a, b, hc_f[:, -1])
    a, b = rglru_gates(jnp.flip(x_c, 1), w_a[1], b_a[1], w_x[1], b_x[1], lam[1])
    hc_b = linear_scan(a, b)
    a, b = rglru_gates(jnp.flip(x_l, 1), w_a[1], b_a[1], w_x[1], b_x[1], lam[1])
    hl_b = jnp.flip(linear_scan(a, b, hc_b[:, -1]), 1)
    y_lat = (jax.nn.gelu(g_l) * (hl_f + hl_b).astype(g_l.dtype)) @ w_out
    y_ctx = None
    if need_ctx:
        y_ctx = (jax.nn.gelu(g_c) * (hc_f + jnp.flip(hc_b, 1)).astype(g_c.dtype)) @ w_out
    return y_ctx, y_lat

def setup_inputs(seed: int = 0) -> dict:
    key = jax.random.key(seed)
    ks = iter(jax.random.split(key, 48))
    f32 = jnp.float32

    def nrm(shape, scale):
        return jax.random.normal(next(ks), shape, f32) * scale

    def gain(shape):
        return 1.0 + nrm(shape, 0.02)

    D = D_MODEL
    lam_u = jax.random.uniform(next(ks), (N_ODD, 2, D_RNN), f32, 0.9, 0.999)
    lam_a = lam_u ** (1.0 / RG_C)
    rg_lambda = jnp.log(lam_a) - jnp.log1p(-lam_a)
    return {
        'x': nrm((BATCH, SEQ, D), 1.0),
        'c': nrm((BATCH, D), 1.0),
        'ctx': nrm((BATCH, CTX_LEN, D), 1.0),
        'c_ctx': nrm((D,), 1.0),
        'ada_w': nrm((DEPTH, D, 6 * D), 0.02),
        'ada_b': nrm((DEPTH, 6 * D), 0.02),
        'norm1_g': gain((DEPTH, D)),
        'norm2_g': gain((DEPTH, D)),
        'ffn_w_in': nrm((DEPTH, D, 2 * D_FF), D ** -0.5),
        'ffn_w_out': nrm((DEPTH, D_FF, D), D_FF ** -0.5),
        'ev_w_in': nrm((N_EVEN, D, EVEN_IN), D ** -0.5),
        'hy_short_w': nrm((N_EVEN, HY_SHORT, (HY_ORDER + 1) * D_HY), HY_SHORT ** -0.5),
        'hy_short_b': nrm((N_EVEN, (HY_ORDER + 1) * D_HY), 0.02),
        'hy_w1': nrm((N_EVEN, HY_EMB, HY_FILTER_ORDER), HY_EMB ** -0.5),
        'hy_b1': nrm((N_EVEN, HY_FILTER_ORDER), 0.02),
        'hy_w2': nrm((N_EVEN, HY_FILTER_ORDER, HY_FILTER_ORDER), HY_FILTER_ORDER ** -0.5),
        'hy_b2': nrm((N_EVEN, HY_FILTER_ORDER), 0.02),
        'hy_w3': nrm((N_EVEN, HY_FILTER_ORDER, HY_ORDER * D_HY), 0.05 * HY_FILTER_ORDER ** -0.5),
        'hy_freq': gain((N_EVEN, HY_FILTER_ORDER)),
        'hy_bias': nrm((N_EVEN, HY_ORDER, D_HY), 0.5),
        'mla_q_norm_g': gain((N_EVEN, MLA_Q_RANK)),
        'mla_w_uq': nrm((N_EVEN, MLA_Q_RANK, MLA_HEADS * (MLA_NOPE + MLA_ROPE)), MLA_Q_RANK ** -0.5),
        'mla_kv_norm_g': gain((N_EVEN, MLA_KV_RANK)),
        'mla_w_ukv': nrm((N_EVEN, MLA_KV_RANK, MLA_HEADS * (MLA_NOPE + MLA_V)), MLA_KV_RANK ** -0.5),
        'mla_qk_g_q': gain((N_EVEN, MLA_NOPE + MLA_ROPE)),
        'mla_qk_g_k': gain((N_EVEN, MLA_NOPE + MLA_ROPE)),
        'ev_w_out': nrm((N_EVEN, EVEN_MIX, D), EVEN_MIX ** -0.5),
        'rg_w_in': nrm((N_ODD, D, 2 * D_RNN), D ** -0.5),
        'rg_conv_w': nrm((N_ODD, RG_CONV, D_RNN), RG_CONV ** -0.5),
        'rg_conv_b': nrm((N_ODD, D_RNN), 0.02),
        'rg_w_a': nrm((N_ODD, 2, RG_BLOCKS, RG_BW, RG_BW), RG_BW ** -0.5),
        'rg_b_a': nrm((N_ODD, 2, D_RNN), 0.02),
        'rg_w_x': nrm((N_ODD, 2, RG_BLOCKS, RG_BW, RG_BW), RG_BW ** -0.5),
        'rg_b_x': nrm((N_ODD, 2, D_RNN), 0.02),
        'rg_lambda': rg_lambda,
        'rg_w_out': nrm((N_ODD, D_RNN, D), D_RNN ** -0.5),
    }

def reference(x, c, ctx, c_ctx, ada_w, ada_b, norm1_g, norm2_g, ffn_w_in, ffn_w_out,
              ev_w_in, hy_short_w, hy_short_b, hy_w1, hy_b1, hy_w2, hy_b2, hy_w3, hy_freq, hy_bias,
              mla_q_norm_g, mla_w_uq, mla_kv_norm_g, mla_w_ukv, mla_qk_g_q, mla_qk_g_k, ev_w_out,
              rg_w_in, rg_conv_w, rg_conv_b, rg_w_a, rg_b_a, rg_w_x, rg_b_x, rg_lambda, rg_w_out):
    L = x.shape[1]
    rows = L // GRID_W
    row = jnp.repeat(jnp.arange(rows, dtype=jnp.float32), GRID_W)
    col = jnp.tile(jnp.arange(GRID_W, dtype=jnp.float32), rows)
    inv_freq = ROPE_BASE ** (-jnp.arange(0, ROPE_AXIS, 2, dtype=jnp.float32) / ROPE_AXIS)
    ang_row = row[:, None] * inv_freq[None, :]
    ang_col = col[:, None] * inv_freq[None, :]
    s_lat = jax.nn.silu(c)
    s_ctx = jax.nn.silu(c_ctx)
    x_lat, x_ctx = x, ctx
    for i in range(DEPTH):
        j = i // 2
        need_ctx = i < DEPTH - 1
        m_lat = jnp.split((s_lat @ ada_w[i] + ada_b[i])[:, None, :], 6, axis=-1)
        m_ctx = jnp.split(s_ctx @ ada_w[i] + ada_b[i], 6, axis=-1)
        h_lat = modulate(rmsnorm(x_lat, norm1_g[i]), m_lat[0], m_lat[1])
        h_ctx = modulate(rmsnorm(x_ctx, norm1_g[i]), m_ctx[0], m_ctx[1])
        if i % 2 == 0:
            filt = (hy_w1[j], hy_b1[j], hy_w2[j], hy_b2[j], hy_w3[j], hy_freq[j])
            y_ctx, y_lat = even_mixer(h_ctx, h_lat, ang_row, ang_col, ev_w_in[j], hy_short_w[j], hy_short_b[j],
                                      filt, hy_bias[j], mla_q_norm_g[j], mla_w_uq[j], mla_kv_norm_g[j],
                                      mla_w_ukv[j], mla_qk_g_q[j], mla_qk_g_k[j], ev_w_out[j], need_ctx)
        else:
            y_ctx, y_lat = odd_mixer(h_ctx, h_lat, rg_w_in[j], rg_conv_w[j], rg_conv_b[j], rg_w_a[j], rg_b_a[j],
                                     rg_w_x[j], rg_b_x[j], rg_lambda[j], rg_w_out[j], need_ctx)
        x_lat = x_lat + m_lat[2] * y_lat
        x_lat = x_lat + m_lat[5] * swiglu(modulate(rmsnorm(x_lat, norm2_g[i]), m_lat[3], m_lat[4]),
                                          ffn_w_in[i], ffn_w_out[i])
        if need_ctx:
            x_ctx = x_ctx + m_ctx[2] * y_ctx
            x_ctx = x_ctx + m_ctx[5] * swiglu(modulate(rmsnorm(x_ctx, norm2_g[i]), m_ctx[3], m_ctx[4]),
                                              ffn_w_in[i], ffn_w_out[i])
    return x_lat


_drawn_inputs = setup_inputs


def setup_inputs(seed=0):
    import zlib

    import numpy as np

    out = dict(_drawn_inputs(seed))
    spreads = {}
    factors = {'norm1_g': 3.461,
     'norm2_g': 6.049,
     'hy_short_b': 4.031,
     'hy_b1': 5.834,
     'hy_b2': 4.245,
     'hy_freq': 8.0,
     'mla_q_norm_g': 8.0,
     'mla_kv_norm_g': 8.0,
     'mla_qk_g_q': 8.0,
     'mla_qk_g_k': 8.0,
     'rg_b_a': 48.126,
     'rg_b_x': 32.146,
     'rg_conv_b': 3.33}
    for name, (base, spread) in spreads.items():
        noise = np.random.default_rng([zlib.crc32(name.encode()), seed]).standard_normal(out[name].shape)
        drawn = base * np.exp(spread * noise) if base else spread * noise
        out[name] = jnp.asarray(drawn.astype(out[name].dtype))
    for name, factor in factors.items():
        out[name] = (out[name] * factor).astype(out[name].dtype)
    return out
```

```python
import math
from contextlib import ExitStack, contextmanager

import numpy as np

import concourse.bass as bass
from concourse import mybir

F32 = mybir.dt.float32
ACT = mybir.ActivationFunctionType
ALU = mybir.AluOpType
AX_X = mybir.AxisListType.X

P = 128
D = 1024
KT = D // P
LAT, CTX = 1024, 256
T = LAT + CTX
NT = T // P
EPS = 1e-6
D_FF = 2816
HT = D_FF // P
GROUPS = 2
HG = HT // GROUPS
D_HY = 512
CT = D_HY // P
Q_RANK, KV_RANK, ROPE = 384, 256, 32
NOPE, VD, HEADS = 64, 64, 8
QD = NOPE + ROPE
LT = (Q_RANK + KV_RANK) // P
MLA_SCALE = QD ** -0.5
D_RNN = 1280
RT = D_RNN // P
HID_F = 64
EMB = 33
GRID_W = 64
BANK = 512
CHUNKS = {T: [(0, 512), (512, 512), (1024, 256)], LAT: [(0, 512), (512, 512)]}

N_LAT, R_LAT, M_LAT = 1536, 12, 8
N_CTX, R_CTX, M_CTX = 384, 3, 2
ORDER_LAT = [0, 6, 1, 2, 3, 4, 5]
ORDER_CTX = [0, 4]
S3 = math.sqrt(3.0) / 2.0
TF = {}
TI = {}
_n = 0
for _r in ORDER_LAT:
    TF[_r] = TI[_r] = _n
    _n += 2 if _r in (0, 6) else 3
TAB = _n * P
YO_LAT = {1: 0, 2: 256, 3: 512, 4: 768, 5: 1024, 0: 1280, 6: 1408}
YO_CTX = {4: 0, 0: 256}
JOBS = [("lat", 0), ("lat", 1), ("ctx", 0), ("ctx", 1)]

BASE = 16512
C0 = 0
SS0 = 2000
W0 = SS0 + T
WS = HG * P
X0 = W0 + 2 * WS
H0 = X0 + KT * T
R0 = H0 + KT * T
END = (229368 - BASE) // 32 * 8
ATT0 = END - 4 * T

CONSTS = {}
_at = C0
for _name, _len in (("ident", P), ("ones", P), ("mods", 2 * 96), ("coef", 4 * 32), ("gains", 4 * KT), ("ada_b", 2 * 48),
                    ("hy_w", 12 * 3), ("hy_b", 12), ("hy_bias", 8), ("mlp", 3), ("cc", 16), ("silu_c", 16),
                    ("g_lat", 5), ("rg_w", 40), ("rg_b", 10), ("rg_ba", 40), ("rg_lam", 20), ("rg_sp", 80),
                    ("stat", 16), ("rstd", 16)):
    CONSTS[_name] = (_at, _len)
    _at += -(-_len // 8) * 8
assert _at <= SS0


class Phase:

    def __init__(self, name, pairs, kt, uses=1):
        self.name, self.pairs, self.kt, self.uses = name, pairs, kt, uses


PHASES = ([Phase("ev_in", 9, KT), Phase("ev_out", 4, KT)]
          + [Phase(f"{a}0{g}", HG if a == "ffn_in" else 4, KT if a == "ffn_in" else HG)
             for g in range(GROUPS) for a in ("ffn_in", "ffn_out")]
          + [Phase("rg_in", RT, KT, uses=3), Phase("rg_out", 4, RT)]
          + [Phase(f"{a}1{g}", HG if a == "ffn_in" else 4, KT if a == "ffn_in" else HG)
             for g in range(GROUPS) for a in ("ffn_in", "ffn_out")])
PH = {}
_w = _a = 0
for _i, _p in enumerate(PHASES):
    _p.w0, _p.a0, _p.next = _w, _a, (PHASES[_i + 1] if _i + 1 < len(PHASES) else None)
    _w += _p.pairs
    _a += _p.pairs * _p.uses
    PH[_p.name] = _p


class Steps:

    def __init__(self, eng, sem):
        self.eng, self.sem, self.n, self.extra = eng, sem, 0, 0

    def __call__(self, ins):
        self.n += 1
        ins.then_inc(self.sem, 1)
        self.eng.wait_ge(self.sem, self.extra + self.n)

    @contextmanager
    def loop(self, count, per):
        before = self.n
        with self.eng.Fori(0, count) as i:
            self.extra = i * per
            yield i
        assert self.n == before + per, (self.n - before, per)
        self.extra, self.n = 0, before + count * per


class Kernel:

    def __init__(self, nc, ctx, dram):
        self.nc, self.ctx, self.d, self.placed = nc, ctx, dram, {}
        self.bank = ctx.enter_context(nc.psum_tensor("bank", [P, 8, BANK], F32))
        self.acc = [self.bank[:, 3 * s:3 * s + 3, :].rearrange("p b n -> p (b n)") for s in range(2)]
        self.w = [self.at(f"wslot{s}", W0 + s * WS, [P, WS]) for s in range(2)]
        self.x = self.at("x", X0, [P, KT, T])
        self.h = self.at("h", H0, [P, KT, T])
        self.ss = self.at("ss", SS0, [P, T])
        self.c = c = {name: self.at("c_" + name, at, [P, n]) for name, (at, n) in CONSTS.items()}
        self.ident, self.ones, self.mods, self.coef = c["ident"], c["ones"], c["mods"], c["coef"]
        self.gains, self.ada_b, self.cc, self.silu_c = c["gains"], c["ada_b"], c["cc"], c["silu_c"]
        self.hy_w, self.hy_b, self.hy_bias, self.mlp = c["hy_w"], c["hy_b"], c["hy_bias"], c["mlp"]
        self.g_lat, self.stat, self.rstd = c["g_lat"], c["stat"], c["rstd"]
        self.rg_w, self.rg_b, self.rg_ba = c["rg_w"], c["rg_b"], c["rg_ba"]
        self.rg_lam, self.rg_sp = c["rg_lam"], c["rg_sp"]
        self.w_full = [self.sem(f"weights_landed{s}") for s in range(2)]
        self.acc_full = [self.sem(f"sums_ready{s}") for s in range(2)]
        self.acc_free = [self.sem(f"sums_read{s}") for s in range(2)]
        self.stat_full, self.ms_ready, self.sd_ready = self.sem("stat_full"), self.sem("ms_ready"), self.sem("sd_ready")
        self.diag_ready, self.bc_full, self.rr_ready = self.sem("diag_ready"), self.sem("bc_full"), self.sem("rr_ready")
        self.xr_ready, self.h_ready = self.sem("xr_ready"), self.sem("h_ready")
        self.x_new, self.sq_ready, self.ss_done = self.sem("x_new"), self.sem("sq_ready"), self.sem("ss_done")
        self.sqs = 0

    def at(self, name, word, shape, dt=F32):
        key = (word, tuple(shape), str(dt))
        if key not in self.placed:
            self.placed[key] = self.nc.alloc_sbuf_tensor_at(name, shape, dt, offset=BASE + 4 * word)
        return self.placed[key]

    def sem(self, name):
        return self.ctx.enter_context(self.nc.semaphore(name))



def weight_source(k, name):
    d = k.d
    if name == "ev_in":
        return lambda i, s: d["ev_in"][2 * i + s]
    if name == "ev_out":
        return lambda i, s: d["ev_out"][2 * i + s]
    if name.startswith("ffn_in"):
        l, g = int(name[-2]), int(name[-1])
        return lambda i, s: d["ffn_in"][l, g, i, s]
    if name.startswith("ffn_out"):
        l, g = int(name[-2]), int(name[-1])
        return lambda i, s: d["ffn_out"][l, g, 2 * i + s]
    if name == "rg_in":
        return lambda i, s: d["rg_in"][i, s]
    return lambda i, s: d["rg_out"][2 * i + s]


def load_pair(k, e, ph, i):
    for s in range(2):
        e.dma_start(k.w[s][:, 0:ph.kt * P], weight_source(k, ph.name)(i, s)).then_inc(k.w_full[s], 16)


def sync_weights(k, e, ph, between=None):
    src = weight_source(k, ph.name)
    with e.Fori(0, ph.pairs - 1) as i:
        for s in range(2):
            e.wait_ge(k.acc_full[s], i * ph.uses + (ph.a0 + 1))
            e.dma_start(k.w[s][:, 0:ph.kt * P], src(i + 1, s)).then_inc(k.w_full[s], 16)
        if between:
            between(i)
    if ph.next:
        for s in range(2):
            e.wait_ge(k.acc_full[s], ph.a0 + (ph.pairs - 1) * ph.uses + 1)
        load_pair(k, e, ph.next, 0)


def item(k, e, s, w_use, a_use, kt, rhs, tokens, rows=P, h_base=None):
    e.wait_ge(k.w_full[s], w_use * 16 + 16)
    e.wait_ge(k.acc_free[s], a_use + 1)
    for kk in range(kt):
        if h_base is not None:
            e.wait_ge(k.h_ready, h_base + kk + 1)
        for c, n in CHUNKS[tokens]:
            mm = e.matmul(k.acc[s][0:rows, c:c + n], k.w[s][:, kk * P:kk * P + rows],
                          rhs(kk)[:, c:c + n], start=(kk == 0), stop=(kk == kt - 1))
    mm.then_inc(k.acc_full[s], 1)



NORM_TILES = [NT, NT, NT, LAT // P]


class Norm:

    def __init__(self, k, n):
        self.n, self.tiles = n, NORM_TILES[n]
        self.tokens = self.tiles * P
        self.chunks = CHUNKS[self.tokens]
        self.diag = k.at(f"diag{n}", R0, [P, T])
        self.rr = k.at(f"rr{n}", R0 + T, [P, T])
        self.xr = k.at(f"xr{n}", R0 + 2 * T, [P, 2, T])
        self.diags = sum(NORM_TILES[:n])
        self.bcs = sum(len(CHUNKS[t * P]) for t in NORM_TILES[:n])
        self.h_base = n * KT

    def tensor(self, k, e):
        if k.sqs:
            e.wait_ge(k.ss_done, k.sqs)
        for j in range(self.tiles):
            mm = e.matmul(k.bank[:, 6, j:j + 1], k.ss[:, j * P:(j + 1) * P], k.ones[:, 0:1], start=True, stop=True)
        mm.then_inc(k.stat_full, 1)
        for c, (c0, n) in enumerate(self.chunks):
            e.wait_ge(k.diag_ready, self.diags + (c0 + n) // P)
            if c == 2:
                e.wait_ge(k.rr_ready, self.bcs + 1)
            e.matmul(k.bank[:, 7 - c % 2, 0:n], k.ones[:, :], self.diag[:, c0:c0 + n],
                     start=True, stop=True).then_inc(k.bc_full, 1)

    def vector(self, k, e, steps):
        t = self.tiles
        e.wait_ge(k.stat_full, self.n + 1)
        e.tensor_scalar(k.stat[:, 0:t], k.bank[:, 6, 0:t], 1.0 / D, EPS, ALU.mult, ALU.add).then_inc(k.ms_ready, 1)
        e.wait_ge(k.sd_ready, self.n + 1)
        steps(e.reciprocal(k.rstd[:, 0:t], k.stat[:, 0:t]))
        for j in range(t):
            e.tensor_scalar(self.diag[:, j * P:(j + 1) * P], k.ident[:, :], k.rstd[:, j:j + 1], None,
                            ALU.mult).then_inc(k.diag_ready, 1)
        e.wait_ge(k.rr_ready, self.bcs + len(self.chunks))
        for kk in range(KT):
            if kk >= 2:
                e.wait_ge(k.h_ready, self.h_base + kk - 1)
            e.tensor_tensor(self.xr[:, kk % 2, 0:self.tokens], k.x[:, kk, 0:self.tokens], self.rr[:, 0:self.tokens],
                            ALU.mult).then_inc(k.xr_ready, 1)

    def scalar(self, k, e):
        t, n = self.tiles, self.n
        e.wait_ge(k.ms_ready, n + 1)
        e.activation(k.stat[:, 0:t], k.stat[:, 0:t], ACT.Sqrt).then_inc(k.sd_ready, 1)
        for c, (c0, m) in enumerate(self.chunks):
            e.wait_ge(k.bc_full, self.bcs + c + 1)
            e.activation(self.rr[:, c0:c0 + m], k.bank[:, 7 - c % 2, 0:m], ACT.Copy).then_inc(k.rr_ready, 1)
        for kk in range(KT):
            e.wait_ge(k.xr_ready, self.h_base + kk + 1)
            for who, (c0, c1) in enumerate(((0, LAT), (LAT, T))[:1 + (self.tokens > LAT)]):
                at = (n * 2 + who) * 2 * KT + kk
                ins = e.activation(k.h[:, kk, c0:c1], self.xr[:, kk % 2, c0:c1], ACT.Identity,
                                   scale=k.coef_a(n, who, kk), bias=k.coef_b(n, who, kk))
            ins.then_inc(k.h_ready, 1)



def load_constants(k):
    nc, d = k.nc, k.d
    landed = k.sem("constants_landed")
    names = ["ident", "ones", "gains", "ada_b", "hy_w", "hy_b", "hy_bias", "cc", "g_lat", "rg_w", "rg_b",
             "rg_ba", "rg_lam"]
    lam, sp, steps_sem, acts = k.rg_lam, k.rg_sp, k.sem("setup_steps"), k.sem("setup_acts")
    credit = k.sem("x_squared")
    sq = k.at("sq_first", H0, [P, 2, T])
    with nc.Block() as block:
        @block.sync
        def _(e):
            e.dma_start(k.x[:, :, :], d["x"]).then_inc(landed, 16)
            for name in names:
                e.dma_start(k.c[name][:, :], d[name]).then_inc(landed, 16)
            e.dma_start(k.mlp[0:HID_F, :], d["mlp"]).then_inc(landed, 16)
            load_pair(k, e, PH["ev_in"], 0)
            e.wait_ge(landed, 16 * (len(names) + 2))

        @block.scalar
        def _(e):
            e.wait_ge(landed, 16 * (len(names) + 2))
            e.activation(k.silu_c[:, :], k.cc[:, :], ACT.Silu)
            e.activation(sp[:, 0:20], lam[:, :], ACT.Abs).then_inc(acts, 1)
            e.wait_ge(acts, 1)
            e.activation(sp[:, 20:40], sp[:, 0:20], ACT.Exp, scale=-1.0).then_inc(acts, 1)
            e.wait_ge(steps_sem, 2)
            e.activation(sp[:, 60:80], sp[:, 40:60], ACT.Ln).then_inc(acts, 1)
            for kk in range(KT):
                if kk >= 2:
                    e.wait_ge(k.ss_done, kk - 1)
                e.activation(sq[:, kk % 2, :], k.x[:, kk, :], ACT.Square).then_inc(k.sq_ready, 1)

        @block.vector
        def _(e):
            steps = Steps(e, steps_sem)
            e.wait_ge(acts, 2)
            steps(e.tensor_scalar(sp[:, 0:20], lam[:, :], -1.0, 0.0, ALU.mult, ALU.max))
            steps(e.tensor_scalar(sp[:, 40:60], sp[:, 20:40], 1.0, None, ALU.add))
            e.wait_ge(acts, 3)
            steps(e.tensor_tensor(sp[:, 20:40], sp[:, 0:20], sp[:, 60:80], ALU.add))
            steps(e.tensor_scalar(sp[:, 0:20], sp[:, 20:40], -8.0, None, ALU.mult))
            steps(e.tensor_scalar(sp[:, 60:80], sp[:, 20:40], 8.0, None, ALU.mult))

        @block.gpsimd
        def _(e):
            e.memset(k.ss[:, :], 0.0).then_inc(credit, 1)
            e.wait_ge(credit, 1)
            for kk in range(KT):
                e.wait_ge(k.sq_ready, kk + 1)
                e.tensor_tensor(k.ss[:, :], k.ss[:, :], sq[:, kk % 2, :], ALU.add).then_inc(k.ss_done, 1)
                e.wait_ge(k.ss_done, kk + 1)

        @block.tensor
        def _(e):
            for s in range(2):
                e.sem_inc(k.acc_free[s], 1)
    k.sqs += KT


ADA_M = 3
ADA_LOADS = 48 // ADA_M


def adaln(k):
    nc, d = k.nc, k.d
    w = [k.at(f"ada_w{s}", END - 2 * KT * ADA_M * P + s * KT * ADA_M * P, [P, KT, ADA_M, P]) for s in range(2)]
    full = [k.sem(f"ada_landed{s}") for s in range(2)]
    used, sums, read, steps_sem = k.sem("ada_used"), k.sem("ada_sums"), k.sem("ada_read"), k.sem("ada_steps")
    with nc.Block() as block:
        @block.sync
        def _(e):
            for l in range(2):
                if l == 0:
                    for s in range(2):
                        e.dma_start(w[s][:, :, :, :], d["ada_w"][0, s]).then_inc(full[s], 16)
                with e.Fori(1 - l, ADA_LOADS // 2) as i:
                    for s in range(2):
                        e.wait_ge(used, i * 2 + (l * ADA_LOADS + s - 1))
                        e.dma_start(w[s][:, :, :, :], d["ada_w"][l, i * 2 + s]).then_inc(full[s], 16)

        @block.tensor
        def _(e):
            for l in range(2):
                with e.Fori(0, ADA_LOADS // 2) as i:
                    for s in range(2):
                        e.wait_ge(full[s], i * 16 + (l * ADA_LOADS // 2 * 16 + 16))
                        for m in range(ADA_M):
                            for kk in range(KT):
                                mm = e.matmul(k.bank[:, 6 + l, bass.ds(i * (4 * ADA_M) + (s * ADA_M + m) * 2, 2)],
                                              w[s][:, kk, m, :], k.silu_c[:, 2 * kk:2 * kk + 2],
                                              start=(kk == 0), stop=(kk == KT - 1))
                        mm.then_inc(used, 1)

        @block.vector
        def _(e):
            steps = Steps(e, steps_sem)
            for l in range(2):
                e.wait_ge(used, (l + 1) * ADA_LOADS)
                mods = k.mods[:, 96 * l:96 * l + 96].rearrange("p (m w) -> p m w", w=2)
                bias = k.ada_b[:, 48 * l:48 * l + 48].unsqueeze(2).to_broadcast([P, 48, 2])
                steps(e.tensor_tensor(mods, k.bank[:, 6 + l, 0:96].rearrange("p (m w) -> p m w", w=2), bias, ALU.add))
                for which in range(2):
                    n = 2 * l + which
                    gain = k.gains[:, n * KT:(n + 1) * KT]
                    for who in range(2):
                        shift = mods[:, 24 * which:24 * which + 8, who]
                        scale = mods[:, 24 * which + 8:24 * which + 16, who]
                        a = k.coef[:, (n * 2 + who) * 16:(n * 2 + who) * 16 + 8]
                        b = k.coef[:, (n * 2 + who) * 16 + 8:(n * 2 + who) * 16 + 16]
                        steps(e.scalar_tensor_tensor(out=a, in0=scale, scalar=1.0, in1=gain, op0=ALU.add, op1=ALU.mult))
                        steps(e.tensor_copy(b, shift))



def butterfly_lat(e, steps, x, y, t):
    def add(o, a, b):
        steps(e.tensor_tensor(o, a, b, ALU.add))

    def sub(o, a, b):
        steps(e.tensor_tensor(o, a, b, ALU.subtract))

    def fma(o, a, c, b, op=ALU.add):
        steps(e.scalar_tensor_tensor(out=o, in0=a, scalar=c, in1=b, op0=ALU.mult, op1=op))

    def scale(o, a, c):
        steps(e.tensor_scalar(o, a, c, None, ALU.mult))

    add(t[:, 0:2], x[:, 0:2], x[:, 6:8])
    sub(t[:, 2:4], x[:, 0:2], x[:, 6:8])
    add(t[:, 4:6], t[:, 0:2], x[:, 3:5])
    add(t[:, 6], x[:, 2], x[:, 5])
    sub(t[:, 7:9], t[:, 0:2], x[:, 3:5])
    sub(t[:, 9], x[:, 2], x[:, 5])
    add(t[:, 0], t[:, 5], t[:, 6])
    add(y[:, 0], t[:, 4], t[:, 0])
    fma(y[:, 8], t[:, 0], -0.5, t[:, 4])
    sub(t[:, 1], t[:, 5], t[:, 6])
    scale(y[:, 9], t[:, 1], -S3)
    sub(t[:, 0], t[:, 8], t[:, 9])
    sub(y[:, 1], t[:, 7], t[:, 0])
    fma(y[:, 4], t[:, 0], 0.5, t[:, 7])
    add(t[:, 1], t[:, 8], t[:, 9])
    scale(y[:, 5], t[:, 1], -S3)
    sub(t[:, 0], x[:, 2], x[:, 4])
    sub(y[:, 6], t[:, 2], t[:, 0])
    fma(t[:, 4], t[:, 0], 0.5, t[:, 2])
    add(t[:, 1], t[:, 3], x[:, 5])
    sub(y[:, 7], x[:, 3], t[:, 1])
    fma(t[:, 5], t[:, 1], 0.5, x[:, 3])
    sub(t[:, 6], t[:, 3], x[:, 5])
    fma(y[:, 2], t[:, 6], S3, t[:, 4])
    fma(y[:, 10], t[:, 6], -S3, t[:, 4])
    add(t[:, 7], x[:, 2], x[:, 4])
    fma(y[:, 3], t[:, 7], -S3, t[:, 5], ALU.subtract)
    fma(y[:, 11], t[:, 7], S3, t[:, 5], ALU.subtract)


def butterfly_ctx(e, steps, x, y):
    steps(e.tensor_tensor(y[:, 0], x[:, 0], x[:, 1], ALU.add))
    steps(e.scalar_tensor_tensor(out=y[:, 2], in0=x[:, 1], scalar=-0.5, in1=x[:, 0], op0=ALU.mult, op1=ALU.add))
    steps(e.tensor_scalar(y[:, 3], x[:, 1], -S3, None, ALU.mult))


SPREAD_LAT = {0: (0,), 6: (1,), 1: (2, 3), 2: (4, 5), 3: (6, 7), 4: (8, 9), 5: (10, 11)}
SPREAD_CTX = {0: (0,), 4: (2, 3)}


def forward(e, k, tab, xh, r, spread, re, im):
    c = TF[r]
    tile = [tab[:, (c + n) * P:(c + n + 1) * P] for n in range(2 if len(spread) == 1 else 3)]
    if len(spread) == 1:
        e.matmul(re, tile[0], xh[:, spread[0], :], start=True, stop=True)
        return e.matmul(im, tile[1], xh[:, spread[0], :], start=True, stop=True)
    a, b = (xh[:, n, :] for n in spread)
    e.matmul(re, tile[0], a, start=True, stop=False)
    e.matmul(re, tile[1], b, start=False, stop=True)
    e.matmul(im, tile[0], b, start=True, stop=False)
    return e.matmul(im, tile[2], a, start=False, stop=True)


def inverse(e, tab, ys, r, pos, ct, out):
    c = TI[r]
    re, im = (ys[:, 2 * pos + n, ct * P:(ct + 1) * P] for n in range(2))
    if r in (0, 6):
        e.matmul(out, re, tab[:, (c + 1) * P:(c + 2) * P], start=True, stop=False)
        return e.matmul(out, im, tab[:, c * P:(c + 1) * P], start=False, stop=True)
    e.matmul(out, re, tab[:, (c + 1) * P:(c + 3) * P], start=True, stop=False)
    return e.matmul(out, im, tab[:, c * P:(c + 2) * P], start=False, stop=True)


def filters(k):
    nc, d = k.nc, k.d
    Q = H0
    hw = k.at("hw", Q, [P, NT, D_HY])
    xh = k.at("f_xh", Q + 5120, [P, 12, D_HY])
    spec = k.at("f_spec", Q + 11264, [P, 14, D_HY])
    tab = k.at("f_tab", Q + 18432, [P, TAB])
    win = k.at("window", Q + 20864, [P, NT, D_HY])
    arg = k.at("f_arg", Q + 25984, [P, T])
    tmp = k.at("f_tmp", Q + 27264, [P, T])
    zin = k.at("f_z", Q + 28544, [P, T])
    w3 = k.at("f_w3", Q + 28544, [P, 2 * D_HY])
    w12 = k.at("f_w12", Q + 29824, [P, 2 * HID_F])
    TWO_PI = 2.0 * math.pi
    C1 = 6.28125
    C2 = float(np.float32(TWO_PI - C1))
    C3 = float(np.float32(TWO_PI - C1 - C2))
    MAGIC = 1.5 * 2.0 ** 23
    PI = float(np.nextafter(np.float32(math.pi), np.float32(0)))
    landed, w3_landed, mm_full, arg_ready = k.sem("f_landed"), k.sem("f_w3_landed"), k.sem("f_sums"), k.sem("f_arg")
    sin_ready, steps_sem, tile_full, hw_ready = k.sem("f_sin"), k.sem("f_steps"), k.sem("f_tile"), k.sem("f_hw")
    xh_ready, spec_full, spec_read, stored = k.sem("f_xh"), k.sem("f_spec"), k.sem("f_spec_read"), k.sem("f_stored")
    npos = {"lat": len(ORDER_LAT), "ctx": len(ORDER_CTX)}
    jobs = [("lat", 0), ("ctx", 0), ("lat", 1), ("ctx", 1)]
    before = [sum(npos[p] for p, _ in jobs[:j]) for j in range(5)]
    with nc.Block() as block:
        @block.sync
        def _(e):
            e.dma_start(zin[0:EMB, :], d["filter_z"]).then_inc(landed, 16)
            e.dma_start(w12[0:EMB, 0:HID_F], d["hy_w1"]).then_inc(landed, 16)
            e.dma_start(w12[0:HID_F, HID_F:2 * HID_F], d["hy_w2"]).then_inc(landed, 16)
            e.dma_start(win[:, :, :], d["window"]).then_inc(landed, 16)
            e.dma_start(tab[:, :], d["tab_f"]).then_inc(landed, 16)
            e.wait_ge(arg_ready, 1)
            e.dma_start(w3[0:HID_F, :], d["hy_w3"]).then_inc(w3_landed, 16)
            for j, (part, order) in enumerate(jobs):
                n = 2 * npos[part]
                e.wait_ge(spec_read, before[j + 1])
                e.dma_start(d["spec_" + part][order], spec[:, 0:n, :]).then_inc(stored, 16)
            e.wait_ge(stored, 64)

        @block.tensor
        def _(e):
            e.wait_ge(landed, 80)
            for c, n in CHUNKS[T]:
                mm = e.matmul(k.acc[0][0:HID_F, c:c + n], w12[0:EMB, 0:HID_F], zin[0:EMB, c:c + n], start=True, stop=True)
            mm.then_inc(mm_full, 1)
            e.wait_ge(sin_ready, 1)
            for c, n in CHUNKS[T]:
                mm = e.matmul(k.acc[1][0:HID_F, c:c + n], w12[0:HID_F, HID_F:2 * HID_F], tmp[0:HID_F, c:c + n],
                              start=True, stop=True)
            mm.then_inc(mm_full, 1)
            e.wait_ge(sin_ready, 2)
            e.wait_ge(w3_landed, 16)
            for order in range(2):
                for t in range(NT):
                    g = order * NT + t
                    if g >= 2:
                        e.wait_ge(hw_ready, g - 1)
                    e.matmul(k.bank[:, 6 + g % 2, :], tmp[0:HID_F, t * P:(t + 1) * P],
                             w3[0:HID_F, order * D_HY:(order + 1) * D_HY], start=True, stop=True).then_inc(tile_full, 1)
                for j in (2 * order, 2 * order + 1):
                    part = jobs[j][0]
                    e.wait_ge(xh_ready, j + 1)
                    residues, spread = (ORDER_LAT, SPREAD_LAT) if part == "lat" else (ORDER_CTX, SPREAD_CTX)
                    for pos, r in enumerate(residues):
                        g = before[j] + pos
                        if g >= 3:
                            e.wait_ge(spec_read, g - 2)
                        b = 2 * (g % 3)
                        forward(e, k, tab, xh, r, spread[r], k.bank[:, b, :], k.bank[:, b + 1, :]).then_inc(spec_full, 1)

        @block.vector
        def _(e):
            steps = Steps(e, steps_sem)

            def reduce_angle(sums, n):
                rows = slice(0, HID_F)
                e.wait_ge(mm_full, n + 1)
                steps(e.tensor_scalar(arg[rows, :], sums[rows, 0:T], k.mlp[rows, n:n + 1], k.mlp[rows, 2:3], ALU.add, ALU.mult))
                steps(e.tensor_scalar(tmp[rows, :], arg[rows, :], 1.0 / TWO_PI, MAGIC, ALU.mult, ALU.add))
                steps(e.tensor_scalar(tmp[rows, :], tmp[rows, :], MAGIC, None, ALU.subtract))
                for c in (C1, C2, C3):
                    steps(e.scalar_tensor_tensor(out=arg[rows, :], in0=tmp[rows, :], scalar=-c, in1=arg[rows, :],
                                                 op0=ALU.mult, op1=ALU.add))
                e.tensor_scalar(arg[rows, :], arg[rows, :], PI, -PI, ALU.min, ALU.max).then_inc(arg_ready, 1)

            reduce_angle(k.acc[0], 0)
            reduce_angle(k.acc[1], 1)
            for order in range(2):
                for t in range(NT):
                    g = order * NT + t
                    e.wait_ge(tile_full, g + 1)
                    e.tensor_tensor(hw[:, t, :], k.bank[:, 6 + g % 2, :], win[:, t, :], ALU.mult).then_inc(hw_ready, 1)
                e.wait_ge(hw_ready, (order + 1) * NT)
                j = 2 * order
                if j:
                    e.wait_ge(spec_full, before[j])
                    e.wait_ge(stored, 16 * j)
                butterfly_lat(e, steps, hw[:, 0:M_LAT], xh, spec[:, 0:10])
                e.sem_inc(xh_ready, 1)
                e.wait_ge(spec_full, before[j + 1])
                butterfly_ctx(e, steps, hw[:, M_LAT:NT], xh)
                e.sem_inc(xh_ready, 1)

        @block.scalar
        def _(e):
            for n in range(2):
                e.wait_ge(arg_ready, n + 1)
                e.activation(tmp[0:HID_F, :], arg[0:HID_F, :], ACT.Sin).then_inc(sin_ready, 1)
            for j, (part, order) in enumerate(jobs):
                if j:
                    e.wait_ge(stored, 16 * j)
                for pos in range(npos[part]):
                    g = before[j] + pos
                    e.wait_ge(spec_full, g + 1)
                    b = 2 * (g % 3)
                    e.activation(spec[:, 2 * pos:2 * pos + 2, :], k.bank[:, b:b + 2, :], ACT.Copy).then_inc(spec_read, 1)



def even_in(k):
    nc, d, ph = k.nc, k.d, PH["ev_in"]
    norm = Norm(k, 0)
    uc = k.at("uc", R0 + 5120, [P, 2, T])
    lat = k.at("lat_w", R0 + 7680, [P, LT, T])
    rope = k.at("rope_w", R0 + 14080, [P, T])
    centre, done, steps_sem, stored = k.sem("tap1"), k.sem("conv3_done"), k.sem("conv3_steps"), k.sem("u_stored")
    uc_free = k.sem("uc_free")
    w0, a0 = ph.w0, ph.a0
    HP = 6
    taps = k.hy_w[:, :].rearrange("p (m t) -> p m t", t=3)
    with nc.Block() as block:
        @block.sync
        def _(e):
            sync_weights(k, e, ph)

        @block.tensor
        def _(e):
            norm.tensor(k, e)
            rhs = lambda kk: k.h[:, kk, :]
            with e.Fori(0, 8) as i:
                for s in range(2):
                    item(k, e, s, i + w0, i + a0, KT, rhs, T, h_base=norm.h_base)
            item(k, e, 0, w0 + 8, a0 + 8, KT, rhs, T)
            item(k, e, 1, w0 + 8, a0 + 8, KT, rhs, T, rows=ROPE)

        @block.scalar
        def _(e):
            norm.scalar(k, e)
            with e.Fori(0, HP) as i:
                for s in range(2):
                    e.wait_ge(k.acc_full[s], i + (a0 + 1))
                    e.wait_ge(uc_free, i * 2 + (s + 1))
                    e.activation(uc[:, s, :], k.acc[s][:, 0:T], ACT.Identity, scale=taps[:, i * 2 + s, 1:2],
                                 bias=k.hy_b[:, bass.ds(i * 2 + s, 1)]).then_inc(centre, 1)
            for j in range(LT + 1):
                s, pair = j % 2, HP + j // 2
                e.wait_ge(k.acc_full[s], a0 + pair + 1)
                if j < LT:
                    e.activation(lat[:, j, :], k.acc[s][:, 0:T], ACT.Copy).then_inc(k.acc_free[s], 1)
                else:
                    e.activation(rope[0:ROPE, :], k.acc[s][0:ROPE, 0:T], ACT.Copy).then_inc(k.acc_free[s], 1)

        @block.vector
        def _(e):
            steps = Steps(e, steps_sem)
            norm.vector(k, e, steps)
            with steps.loop(HP, 6) as i:
                for s in range(2):
                    e.wait_ge(centre, i * 2 + (s + 1))
                    n = 0
                    for a, b in ((0, LAT), (LAT, T)):
                        for tap, lo, hi, sh in ((0, a + 1, b, -1), (2, a, b - 1, 1)):
                            ins = e.scalar_tensor_tensor(
                                out=uc[:, s, lo:hi], in0=k.acc[s][:, lo + sh:hi + sh],
                                scalar=taps[:, i * 2 + s, tap:tap + 1], in1=uc[:, s, lo:hi], op0=ALU.mult, op1=ALU.add)
                            n += 1
                            if n < 4:
                                steps(ins)
                            else:
                                ins.then_inc(k.acc_free[s], 1)
                    e.wait_ge(k.acc_free[s], i + (a0 + 2))
                    e.sem_inc(done, 1)

        @block.gpsimd
        def _(e):
            e.sem_inc(uc_free, 2)
            with e.Fori(0, HP) as i:
                for s in range(2):
                    e.wait_ge(done, i * 2 + (s + 1))
                    e.dma_start(d["u"][i * 2 + s], uc[:, s, :]).then_inc(stored, 16)
                    e.wait_ge(stored, i * 32 + (16 * s + 16))
                    e.sem_inc(uc_free, 1)


def rotate(e, steps, x, out, cos, sin, t1, heads):
    shape = [P, heads, ROPE]
    steps(e.tensor_tensor(t1, x, cos.unsqueeze(1).to_broadcast(shape), ALU.mult))
    halves = lambda a: a.rearrange("p h (g c) -> p h g c", g=2)
    sb = halves(sin.unsqueeze(1).to_broadcast(shape))
    xv, ov = halves(x), halves(out)
    return t1, xv, sb


def latents(k):
    nc, d = k.nc, k.d
    lat = k.at("lat", R0 + 7680, [P, LT, T])
    rope = k.at("rope", R0 + 14080, [P, T])
    wq = k.at("wq", R0 + 15360, [P, 3, HEADS * QD])
    wkv = k.at("wkv", R0 + 17664, [P, 2, 1024])
    gq = k.at("gq", R0 + 19712, [P, QD])
    gk = k.at("gk", R0 + 19808, [P, QD])
    cos = k.at("cos", R0 + 19904, [P, NT, ROPE])
    sin = k.at("sin", R0 + 20224, [P, NT, ROPE])
    kT = k.at("kT_w", X0, [P, HEADS, T])
    qT = k.at("qT_w", H0, [P, HEADS, T])
    v = k.at("v_w", R0, [P, NT, HEADS * VD])
    lcur = k.at("lcur", R0 + 5120, [P, 2, LT, P])
    sqc = k.at("sqc", R0 + 6400, [P, 2, LT, P])
    at = R0 + 20544
    qb = k.at("qb", at, [P, 2, HEADS, QD])
    kb = k.at("kb", at + 1536, [P, 2, HEADS, QD])
    sqq = k.at("sqq", at + 3072, [P, HEADS, QD])
    sqk = k.at("sqk", at + 3840, [P, HEADS, NOPE])
    sqr = k.at("sqr", at + 4352, [P, ROPE])
    rcur = k.at("rcur", at + 4384, [P, 2, P])
    t1 = k.at("rot1", at + 4640, [P, HEADS, ROPE])
    t2 = k.at("rot2", at + 4896, [P, HEADS, ROPE])
    krow = k.at("krow", at + 5152, [P, 1, ROPE])
    kout = k.at("kout", at + 5184, [P, 1, ROPE])
    st = k.at("st", at + 5216, [P, 8])
    ss = k.at("hs", at + 5224, [P, 32])
    landed, folded = k.sem("m_landed"), k.sem("m_folded")
    cur, sq_ready = [k.sem(f"m_cur{s}") for s in range(2)], k.sem("m_sq")
    sums, tr_full = k.sem("m_sums"), k.sem("m_tr")
    ms, sd, hsq, hss, hsd, vout, tok = (k.sem("m_" + n) for n in ("ms", "sd", "hsq", "hss", "hsd", "v", "tok"))
    freed = [k.sem(f"m_freed{s}") for s in range(2)]
    steps_sem = k.sem("m_steps")
    HH = HEADS // 2
    qps = lambda s: k.bank[:, 4 * s:4 * s + 2, 0:HH * QD].rearrange("p b (h c) -> p b h c", c=QD)
    kvps = lambda s: k.bank[:, 4 * s + 2:4 * s + 4, :].rearrange("p b (h c) -> p b h c", c=NOPE + VD)
    two = lambda a: a.rearrange("p (b h) c -> p b h c", b=2)

    with nc.Block() as block:
        @block.sync
        def _(e):
            for t, name in ((wq, "w_uq"), (wkv, "w_ukv"), (cos, "cos"), (sin, "sin")):
                e.dma_start(t[:, :, :], d[name]).then_inc(landed, 16)
            e.dma_start(gq[:, :], d["gq"]).then_inc(landed, 16)
            e.dma_start(gk[:, :], d["gk"]).then_inc(landed, 16)
            e.wait_ge(landed, 96)

        @block.gpsimd
        def _(e):
            with e.Fori(0, NT // 2) as i:
                for s in range(2):
                    e.wait_ge(freed[s], i * 2 + 2)
                    e.tensor_copy(lcur[:, s, :, :], lat[:, :, bass.ds(i * 256 + s * P, P)]).then_inc(cur[s], 1)
                    e.tensor_copy(rcur[0:ROPE, s, :], rope[0:ROPE, bass.ds(i * 256 + s * P, P)]).then_inc(cur[s], 1)

        @block.tensor
        def _(e):
            e.wait_ge(folded, 5)
            with e.Fori(0, NT // 2) as i:
                for s in range(2):
                    e.wait_ge(freed[s], i * 2 + 2)
                    e.wait_ge(cur[s], i * 2 + 2)
                    for half in range(2):
                        for kk in range(3):
                            e.matmul(k.bank[:, 4 * s + half, 0:HH * QD], lcur[:, s, kk, :],
                                     wq[:, kk, half * HH * QD:(half + 1) * HH * QD], start=(kk == 0), stop=(kk == 2))
                        for kk in range(2):
                            e.matmul(k.bank[:, 4 * s + 2 + half, :], lcur[:, s, 3 + kk, :],
                                     wkv[:, kk, half * 512:(half + 1) * 512], start=(kk == 0), stop=(kk == 1))
                    e.transpose(k.bank[:, 4 * s + 1, 384:384 + ROPE], rcur[0:ROPE, s, :], k.ident[0:ROPE, 0:ROPE])
                    e.wait_ge(sq_ready, i * 2 + (s + 1))
                    for kk in range(LT):
                        c = 384 if kk < 3 else 386
                        mm = e.matmul(k.bank[:, 4 * s, c:c + 1], sqc[:, s, kk, :], k.ones[:, 0:1],
                                      start=kk in (0, 3), stop=kk in (2, 4))
                    mm.then_inc(sums, 1)
                for s in range(2):
                    e.wait_ge(tok, i * 2 + (s + 1))
                    e.wait_ge(vout, i * 2 + (s + 1))
                    for h in range(HEADS):
                        e.transpose(k.bank[0:QD, 4 * s + h // 4, (h % 4) * P:(h % 4 + 1) * P], qb[:, s, h, :], k.ident[:, :])
                    for h in range(HEADS):
                        mm = e.transpose(k.bank[0:QD, 4 * s + 2 + h // 4, (h % 4) * P:(h % 4 + 1) * P], kb[:, s, h, :],
                                         k.ident[:, :])
                    mm.then_inc(tr_full, 1)

        @block.scalar
        def _(e):
            with e.Fori(0, NT // 2) as i:
                for s in range(2):
                    e.wait_ge(cur[s], i * 2 + 2)
                    e.activation(sqc[:, s, :, :], lcur[:, s, :, :], ACT.Square).then_inc(sq_ready, 1)
                for s in range(2):
                    e.wait_ge(ms, i * 2 + (s + 1))
                    e.activation(st[:, 2:4], st[:, 0:2], ACT.Sqrt).then_inc(sd, 1)
                    e.wait_ge(hss, i * 4 + (2 * s + 1))
                    e.activation(two(sqq[:, :, :]), qps(s), ACT.Square, scale=st[:, 4:5]).then_inc(hsq, 1)
                    e.activation(two(sqk[:, :, :]), kvps(s)[:, :, :, 0:NOPE], ACT.Square, scale=st[:, 5:6]).then_inc(hsq, 1)
                    e.activation(sqr[:, :], k.bank[:, 4 * s + 1, 384:384 + ROPE], ACT.Square).then_inc(hsq, 1)
                    e.activation(v[:, i * 2 + s, :].rearrange("p (b h c) -> p b h c", b=2, c=VD), kvps(s)[:, :, :, NOPE:],
                                 ACT.Copy, scale=st[:, 5:6]).then_inc(vout, 1)
                    e.wait_ge(hss, i * 4 + (2 * s + 2))
                    e.activation(ss[:, 0:25], ss[:, 0:25], ACT.Sqrt).then_inc(hsd, 1)
                for s in range(2):
                    e.wait_ge(tr_full, i * 2 + (s + 1))
                    e.activation(qT[0:QD, :, bass.ds(i * 256 + s * P, P)].rearrange("p (b h) c -> p b h c", b=2),
                                 k.bank[0:QD, 4 * s:4 * s + 2, :].rearrange("p b (h c) -> p b h c", c=P),
                                 ACT.Copy).then_inc(freed[s], 1)

        @block.vector
        def _(e):
            for s in range(2):
                e.sem_inc(freed[s], 2)
            steps = Steps(e, steps_sem)
            e.wait_ge(landed, 96)
            for kk in range(3):
                e.tensor_scalar(wq[:, kk, :], wq[:, kk, :], k.g_lat[:, kk:kk + 1], None, ALU.mult).then_inc(folded, 1)
            for kk in range(2):
                e.tensor_scalar(wkv[:, kk, :], wkv[:, kk, :], k.g_lat[:, 3 + kk:4 + kk], None, ALU.mult).then_inc(folded, 1)
            with steps.loop(NT // 2, 48) as i:
                for s in range(2):
                    q, kk_, kr = qb[:, s, :, :], kb[:, s, :, :], k.bank[:, 4 * s + 1, 384:384 + ROPE]
                    e.wait_ge(sums, i * 2 + (s + 1))
                    steps(e.tensor_scalar(st[:, 0:1], k.bank[:, 4 * s, 384:385], 1.0 / Q_RANK, EPS, ALU.mult, ALU.add))
                    e.tensor_scalar(st[:, 1:2], k.bank[:, 4 * s, 386:387], 1.0 / KV_RANK, EPS, ALU.mult, ALU.add).then_inc(ms, 1)
                    e.wait_ge(sd, i * 2 + (s + 1))
                    e.reciprocal(st[:, 4:6], st[:, 2:4]).then_inc(hss, 1)
                    e.wait_ge(hsq, i * 6 + (3 * s + 3))
                    e.wait_ge(hss, i * 4 + (2 * s + 1))
                    steps(e.tensor_reduce(ss[:, 0:8], sqq[:, :, 0:NOPE], AX_X, ALU.add))
                    steps(e.tensor_reduce(ss[:, 8:16], sqk[:, :, :], AX_X, ALU.add))
                    steps(e.tensor_reduce(ss[:, 16:24], sqq[:, :, NOPE:QD], AX_X, ALU.add))
                    steps(e.tensor_reduce(ss[:, 24:25], sqr[:, :], AX_X, ALU.add))
                    steps(e.tensor_scalar(ss[:, 0:16], ss[:, 0:16], 1.0 / NOPE, EPS, ALU.mult, ALU.add))
                    e.tensor_scalar(ss[:, 16:25], ss[:, 16:25], 1.0 / ROPE, EPS, ALU.mult, ALU.add).then_inc(hss, 1)
                    e.wait_ge(hsd, i * 2 + (s + 1))
                    steps(e.reciprocal(ss[:, 0:25], ss[:, 0:25]))
                    steps(e.tensor_scalar(ss[:, 0:8], ss[:, 0:8], st[:, 4:5], None, ALU.mult))
                    steps(e.tensor_scalar(ss[:, 16:24], ss[:, 16:24], st[:, 4:5], None, ALU.mult))
                    steps(e.tensor_scalar(ss[:, 8:16], ss[:, 8:16], st[:, 5:6], None, ALU.mult))
                    bc = lambda a, n: a.rearrange("p (b h) -> p b h", b=2).unsqueeze(3).to_broadcast([P, 2, HH, n])
                    steps(e.tensor_tensor(two(q[:, :, 0:NOPE]), qps(s)[:, :, :, 0:NOPE], bc(ss[:, 0:8], NOPE), ALU.mult))
                    steps(e.tensor_tensor(two(q[:, :, NOPE:QD]), qps(s)[:, :, :, NOPE:QD], bc(ss[:, 16:24], ROPE), ALU.mult))
                    steps(e.tensor_tensor(two(kk_[:, :, 0:NOPE]), kvps(s)[:, :, :, 0:NOPE], bc(ss[:, 8:16], NOPE), ALU.mult))
                    steps(e.scalar_tensor_tensor(out=krow[:, 0, :], in0=kr, scalar=ss[:, 24:25], in1=gk[:, NOPE:QD],
                                                 op0=ALU.mult, op1=ALU.mult))
                    steps(e.tensor_tensor(q, q, gq[:, :].unsqueeze(1).to_broadcast([P, HEADS, QD]), ALU.mult))
                    steps(e.tensor_tensor(kk_[:, :, 0:NOPE], kk_[:, :, 0:NOPE],
                                          gk[:, 0:NOPE].unsqueeze(1).to_broadcast([P, HEADS, NOPE]), ALU.mult))
                    for x, out, tmp1, tmp2, n in ((q[:, :, NOPE:QD], q[:, :, NOPE:QD], t1[:, :, :], t2[:, :, :], HEADS),
                                                  (krow[:, :, :], kout[:, :, :], t1[:, 0:1, :], t2[:, 0:1, :], 1)):
                        tile = i * 2 + s
                        co = cos[:, tile, :].unsqueeze(1).to_broadcast([P, n, ROPE])
                        steps(e.tensor_tensor(tmp1, x, co, ALU.mult))
                        for a in range(2):
                            pick = lambda y, b: y.rearrange("p h (g c) -> p h g c", g=2)[:, :, :, 8 * b:8 * b + 8]
                            si = sin[:, tile, :].rearrange("p (g c) -> p g c", g=2)[:, :, 8 * a:8 * a + 8]
                            steps(e.tensor_tensor(pick(tmp2, a), pick(x, 1 - a),
                                                  si.unsqueeze(1).to_broadcast([P, n, 2, 8]), ALU.mult))
                        steps(e.tensor_tensor(out, tmp1, tmp2, ALU.add))
                    e.tensor_copy(kk_[:, :, NOPE:QD], kout[:, :, :].to_broadcast([P, HEADS, ROPE])).then_inc(tok, 1)
                for s in range(2):
                    e.wait_ge(tr_full, i * 2 + (s + 1))
                    e.tensor_copy(kT[0:QD, :, bass.ds(i * 256 + s * P, P)].rearrange("p (b h) c -> p b h c", b=2),
                                  k.bank[0:QD, 4 * s + 2:4 * s + 4, :].rearrange("p b (h c) -> p b h c", c=P)
                                  ).then_inc(freed[s], 1)


def attention(k):
    nc = k.nc
    kT = k.at("kT", X0, [P, HEADS, T])
    qT = k.at("qT", H0, [P, HEADS, T])
    v = k.at("v", R0, [P, NT, HEADS * VD])
    att = k.at("att_tok", R0 + 5120, [P, NT, HEADS * VD])
    p = k.at("probs", R0 + 10240, [P, 2, T])
    pT = k.at("probsT", R0 + 12800, [P, 2, NT, P])
    qcur = k.at("qcur", R0 + 15360, [P, 2, T])
    mx = k.at("mx", R0 + 17920, [P, 2])
    ng = k.at("ng", R0 + 17928, [P, 2])
    rs = k.at("rs", R0 + 17936, [P, 2])
    ri = k.at("ri", R0 + 17944, [P, 2])
    attT = k.at("attT_w", ATT0, [P, 4, T])
    q_ready, s_full, mx_ready, p_ready = k.sem("a_q"), k.sem("a_scores"), k.sem("a_max"), k.sem("a_p")
    t_full, t_read, pv_full, pv_out = k.sem("a_t"), k.sem("a_t_read"), k.sem("a_pv"), k.sem("a_out")
    q_free, steps_sem, aT_full, aT_read = k.sem("a_qfree"), k.sem("a_steps"), k.sem("a_aT"), k.sem("a_aT_read")
    N = 2 * NT
    steps_of = []
    for hp in range(2):
        for j in range(NT):
            keys = NT if j < LAT // P else CTX // P
            steps_of.append((hp, j, keys, 0 if keys == NT else LAT))
    groups = lambda keys: [(g, min(4, keys - g)) for g in range(0, keys, 4)]
    G = [sum(len(groups(st[2])) for st in steps_of[:n]) for n in range(N + 1)]
    with nc.Block() as block:
        @block.gpsimd
        def _(e):
            e.sem_inc(q_free, 2)
            with e.Fori(0, HEADS // 2) as i:
                for hp in range(2):
                    e.wait_ge(q_free, i * 2 + (hp + 2 - 1))
                    e.tensor_copy(qcur[0:QD, hp, :], qT[0:QD, i * 2 + hp, :]).then_inc(q_ready, 1)

        @block.tensor
        def _(e):
            for _ in range(1):
                e.sem_inc(pv_out, 2)
                e.sem_inc(t_read, 2)
            with e.Fori(0, HEADS // 2) as i:
                def scores(n):
                    hp, j, keys, k0 = steps_of[n]
                    if j == 0:
                        e.wait_ge(q_ready, i * 2 + (hp + 1))
                    e.wait_ge(pv_out, i * N + (n + 1))
                    kh = kT[0:QD, i * 2 + hp, :]
                    for c in range(0, keys * P, BANK):
                        m = min(BANK, keys * P - c)
                        mm = e.matmul(k.bank[:, 3 * (n % 2) + c // BANK, 0:m], qcur[0:QD, hp, j * P:(j + 1) * P],
                                      kh[:, k0 + c:k0 + c + m], start=True, stop=True)
                    mm.then_inc(s_full, 1)

                def values(n):
                    hp, j, keys, k0 = steps_of[n]
                    e.wait_ge(p_ready, i * N + (n + 1))
                    for g, (g0, m) in enumerate(groups(keys)):
                        at = G[n] + g
                        e.wait_ge(t_read, i * G[N] + (at + 1))
                        for t in range(g0, g0 + m):
                            tr = e.transpose(k.bank[:, 6 + at % 2, (t - g0) * P:(t - g0 + 1) * P],
                                             p[:, n % 2, t * P:(t + 1) * P], k.ident[:, :])
                        tr.then_inc(t_full, 1)
                    e.wait_ge(t_read, i * G[N] + (G[n + 1] + 2))
                    for t in range(keys):
                        mm = e.matmul(k.bank[:, 3 * (n % 2) + 2, 256:256 + VD], pT[:, n % 2, t, :],
                                      v[:, k0 // P + t, bass.ds(i * 2 * VD + hp * VD, VD)],
                                      start=(t == 0), stop=(t == keys - 1))
                    mm.then_inc(pv_full, 1)
                    if n % NT == NT - 1:
                        e.sem_inc(q_free, 1)

                scores(0)
                for n in range(N):
                    if n + 1 < N:
                        scores(n + 1)
                    values(n)
            for t in range(NT):
                if t >= 8:
                    e.wait_ge(aT_read, t - 7)
                e.wait_ge(pv_out, 2 + N * HEADS // 2)
                for f in range(4):
                    tr = e.transpose(k.bank[:, t % 8, f * P:(f + 1) * P], att[:, t, f * P:(f + 1) * P], k.ident[:, :])
                tr.then_inc(aT_full, 1)

        @block.vector
        def _(e):
            steps = Steps(e, steps_sem)
            with steps.loop(HEADS // 2, 2 * N) as i:
                def maximum(n):
                    keys = steps_of[n][2]
                    e.wait_ge(s_full, i * N + (n + 1))
                    flat = k.bank[:, 3 * (n % 2):3 * (n % 2) + 3, :].rearrange("p b n -> p (b n)")
                    steps(e.reduce_max(mx[:, n % 2:n % 2 + 1], flat[:, 0:keys * P], AX_X))
                    e.tensor_scalar(ng[:, n % 2:n % 2 + 1], mx[:, n % 2:n % 2 + 1], -MLA_SCALE, None,
                                    ALU.mult).then_inc(mx_ready, 1)

                def output(n):
                    hp, j, keys, k0 = steps_of[n]
                    steps(e.reciprocal(ri[:, n % 2:n % 2 + 1], rs[:, n % 2:n % 2 + 1]))
                    e.wait_ge(pv_full, i * N + (n + 1))
                    e.tensor_scalar(att[:, j, bass.ds(i * 2 * VD + hp * VD, VD)], k.bank[:, 3 * (n % 2) + 2, 256:256 + VD],
                                    ri[:, n % 2:n % 2 + 1], None, ALU.mult).then_inc(pv_out, 1)

                maximum(0)
                for n in range(N):
                    if n + 1 < N:
                        maximum(n + 1)
                    e.wait_ge(p_ready, i * N + (n + 1))
                    output(n)

        @block.scalar
        def _(e):
            with e.Fori(0, HEADS // 2) as i:
                def exps(n):
                    keys = steps_of[n][2]
                    flat = k.bank[:, 3 * (n % 2):3 * (n % 2) + 3, :].rearrange("p b n -> p (b n)")
                    e.wait_ge(mx_ready, i * N + (n + 1))
                    e.wait_ge(pv_out, i * N + (n + 1))
                    e.activation(p[:, n % 2, 0:keys * P], flat[:, 0:keys * P], ACT.Exp, bias=ng[:, n % 2:n % 2 + 1],
                                 scale=MLA_SCALE, accum_out=rs[:, n % 2:n % 2 + 1]).then_inc(p_ready, 1)

                def evacuate(n):
                    keys = steps_of[n][2]
                    for g, (g0, m) in enumerate(groups(keys)):
                        at = G[n] + g
                        e.wait_ge(t_full, i * G[N] + (at + 1))
                        e.activation(pT[:, n % 2, g0:g0 + m, :].rearrange("p a b -> p (a b)"),
                                     k.bank[:, 6 + at % 2, 0:m * P], ACT.Copy).then_inc(t_read, 1)

                exps(0)
                for n in range(N):
                    evacuate(n)
                    if n + 1 < N:
                        exps(n + 1)
            for t in range(NT):
                e.wait_ge(aT_full, t + 1)
                e.activation(attT[:, :, t * P:(t + 1) * P], k.bank[:, t % 8, :].rearrange("p (f c) -> p f c", c=P),
                             ACT.Copy).then_inc(aT_read, 1)


def hyena(k):
    nc, d = k.nc, k.d
    at = X0
    xh = k.at("h_xh", at, [P, 14, D_HY])
    yr = k.at("h_yr", at, [P, CT, 1536])
    ys = k.at("h_ys", at + 7168, [P, 14, D_HY])
    spec = k.at("h_spec", at + 14336, [P, 14, D_HY])
    gate = k.at("h_gate", at + 21504, [P, CT, T])
    z = k.at("h_z", at + 26624, [P, CT, T])
    zt = k.at("h_zt", at + 31744, [P, M_LAT, D_HY])
    cv = k.at("h_cv", at + 31744, [P, CT, LAT])
    tf = k.at("h_tf", at + 35840, [P, TAB])
    ti = k.at("h_ti", at + 35840 + TAB, [P, TAB])
    t = [k.at(f"h_t{n}", at + 35840 + 2 * TAB + n * D_HY, [P, D_HY]) for n in range(2)]
    assert 35840 + 2 * TAB + 2 * D_HY <= ATT0 - X0
    g_tmp = k.at("h_bt", at + 7168, [P, 10, D_HY])
    i_tmp = k.at("h_it", at + 7168, [P, 7168])
    landed, spec_in, gate_in = k.sem("y_landed"), k.sem("y_spec_in"), k.sem("y_gate_in")
    zt_full, zt_read, xh_ready, sp_full, sp_read = (k.sem("y_" + n) for n in ("ztf", "ztr", "xh", "spf", "spr"))
    yr_full, yr_read, z_ready, steps_sem = (k.sem("y_" + n) for n in ("yrf", "yrr", "z", "steps"))
    blocks = {"lat": M_LAT, "ctx": M_CTX}
    resid = {"lat": ORDER_LAT, "ctx": ORDER_CTX}
    spread = {"lat": SPREAD_LAT, "ctx": SPREAD_CTX}
    yo = {"lat": YO_LAT, "ctx": YO_CTX}
    zb = [sum(blocks[p] for p, _ in JOBS[:j]) for j in range(5)]
    pb = [sum(len(resid[p]) for p, _ in JOBS[:j]) for j in range(5)]
    tok0 = {"lat": 0, "ctx": LAT}
    width = {"lat": 1536, "ctx": 384}
    with nc.Block() as block:
        @block.sync
        def _(e):
            e.dma_start(z[:, :, :], d["u"][0:CT].rearrange("m p t -> p m t")).then_inc(landed, 16)
            e.dma_start(tf[:, :], d["tab_f"]).then_inc(landed, 16)
            e.dma_start(ti[:, :], d["tab_i"]).then_inc(landed, 16)
            for j, (part, order) in enumerate(JOBS):
                if j:
                    e.wait_ge(sp_read, pb[j])
                e.dma_start(spec[:, 0:2 * len(resid[part]), :], d["spec_" + part][order]).then_inc(spec_in, 16)
                if j:
                    e.wait_ge(z_ready, j)
                e.dma_start(gate[:, :, :], d["u"][CT * (1 + order):CT * (2 + order)].rearrange("m p t -> p m t")
                            ).then_inc(gate_in, 16)
            e.wait_ge(gate_in, 64)

        @block.tensor
        def _(e):
            e.wait_ge(landed, 48)
            for j, (part, order) in enumerate(JOBS):
                if j:
                    e.wait_ge(z_ready, j)
                for m in range(blocks[part]):
                    for ct in range(CT):
                        c = tok0[part] + m * P
                        tr = e.transpose(k.bank[:, m, ct * P:(ct + 1) * P], z[:, ct, c:c + P], k.ident[:, :])
                    tr.then_inc(zt_full, 1)
                e.wait_ge(xh_ready, j + 1)
                for pos, r in enumerate(resid[part]):
                    b = 2 * (pos % 4)
                    if pos >= 4:
                        e.wait_ge(sp_read, pb[j] + pos - 3)
                    forward(e, k, tf, xh, r, spread[part][r], k.bank[:, b, :], k.bank[:, b + 1, :]).then_inc(sp_full, 1)
                e.wait_ge(sp_read, pb[j + 1])
                for ct in range(CT):
                    if ct >= 2:
                        e.wait_ge(yr_read, j * CT + ct - 1)
                    out = k.acc[ct % 2]
                    for pos, r in enumerate(resid[part]):
                        o = yo[part][r]
                        mm = inverse(e, ti, ys, r, pos, ct, out[:, o:o + (P if r in (0, 6) else 2 * P)])
                    mm.then_inc(yr_full, 1)

        @block.scalar
        def _(e):
            for j, (part, order) in enumerate(JOBS):
                for m in range(blocks[part]):
                    e.wait_ge(zt_full, zb[j] + m + 1)
                    e.activation(zt[:, m, :], k.bank[:, m, :], ACT.Copy).then_inc(zt_read, 1)
                for ct in range(CT):
                    e.wait_ge(yr_full, j * CT + ct + 1)
                    e.activation(yr[:, ct, 0:width[part]], k.acc[ct % 2][:, 0:width[part]], ACT.Copy).then_inc(yr_read, 1)

        @block.vector
        def _(e):
            steps = Steps(e, steps_sem)

            def tt(o, a, b, op):
                steps(e.tensor_tensor(o, a, b, op))

            def fma(o, a, c, b, op=ALU.add):
                steps(e.scalar_tensor_tensor(out=o, in0=a, scalar=c, in1=b, op0=ALU.mult, op1=op))

            def products(j, part):
                for pos in range(len(resid[part])):
                    e.wait_ge(sp_full, pb[j] + pos + 1)
                    b = 2 * (pos % 4)
                    zr, zi = k.bank[:, b, :], k.bank[:, b + 1, :]
                    hr, hi = spec[:, 2 * pos, :], spec[:, 2 * pos + 1, :]
                    tt(t[0][:, :], zr, hr, ALU.mult)
                    tt(t[1][:, :], zi, hi, ALU.mult)
                    tt(ys[:, 2 * pos, :], t[0][:, :], t[1][:, :], ALU.subtract)
                    tt(t[0][:, :], zr, hi, ALU.mult)
                    tt(t[1][:, :], zi, hr, ALU.mult)
                    e.tensor_tensor(ys[:, 2 * pos + 1, :], t[0][:, :], t[1][:, :], ALU.add).then_inc(sp_read, 1)
                    e.wait_ge(sp_read, pb[j] + pos + 1)

            def back_lat():
                y = lambda r, im=0, n=P: yr[:, :, YO_LAT[r] + im * P:YO_LAT[r] + im * P + n]
                buf = lambda n, w=P: i_tmp[:, n * 512:n * 512 + 4 * w].rearrange("p (c t) -> p c t", c=CT)
                ps, qw = buf(0, 2 * P), buf(2, 2 * P)
                u, v = [buf(4 + n) for n in range(3)], [buf(7 + n) for n in range(3)]
                ev, od, od2 = buf(10), buf(11), buf(12)
                out = lambda m: cv[:, :, m * P:(m + 1) * P]
                tt(ps, y(1, n=2 * P), y(5, n=2 * P), ALU.add)
                tt(qw, y(1, n=2 * P), y(5, n=2 * P), ALU.subtract)
                p_, s_, q_, w_ = ps[:, :, 0:P], ps[:, :, P:], qw[:, :, 0:P], qw[:, :, P:]
                tt(u[0], y(0), y(4), ALU.add)
                fma(ev, y(4), -0.5, y(0))
                fma(u[1], y(4, 1), -S3, ev)
                fma(u[2], y(4, 1), S3, ev)
                tt(v[0], y(6), y(2), ALU.add)
                fma(ev, y(2), -0.5, y(6))
                fma(v[1], y(2, 1), S3, ev)
                fma(v[2], y(2, 1), -S3, ev)

                def emit(m, o):
                    tt(ev, u[m % 3], v[m % 3], ALU.subtract if m % 2 else ALU.add)
                    tt(out(m + 2), ev, o, ALU.subtract)
                    if m >= 4:
                        tt(out(m - 4), ev, o, ALU.add)

                tt(od, p_, y(3), ALU.add)
                emit(0, od)
                fma(od2, s_, -0.5, y(3, 1), ALU.subtract)
                fma(od, q_, S3, od2)
                emit(1, od)
                fma(od, q_, -S3, od2)
                emit(5, od)
                fma(od2, p_, 0.5, y(3), ALU.subtract)
                fma(od, w_, -S3, od2)
                emit(2, od)
                tt(od, y(3, 1), s_, ALU.subtract)
                emit(3, od)
                fma(od2, p_, -0.5, y(3))
                fma(od, w_, -S3, od2)
                emit(4, od)

            def back_ctx():
                re, im, r0 = yr[:, :, 0:P], yr[:, :, P:2 * P], yr[:, :, 2 * P:3 * P]
                tmp = i_tmp[:, 0:512].rearrange("p (c t) -> p c t", c=CT)
                fma(tmp, re, -0.5, r0)
                fma(cv[:, :, 0:P], im, -S3, tmp)
                fma(cv[:, :, P:2 * P], im, S3, tmp)

            for j, (part, order) in enumerate(JOBS):
                c, n = tok0[part], blocks[part] * P
                e.wait_ge(zt_read, zb[j + 1])
                if part == "lat":
                    butterfly_lat(e, steps, zt, xh, g_tmp)
                else:
                    butterfly_ctx(e, steps, zt, xh)
                e.sem_inc(xh_ready, 1)
                e.wait_ge(spec_in, 16 * (j + 1))
                products(j, part)
                e.wait_ge(yr_read, CT * (j + 1))
                if part == "lat":
                    back_lat()
                else:
                    back_ctx()
                for ct in range(CT):
                    fma(cv[:, ct, 0:n], z[:, ct, c:c + n], k.hy_bias[:, order * CT + ct:order * CT + ct + 1], cv[:, ct, 0:n])
                e.wait_ge(gate_in, 16 * (j + 1))
                e.tensor_tensor(z[:, :, c:c + n], cv[:, :, 0:n], gate[:, :, c:c + n], ALU.mult).then_inc(z_ready, 1)
                e.wait_ge(z_ready, j + 1)



def output_items(k, name, kt, rhs, tokens, layer, part, square, load_x=False, store=False):
    nc, d, ph = k.nc, k.d, PH[name]
    w0, a0 = ph.w0, ph.a0
    sq_base = k.sqs
    x_in, cleared, stored = k.sem(name + "_x_in"), k.sem(name + "_cleared"), k.sem(name + "_stored")
    steps_sem = k.sem(name + "_steps")
    sq = k.at("sq_" + name, R0 + 18944, [P, 2, T])
    streams = ((0, LAT), (LAT, T))[:1 + (tokens > LAT)]
    gates = k.mods[:, 96 * layer:96 * layer + 96].rearrange("p (m w) -> p m w", w=2)
    with nc.Block() as block:
        @block.sync
        def _(e):
            if load_x:
                e.dma_start(k.x[:, :, :], d["x"]).then_inc(x_in, 16)
            sync_weights(k, e, ph)
            if load_x:
                e.wait_ge(x_in, 16)

        @block.tensor
        def _(e):
            with e.Fori(0, ph.pairs) as i:
                for s in range(2):
                    item(k, e, s, i + w0, i + a0, kt, rhs, tokens)

        @block.vector
        def _(e):
            if load_x:
                e.wait_ge(x_in, 16)
            with e.Fori(0, ph.pairs) as i:
                for s in range(2):
                    e.wait_ge(k.acc_full[s], i + (a0 + 1))
                    for n, (a, b) in enumerate(streams):
                        ins = e.scalar_tensor_tensor(
                            out=k.x[:, i * 2 + s, a:b], in0=k.acc[s][:, a:b], scalar=gates[:, i * 2 + (8 * part + s), n:n + 1],
                            in1=k.x[:, i * 2 + s, a:b], op0=ALU.mult, op1=ALU.add)
                    ins.then_inc(k.acc_free[s], 1)

        if square:
            @block.scalar
            def _(e):
                with e.Fori(0, ph.pairs) as i:
                    for s in range(2):
                        e.wait_ge(k.acc_free[s], i + (a0 + 2))
                        e.wait_ge(k.ss_done, i * 2 + (sq_base + s - 1))
                        e.activation(sq[:, s, 0:tokens], k.x[:, i * 2 + s, 0:tokens], ACT.Square).then_inc(k.sq_ready, 1)

            @block.gpsimd
            def _(e):
                e.memset(k.ss[:, 0:tokens], 0.0).then_inc(cleared, 1)
                e.wait_ge(cleared, 1)
                with e.Fori(0, ph.pairs) as i:
                    for s in range(2):
                        e.wait_ge(k.sq_ready, i * 2 + (sq_base + s + 1))
                        e.tensor_tensor(k.ss[:, 0:tokens], k.ss[:, 0:tokens], sq[:, s, 0:tokens],
                                        ALU.add).then_inc(k.ss_done, 1)
                        e.wait_ge(k.ss_done, i * 2 + (sq_base + s + 1))

        if store:
            @block.scalar
            def _(e):
                with e.Fori(0, ph.pairs) as i:
                    for s in range(2):
                        e.wait_ge(k.acc_free[s], i + (a0 + 2))
                        e.dma_start(d["out"][:, i * 2 + s, :], k.x[:, i * 2 + s, 0:LAT]).then_inc(stored, 16)
                e.wait_ge(stored, 16 * KT)
    if square:
        k.sqs += KT


def ffn(k, layer, last):
    nc = k.nc
    n = 2 * layer + 1
    tokens = T if layer == 0 else LAT
    hid = k.at(f"hid{layer}", R0, [P, HG, T])
    sg = k.at(f"silu{layer}", R0 + HG * T, [P, T])
    for g in range(GROUPS):
        ph = PH[f"ffn_in{layer}{g}"]
        w0, a0 = ph.w0, ph.a0
        norm = Norm(k, n) if g == 0 else None
        steps_sem, silu_ready = k.sem(f"ffn_steps{layer}{g}"), k.sem(f"silu_ready{layer}{g}")
        with nc.Block() as block:
            @block.sync
            def _(e):
                sync_weights(k, e, ph)

            @block.tensor
            def _(e):
                if norm:
                    norm.tensor(k, e)
                with e.Fori(0, HG) as i:
                    for s in range(2):
                        item(k, e, s, i + w0, i + a0, KT, lambda kk: k.h[:, kk, :], tokens, h_base=n * KT)

            @block.scalar
            def _(e):
                if norm:
                    norm.scalar(k, e)
                with e.Fori(0, HG) as i:
                    e.wait_ge(k.acc_full[0], i + (a0 + 1))
                    e.wait_ge(k.acc_free[1], i + (a0 + 1))
                    e.activation(sg[:, 0:tokens], k.acc[0][:, 0:tokens], ACT.Silu).then_inc(k.acc_free[0], 1)

            @block.vector
            def _(e):
                if norm:
                    norm.vector(k, e, Steps(e, steps_sem))
                with e.Fori(0, HG) as i:
                    e.wait_ge(k.acc_free[0], i + (a0 + 2))
                    e.wait_ge(k.acc_full[1], i + (a0 + 1))
                    e.tensor_tensor(hid[:, i, 0:tokens], sg[:, 0:tokens], k.acc[1][:, 0:tokens],
                                    ALU.mult).then_inc(k.acc_free[1], 1)
        output_items(k, f"ffn_out{layer}{g}", HG, lambda kk: hid[:, kk, :], tokens, layer, 5,
                     square=(g == GROUPS - 1 and not last), store=(g == GROUPS - 1 and last))



def rg_lru(k):
    nc, d, ph = k.nc, k.d, PH["rg_in"]
    w0, a0 = ph.w0, ph.a0
    norm = Norm(k, 2)
    y = k.at("y_w", R0, [P, RT, LAT])
    at = R0 + RT * LAT
    a = k.at("rg_a", at, [P, 2, T])
    th = k.at("rg_th", at + 2 * T, [P, 2, T])
    rg = k.at("rg_g", at + 4 * T, [P, 4, T])
    xc = k.at("rg_xc", at + 8 * T, [P, T])
    gg = k.at("rg_gg", at + 9 * T, [P, LAT])
    gw = k.at("rg_gw", at + 9 * T + LAT, [P, 4, P])
    centre, conv, gw_in, steps_sem = k.sem("r_centre"), k.sem("r_conv"), k.sem("r_gw"), k.sem("r_steps")
    sig, decay, root, v_ready, y_done, gelu_done = (k.sem("r_" + n) for n in ("sig", "decay", "root", "v", "y", "gelu"))
    acts = k.sem("r_acts")
    taps = k.rg_w[:, :].rearrange("p (m t) -> p m t", t=4)
    bias = k.rg_ba[:, :].rearrange("p (n g) -> p n g", g=4)
    exp_scale = k.rg_sp[:, 0:20].rearrange("p (n g) -> p n g", g=2)
    tanh_scale = k.rg_sp[:, 60:80].rearrange("p (n g) -> p n g", g=2)
    with nc.Block() as block:
        @block.sync
        def _(e):
            e.dma_start(gw[:, :, :], d["rg_gw"][0]).then_inc(gw_in, 16)

            def gates(i):
                e.wait_ge(k.acc_full[1], i * 3 + (a0 + 3))
                e.dma_start(gw[:, :, :], d["rg_gw"][i + 1]).then_inc(gw_in, 16)
            sync_weights(k, e, ph, between=gates)

        @block.tensor
        def _(e):
            norm.tensor(k, e)
            rhs = lambda kk: k.h[:, kk, :]
            with e.Fori(0, RT) as i:
                item(k, e, 0, i + w0, i * 3 + a0, KT, rhs, T, h_base=norm.h_base)
                item(k, e, 1, i + w0, i * 3 + a0, KT, rhs, LAT)
                e.wait_ge(gw_in, i * 16 + 16)
                e.wait_ge(conv, i + 1)
                for g in range(4):
                    s = g % 2
                    e.wait_ge(k.acc_free[s], i * 3 + (a0 + 2 + g // 2))
                    for c, n in CHUNKS[T]:
                        mm = e.matmul(k.acc[s][:, c:c + n], gw[:, g, :], xc[:, c:c + n], start=True, stop=True)
                    mm.then_inc(k.acc_full[s], 1)

        @block.scalar
        def _(e):
            norm.scalar(k, e)
            e.sem_inc(y_done, 1)
            with e.Fori(0, RT) as i:
                e.wait_ge(k.acc_full[0], i * 3 + (a0 + 1))
                e.wait_ge(y_done, i + 1)
                e.activation(xc[:, :], k.acc[0][:, 0:T], ACT.Identity, scale=taps[:, i, 2:3],
                             bias=k.rg_b[:, bass.ds(i, 1)]).then_inc(centre, 1)
                e.wait_ge(k.acc_full[1], i * 3 + (a0 + 1))
                e.activation(gg[:, :], k.acc[1][:, 0:LAT], ACT.Gelu_apprx_tanh).then_inc(k.acc_free[1], 1)
                for g in range(4):
                    s = g % 2
                    e.wait_ge(k.acc_full[s], i * 3 + (a0 + 2 + g // 2))
                    e.activation(rg[:, g, :], k.acc[s][:, 0:T], ACT.Sigmoid, bias=bias[:, i, g:g + 1]
                                 ).then_inc(k.acc_free[s], 1)
                e.wait_ge(k.acc_free[0], i * 3 + (a0 + 4))
                e.wait_ge(k.acc_free[1], i * 3 + (a0 + 4))
                for dr in range(2):
                    e.activation(a[:, dr, :], rg[:, 2 * dr, :], ACT.Exp, scale=exp_scale[:, i, dr:dr + 1]).then_inc(acts, 1)
                    e.activation(th[:, dr, :], rg[:, 2 * dr, :], ACT.Tanh, scale=tanh_scale[:, i, dr:dr + 1]).then_inc(acts, 1)
                e.wait_ge(acts, i * 4 + 4)
                for dr in range(2):
                    e.activation(rg[:, 2 * dr, :], a[:, dr, :], ACT.Square).then_inc(decay, 1)
                for dr in range(2):
                    e.wait_ge(v_ready, i * 2 + (dr + 1))
                    e.activation(th[:, dr, :], th[:, dr, :], ACT.Sqrt).then_inc(root, 1)

        @block.vector
        def _(e):
            steps = Steps(e, steps_sem)
            norm.vector(k, e, steps)
            with steps.loop(RT, 14) as i:
                e.wait_ge(centre, i + 1)
                n = 0
                for lo0, hi0 in ((0, LAT), (LAT, T)):
                    for tap, sh in ((0, -2), (1, -1), (3, 1)):
                        lo, hi = lo0 + max(0, -sh), hi0 - max(0, sh)
                        ins = e.scalar_tensor_tensor(out=xc[:, lo:hi], in0=k.acc[0][:, lo + sh:hi + sh],
                                                     scalar=taps[:, i, tap:tap + 1], in1=xc[:, lo:hi],
                                                     op0=ALU.mult, op1=ALU.add)
                        n += 1
                        if n < 6:
                            steps(ins)
                        else:
                            ins.then_inc(k.acc_free[0], 1)
                e.wait_ge(k.acc_free[0], i * 3 + (a0 + 2))
                e.sem_inc(conv, 1)
                e.wait_ge(decay, i * 2 + 2)
                for dr in range(2):
                    steps(e.tensor_tensor(rg[:, 2 * dr + 1, :], rg[:, 2 * dr + 1, :], xc[:, :], ALU.mult))
                    e.scalar_tensor_tensor(out=th[:, dr, :], in0=rg[:, 2 * dr, :], scalar=1.0, in1=th[:, dr, :],
                                           op0=ALU.add, op1=ALU.mult).then_inc(v_ready, 1)
                for dr in range(2):
                    e.wait_ge(root, i * 2 + (dr + 1))
                    steps(e.tensor_tensor(th[:, dr, :], th[:, dr, :], rg[:, 2 * dr + 1, :], ALU.mult))
                steps(e.tensor_tensor_scan(rg[:, 0, LAT:T], a[:, 0, LAT:T], th[:, 0, LAT:T], 0.0, ALU.mult, ALU.add))
                steps(e.tensor_tensor_scan(rg[:, 0, 0:LAT], a[:, 0, 0:LAT], th[:, 0, 0:LAT], rg[:, 0, T - 1:T],
                                           ALU.mult, ALU.add))
                steps(e.tensor_tensor_scan(rg[:, 2, ::-1], a[:, 1, ::-1], th[:, 1, ::-1], 0.0, ALU.mult, ALU.add))
                steps(e.tensor_tensor(rg[:, 0, 0:LAT], rg[:, 0, 0:LAT], rg[:, 2, 0:LAT], ALU.add))
                steps(e.tensor_tensor(y[:, i, :], rg[:, 0, 0:LAT], gg[:, :], ALU.mult))
                e.sem_inc(y_done, 1)



def program(nc, dram):
    with ExitStack() as ctx:
        k = Kernel(nc, ctx, dram)
        k.coef_a = lambda n, who, kk: k.coef[:, (n * 2 + who) * 16 + kk:(n * 2 + who) * 16 + kk + 1]
        k.coef_b = lambda n, who, kk: k.coef[:, (n * 2 + who) * 16 + 8 + kk:(n * 2 + who) * 16 + 9 + kk]
        load_constants(k)
        filters(k)
        adaln(k)
        even_in(k)
        latents(k)
        attention(k)
        hyena(k)
        z = k.at("hyT", X0 + 26624, [P, CT, T])
        attT = k.at("attT", ATT0, [P, 4, T])
        output_items(k, "ev_out", KT, lambda kk: z[:, kk, :] if kk < CT else attT[:, kk - CT, :], T, 0, 2,
                     square=True, load_x=True)
        ffn(k, 0, last=False)
        rg_lru(k)
        y = k.at("y", R0, [P, RT, LAT])
        output_items(k, "rg_out", RT, lambda kk: y[:, kk, :], LAT, 1, 2, square=True)
        ffn(k, 1, last=True)



def _tables():
    t0, q = np.arange(P)[:, None], np.arange(P)[None, :]
    fwd, inv = [], []
    for r in ORDER_LAT:
        ang = 2.0 * np.pi * (t0 * q / P + r * t0 / N_LAT)
        c, s = np.cos(ang), np.sin(ang)
        two = 1.0 if r in (0, 6) else 2.0
        if r in (0, 6):
            fwd += [c, -s]
            inv += [-s.T, c.T]
        else:
            fwd += [c, s, -s]
            inv += [-two * s.T, two * c.T, two * s.T]
    return tuple(np.concatenate(x, axis=1).astype(np.float32) for x in (fwd, inv))


def _filter_constants():
    zs, wins = [], []
    for length, n in ((LAT, N_LAT), (CTX, N_CTX)):
        kk = np.arange(length, dtype=np.float32)
        t = (kk / np.float32(max(length - 1, 1)))[:, None]
        bands = (EMB - 1) // 2
        ang = np.float32(2.0 * math.pi / length) * kk[:, None] * np.linspace(1e-4, bands - 1, bands, dtype=np.float32)[None, :]
        zs.append(np.concatenate([t, np.cos(ang), -np.sin(ang)], axis=-1).T)
        half = length // 2
        dist = np.abs(kk - half) / np.float32(max(half, 1))
        deltas = np.abs(np.linspace(math.log(1e-2) / 1.5, math.log(1e-2) / 0.3, D_HY, dtype=np.float32))
        wins.append((np.exp(-dist[:, None] * deltas[None, :]) / n).reshape(length // P, P, D_HY).transpose(1, 0, 2))
    return (np.ascontiguousarray(np.concatenate(zs, axis=1), dtype=np.float32),
            np.ascontiguousarray(np.concatenate(wins, axis=1), dtype=np.float32))


def _rope_tables():
    row = np.repeat(np.arange(LAT // GRID_W, dtype=np.float32), GRID_W)
    col = np.tile(np.arange(GRID_W, dtype=np.float32), LAT // GRID_W)
    inv = (np.float32(10000.0) ** (-np.arange(0, 16, 2, dtype=np.float32) / np.float32(16))).astype(np.float32)
    cos, sin = np.ones((T, ROPE), np.float32), np.zeros((T, ROPE), np.float32)
    for g, pos in enumerate((row, col)):
        ang = pos[:, None] * inv[None, :]
        c, s = np.cos(ang), np.sin(ang)
        cos[:LAT, 16 * g:16 * g + 16] = np.concatenate([c, c], axis=1)
        sin[:LAT, 16 * g:16 * g + 16] = np.concatenate([-s, s], axis=1)
    lay = lambda a: np.ascontiguousarray(a.reshape(NT, P, ROPE).transpose(1, 0, 2))
    return lay(cos), lay(sin)


def _tiles(w, m=P):
    kk, mm = w.shape
    return np.ascontiguousarray(w.reshape(kk // P, P, mm // m, m).transpose(2, 1, 0, 3))


def _columns(v):
    v = np.asarray(v)
    return np.ascontiguousarray(v.reshape(-1, P).T)


def layout(inp):
    a = {n: np.asarray(v) for n, v in inp.items()}
    o = {}
    x = np.concatenate([a["x"][0], a["ctx"][0]], axis=0)
    o["x"] = np.ascontiguousarray(x.T.reshape(KT, P, T).transpose(1, 0, 2))
    o["cc"] = np.ascontiguousarray(np.stack([a["c"][0], a["c_ctx"]], -1).reshape(KT, P, 2).transpose(1, 0, 2).reshape(P, 16))
    aw = a["ada_w"].reshape(2, KT, P, ADA_LOADS, ADA_M, P)
    o["ada_w"] = np.ascontiguousarray(aw.transpose(0, 3, 2, 1, 4, 5))
    o["ada_b"] = _columns(a["ada_b"])
    o["gains"] = _columns(np.stack([a["norm1_g"][0], a["norm2_g"][0], a["norm1_g"][1], a["norm2_g"][1]]))
    fi = a["ffn_w_in"].reshape(2, KT, P, 2, GROUPS, HG, P)
    o["ffn_in"] = np.ascontiguousarray(fi.transpose(0, 4, 5, 3, 2, 1, 6)).reshape(2, GROUPS, HG, 2, P, KT * P)
    fo = a["ffn_w_out"].reshape(2, GROUPS, HG, P, KT, P)
    o["ffn_out"] = np.ascontiguousarray(fo.transpose(0, 1, 4, 3, 2, 5)).reshape(2, GROUPS, KT, P, HG * P)
    ev = np.zeros((D, 18 * P), np.float32)
    w = a["ev_w_in"][0]
    ev[:, :w.shape[1]] = w
    o["ev_in"] = _tiles(ev).reshape(18, P, KT * P)
    o["ev_out"] = _tiles(a["ev_w_out"][0]).reshape(KT, P, KT * P)
    o["hy_w"] = np.ascontiguousarray(a["hy_short_w"][0].T.reshape(12, P, 3).transpose(1, 0, 2).reshape(P, 36))
    o["hy_b"] = _columns(a["hy_short_b"][0])
    o["hy_bias"] = _columns(a["hy_bias"][0])
    o["mlp"] = np.ascontiguousarray(np.stack([a["hy_b1"][0], a["hy_b2"][0], a["hy_freq"][0]], -1))
    o["hy_w1"], o["hy_w2"], o["hy_w3"] = a["hy_w1"][0], a["hy_w2"][0], a["hy_w3"][0]
    o["g_lat"] = _columns(np.concatenate([a["mla_q_norm_g"][0], a["mla_kv_norm_g"][0]]))
    o["w_uq"] = np.ascontiguousarray(a["mla_w_uq"][0].reshape(3, P, -1).transpose(1, 0, 2))
    o["w_ukv"] = np.ascontiguousarray(a["mla_w_ukv"][0].reshape(2, P, -1).transpose(1, 0, 2))
    o["gq"] = np.ascontiguousarray(np.broadcast_to(a["mla_qk_g_q"][0], (P, QD)))
    o["gk"] = np.ascontiguousarray(np.broadcast_to(a["mla_qk_g_k"][0], (P, QD)))
    ri = a["rg_w_in"][0].reshape(KT, P, 2, RT, P)
    o["rg_in"] = np.ascontiguousarray(ri[:, :, ::-1].transpose(3, 2, 1, 0, 4)).reshape(RT, 2, P, KT * P)
    o["rg_out"] = _tiles(a["rg_w_out"][0]).reshape(KT, P, RT * P)
    o["rg_w"] = np.ascontiguousarray(a["rg_conv_w"][0].T.reshape(RT, P, 4).transpose(1, 0, 2).reshape(P, 40))
    o["rg_b"] = _columns(a["rg_conv_b"][0])
    gw = np.stack([a["rg_w_a"][0], a["rg_w_x"][0]], axis=1)
    o["rg_gw"] = np.ascontiguousarray(gw.transpose(2, 3, 0, 1, 4)).reshape(RT, P, 4, P)
    gb = np.stack([a["rg_b_a"][0], a["rg_b_x"][0]], axis=1).reshape(2, 2, RT, P)
    o["rg_ba"] = np.ascontiguousarray(gb.transpose(3, 2, 0, 1)).reshape(P, 40)
    o["rg_lam"] = np.ascontiguousarray(a["rg_lambda"][0].reshape(2, RT, P).transpose(2, 1, 0)).reshape(P, 20)
    o["tab_f"], o["tab_i"] = _tables()
    o["filter_z"], o["window"] = _filter_constants()
    o["cos"], o["sin"] = _rope_tables()
    o["ident"] = np.eye(P, dtype=np.float32)
    o["ones"] = np.ones((P, P), np.float32)
    return o


def build(nc, arrays):
    dram = {n: nc.dram_tensor("in_" + n, v.shape, mybir.dt.from_np(v.dtype), kind="ExternalInput").ap()
            for n, v in arrays.items()}
    dram["u"] = nc.dram_tensor("u_scratch", (12, P, T), F32, kind="Internal").ap()
    dram["spec_lat"] = nc.dram_tensor("spec_lat", (2, P, 14, D_HY), F32, kind="Internal").ap()
    dram["spec_ctx"] = nc.dram_tensor("spec_ctx", (2, P, 4, D_HY), F32, kind="Internal").ap()
    dram["out"] = nc.dram_tensor("out_0", (P, KT, LAT), F32, kind="ExternalOutput").ap()
    program(nc, dram)


def kernel(**inputs):
    import concourse.bacc as bacc
    from concourse.bass_utils import run_bass_kernel_spmd

    nc = bacc.Bacc("TRN2", target_bir_lowering=False, num_devices=1)
    arrays = layout(inputs)
    build(nc, arrays)
    r = run_bass_kernel_spmd(nc, [{"in_" + n: v for n, v in arrays.items()}], core_ids=[0])
    out = r.results[0]["out_0"]
    return np.ascontiguousarray(out.transpose(1, 0, 2).reshape(D, LAT).T)[None]
```

```python
import math
from contextlib import ExitStack, contextmanager

import numpy as np

import concourse.bass as bass
from concourse import mybir

F32 = mybir.dt.float32
F32R = mybir.dt.float32r
ACT = mybir.ActivationFunctionType
ALU = mybir.AluOpType
AX_X = mybir.AxisListType.X

P = 128
D = 1024
KT = D // P
LAT, CTX = 1024, 256
T = LAT + CTX
NT = T // P
EPS = 1e-6
D_FF = 2816
HT = D_FF // P
HG = 2
GROUPS = HT // HG
D_HY = 512
CT = D_HY // P
Q_RANK, KV_RANK, ROPE = 384, 256, 32
NOPE, VD, HEADS = 64, 64, 8
QD = NOPE + ROPE
LT = (Q_RANK + KV_RANK) // P
MLA_SCALE = QD ** -0.5
D_RNN = 1280
RT = D_RNN // P
HID_F = 64
EMB = 33
GRID_W = 64
BANK = 512
CHUNKS = {T: [(0, 512), (512, 512), (1024, 256)], LAT: [(0, 512), (512, 512)]}

N_LAT, R_LAT, M_LAT = 1536, 12, 8
N_CTX, R_CTX, M_CTX = 384, 3, 2
ORDER_LAT = [0, 6, 1, 2, 3, 4, 5]
ORDER_CTX = [0, 4]
S3 = math.sqrt(3.0) / 2.0
TF = {}
TI = {}
_n = 0
for _r in ORDER_LAT:
    TF[_r] = TI[_r] = _n
    _n += 2 if _r in (0, 6) else 3
TAB = _n * P
YO_LAT = {1: 0, 2: 256, 3: 512, 4: 768, 5: 1024, 0: 1280, 6: 1408}
YO_CTX = {4: 0, 0: 256}
JOBS = [("lat", 0), ("lat", 1), ("ctx", 0), ("ctx", 1)]

BASE = 16512
C0 = 0
SS0 = 2000
WS = KT * P
W0 = SS0 + T
S0 = W0 + 2 * WS
X0 = S0 + 4 * WS
H0 = X0 + KT * T
R0 = H0 + 2 * KT * T
END = (229368 - BASE) // 32 * 8
ATT0 = END - 4 * T

CONSTS = {}
_at = C0
for _name, _len in (("ident", P), ("ones", P), ("mods", 2 * 96), ("coef", 4 * 32), ("gains", 4 * KT), ("ada_b", 2 * 48),
                    ("hy_w", 12 * 3), ("hy_b", 12), ("hy_bias", 8), ("mlp", 3), ("cc", 16), ("silu_c", 16),
                    ("g_lat", 5), ("rg_w", 40), ("rg_b", 10), ("rg_ba", 40), ("rg_lam", 20), ("rg_sp", 80),
                    ("stat", 16), ("rstd", 16)):
    CONSTS[_name] = (_at, _len)
    _at += -(-_len // 8) * 8
assert _at <= SS0


class Phase:

    def __init__(self, name, pairs, uses):
        self.name, self.pairs, self.uses = name, pairs, uses


FFN_PAIRS = GROUPS * 3
PHASES = [Phase("ev_in", 9, 9), Phase("ev_out", 4, 4), Phase("ffn0", FFN_PAIRS, GROUPS * 6),
          Phase("rg_in", RT, 3 * RT), Phase("rg_out", KT, KT // 2), Phase("ffn1", FFN_PAIRS, GROUPS * 6)]
PH = {}
_w = _a = 0
for _p in PHASES:
    _p.w0, _p.a0, _p.last = _w, _a, _p is PHASES[-1]
    _w += _p.pairs
    _a += _p.uses
    PH[_p.name] = _p
ALL_PAIRS = _w


class Steps:

    def __init__(self, eng, sem):
        self.eng, self.sem, self.n, self.extra = eng, sem, 0, 0

    def __call__(self, ins):
        self.n += 1
        ins.then_inc(self.sem, 1)
        self.eng.wait_ge(self.sem, self.extra + self.n)

    @contextmanager
    def loop(self, count, per):
        before = self.n
        with self.eng.Fori(0, count) as i:
            self.extra = i * per
            yield i
        assert self.n == before + per, (self.n - before, per)
        self.extra, self.n = 0, before + count * per


class Kernel:

    def __init__(self, nc, ctx, dram):
        self.nc, self.ctx, self.d, self.placed = nc, ctx, dram, {}
        self.bank = ctx.enter_context(nc.psum_tensor("bank", [P, 8, BANK], F32))
        self.acc = [self.bank[:, 3 * s:3 * s + 3, :].rearrange("p b n -> p (b n)") for s in range(2)]
        self.w = [self.at(f"w_raw{s}", W0 + s * WS, [P, WS]) for s in range(2)]
        self.w_hi = [self.at(f"w_hi{s}", S0 + 2 * s * WS, [P, WS], F32R) for s in range(2)]
        self.w_lo = [self.at(f"w_lo{s}", S0 + (2 * s + 1) * WS, [P, WS], F32R) for s in range(2)]
        self.x = self.at("x", X0, [P, KT, T])
        self.h_hi = self.at("h_hi", H0, [P, KT, T], F32R)
        self.h_lo = self.at("h_lo", H0 + KT * T, [P, KT, T], F32R)
        self.ss = self.at("ss", SS0, [P, T])
        self.c = c = {name: self.at("c_" + name, at, [P, n]) for name, (at, n) in CONSTS.items()}
        self.ident, self.ones, self.mods, self.coef = c["ident"], c["ones"], c["mods"], c["coef"]
        self.gains, self.ada_b, self.cc, self.silu_c = c["gains"], c["ada_b"], c["cc"], c["silu_c"]
        self.hy_w, self.hy_b, self.hy_bias, self.mlp = c["hy_w"], c["hy_b"], c["hy_bias"], c["mlp"]
        self.g_lat, self.stat, self.rstd = c["g_lat"], c["stat"], c["rstd"]
        self.rg_w, self.rg_b, self.rg_ba = c["rg_w"], c["rg_b"], c["rg_ba"]
        self.rg_lam, self.rg_sp = c["rg_lam"], c["rg_sp"]
        self.w_full = [self.sem(f"weights_landed{s}") for s in range(2)]
        self.split_hi = [self.sem(f"weights_hi{s}") for s in range(2)]
        self.split_lo = [self.sem(f"weights_lo{s}") for s in range(2)]
        self.half_done, self.hi_ready, self.h_mid = self.sem("half_done"), self.sem("hi_ready"), self.sem("h_mid")
        self.acc_full = [self.sem(f"sums_ready{s}") for s in range(2)]
        self.acc_free = [self.sem(f"sums_read{s}") for s in range(2)]
        self.stat_full, self.ms_ready, self.sd_ready = self.sem("stat_full"), self.sem("ms_ready"), self.sem("sd_ready")
        self.diag_ready, self.bc_full, self.rr_ready = self.sem("diag_ready"), self.sem("bc_full"), self.sem("rr_ready")
        self.xr_ready, self.h_ready = self.sem("xr_ready"), self.sem("h_ready")
        self.x_new, self.sq_ready, self.ss_done = self.sem("x_new"), self.sem("sq_ready"), self.sem("ss_done")
        self.sqs = 0

    def at(self, name, word, shape, dt=F32):
        key = (word, tuple(shape), str(dt))
        if key not in self.placed:
            self.placed[key] = self.nc.alloc_sbuf_tensor_at(name, shape, dt, offset=BASE + 4 * word)
        return self.placed[key]

    def sem(self, name):
        return self.ctx.enter_context(self.nc.semaphore(name))



def load_pair(k, e, p):
    for s in range(2):
        e.dma_start(k.w[s][:, :], k.d["weights"][p, s]).then_inc(k.w_full[s], 16)


def load_next(k, e, p):
    for s in range(2):
        e.wait_ge(k.split_lo[s], p + 1)
        e.dma_start(k.w[s][:, :], k.d["weights"][p + 1, s]).then_inc(k.w_full[s], 16)


def load_weights(k, e, ph):
    with e.Fori(0, ph.pairs - 1 if ph.last else ph.pairs) as i:
        load_next(k, e, i + ph.w0)


def full(use):
    return use + 2


def split_hi(k, e, s, pair, sem, count):
    e.wait_ge(k.w_full[s], pair * 16 + 16)
    e.wait_ge(sem, count)
    e.activation(k.w_hi[s][:, :], k.w[s][:, :], ACT.Copy).then_inc(k.split_hi[s], 1)


def split_lo(k, e, s, pair):
    e.wait_ge(k.split_hi[s], pair + 1)
    e.tensor_tensor(k.w_lo[s][:, :], k.w[s][:, :], k.w_hi[s][:, :].bitcast(F32), ALU.subtract
                    ).then_inc(k.split_lo[s], 1)


def product(k, e, s, out, kt, rhs, tokens, at=0, stride=P, first=True, last=True, ready=None, base=0):
    for kk in range(kt):
        if ready:
            e.wait_ge(ready, base + kk + 1)
        hi, lo = rhs(kk)
        c1 = at + kk * stride
        passes = ((k.w_hi[s], hi), (k.w_hi[s], lo), (k.w_lo[s], hi))
        for n, (w, x) in enumerate(passes):
            for c, m in CHUNKS[tokens]:
                mm = e.matmul(out[:, c:c + m], w[:, c1:c1 + P], x[:, c:c + m],
                              start=(first and kk == 0 and n == 0), stop=(last and kk == kt - 1 and n == 2))
    return mm


def item(k, e, s, pair, use, rhs, tokens, ready=None, base=0):
    e.wait_ge(k.split_lo[s], pair + 1)
    e.wait_ge(k.acc_free[s], use + 1)
    product(k, e, s, k.acc[s], KT, rhs, tokens, ready=ready, base=base).then_inc(k.acc_full[s], 1)



NORM_TILES = [NT, NT, NT, LAT // P]


class Norm:

    def __init__(self, k, n):
        self.n, self.tiles = n, NORM_TILES[n]
        self.tokens = self.tiles * P
        self.chunks = CHUNKS[self.tokens]
        self.diag = k.at(f"diag{n}", R0, [P, T])
        self.rr = k.at(f"rr{n}", R0 + T, [P, T])
        self.xr = k.at(f"xr{n}", R0 + 2 * T, [P, 2, T])
        self.diags = sum(NORM_TILES[:n])
        self.bcs = sum(len(CHUNKS[t * P]) for t in NORM_TILES[:n])
        self.h_base = n * KT

    def tensor(self, k, e):
        if k.sqs:
            e.wait_ge(k.ss_done, k.sqs)
        for j in range(self.tiles):
            mm = e.matmul(k.bank[:, 6, j:j + 1], k.ss[:, j * P:(j + 1) * P], k.ones[:, 0:1], start=True, stop=True)
        mm.then_inc(k.stat_full, 1)
        for c, (c0, n) in enumerate(self.chunks):
            e.wait_ge(k.diag_ready, self.diags + (c0 + n) // P)
            if c == 2:
                e.wait_ge(k.rr_ready, self.bcs + 1)
            e.matmul(k.bank[:, 7 - c % 2, 0:n], k.ones[:, :], self.diag[:, c0:c0 + n],
                     start=True, stop=True).then_inc(k.bc_full, 1)

    def vector(self, k, e, steps):
        t = self.tiles
        e.wait_ge(k.stat_full, self.n + 1)
        e.tensor_scalar(k.stat[:, 0:t], k.bank[:, 6, 0:t], 1.0 / D, EPS, ALU.mult, ALU.add).then_inc(k.ms_ready, 1)
        e.wait_ge(k.sd_ready, self.n + 1)
        steps(e.reciprocal(k.rstd[:, 0:t], k.stat[:, 0:t]))
        for j in range(t):
            e.tensor_scalar(self.diag[:, j * P:(j + 1) * P], k.ident[:, :], k.rstd[:, j:j + 1], None,
                            ALU.mult).then_inc(k.diag_ready, 1)
        e.wait_ge(k.rr_ready, self.bcs + len(self.chunks))
        def low(kk):
            e.wait_ge(k.hi_ready, self.h_base + kk + 1)
            e.tensor_tensor(k.h_lo[:, kk, 0:self.tokens], self.xr[:, kk % 2, 0:self.tokens],
                            k.h_hi[:, kk, 0:self.tokens].bitcast(F32), ALU.subtract).then_inc(k.h_ready, 1)

        for kk in range(KT):
            if kk >= 2:
                low(kk - 2)
                e.wait_ge(k.h_ready, self.h_base + kk - 1)
            e.tensor_tensor(self.xr[:, kk % 2, 0:self.tokens], k.x[:, kk, 0:self.tokens], self.rr[:, 0:self.tokens],
                            ALU.mult).then_inc(k.xr_ready, 1)
        low(KT - 2)
        low(KT - 1)

    def scalar(self, k, e):
        t, n = self.tiles, self.n
        e.wait_ge(k.ms_ready, n + 1)
        e.activation(k.stat[:, 0:t], k.stat[:, 0:t], ACT.Sqrt).then_inc(k.sd_ready, 1)
        for c, (c0, m) in enumerate(self.chunks):
            e.wait_ge(k.bc_full, self.bcs + c + 1)
            e.activation(self.rr[:, c0:c0 + m], k.bank[:, 7 - c % 2, 0:m], ACT.Copy).then_inc(k.rr_ready, 1)
        for kk in range(KT):
            e.wait_ge(k.xr_ready, self.h_base + kk + 1)
            for who, (c0, c1) in enumerate(((0, LAT), (LAT, T))[:1 + (self.tokens > LAT)]):
                at = (n * 2 + who) * 2 * KT + kk
                half = self.xr[:, kk % 2, c0:c1]
                ins = e.activation(half, half, ACT.Identity, scale=k.coef_a(n, who, kk), bias=k.coef_b(n, who, kk))
            ins.then_inc(k.h_mid, 1)
            e.wait_ge(k.h_mid, self.h_base + kk + 1)
            e.activation(k.h_hi[:, kk, 0:self.tokens], self.xr[:, kk % 2, 0:self.tokens], ACT.Copy
                         ).then_inc(k.hi_ready, 1)



def load_constants(k):
    nc, d = k.nc, k.d
    landed = k.sem("constants_landed")
    names = ["ident", "ones", "gains", "ada_b", "hy_w", "hy_b", "hy_bias", "cc", "g_lat", "rg_w", "rg_b",
             "rg_ba", "rg_lam"]
    lam, sp, steps_sem, acts = k.rg_lam, k.rg_sp, k.sem("setup_steps"), k.sem("setup_acts")
    credit = k.sem("x_squared")
    sq = k.at("sq_first", H0, [P, 2, T])
    with nc.Block() as block:
        @block.sync
        def _(e):
            e.dma_start(k.x[:, :, :], d["x"]).then_inc(landed, 16)
            for name in names:
                e.dma_start(k.c[name][:, :], d[name]).then_inc(landed, 16)
            e.dma_start(k.mlp[0:HID_F, :], d["mlp"]).then_inc(landed, 16)
            load_pair(k, e, 0)
            e.wait_ge(landed, 16 * (len(names) + 2))

        @block.scalar
        def _(e):
            e.wait_ge(landed, 16 * (len(names) + 2))
            e.activation(k.silu_c[:, :], k.cc[:, :], ACT.Silu)
            e.activation(sp[:, 0:20], lam[:, :], ACT.Abs).then_inc(acts, 1)
            e.wait_ge(acts, 1)
            e.activation(sp[:, 20:40], sp[:, 0:20], ACT.Exp, scale=-1.0).then_inc(acts, 1)
            e.wait_ge(steps_sem, 2)
            e.activation(sp[:, 60:80], sp[:, 40:60], ACT.Ln).then_inc(acts, 1)
            for kk in range(KT):
                if kk >= 2:
                    e.wait_ge(k.ss_done, kk - 1)
                e.activation(sq[:, kk % 2, :], k.x[:, kk, :], ACT.Square).then_inc(k.sq_ready, 1)

        @block.vector
        def _(e):
            steps = Steps(e, steps_sem)
            e.wait_ge(acts, 2)
            steps(e.tensor_scalar(sp[:, 0:20], lam[:, :], -1.0, 0.0, ALU.mult, ALU.max))
            steps(e.tensor_scalar(sp[:, 40:60], sp[:, 20:40], 1.0, None, ALU.add))
            e.wait_ge(acts, 3)
            steps(e.tensor_tensor(sp[:, 20:40], sp[:, 0:20], sp[:, 60:80], ALU.add))
            steps(e.tensor_scalar(sp[:, 0:20], sp[:, 20:40], -8.0, None, ALU.mult))
            steps(e.tensor_scalar(sp[:, 60:80], sp[:, 20:40], 8.0, None, ALU.mult))

        @block.gpsimd
        def _(e):
            e.memset(k.ss[:, :], 0.0).then_inc(credit, 1)
            e.wait_ge(credit, 1)
            for kk in range(KT):
                e.wait_ge(k.sq_ready, kk + 1)
                e.tensor_tensor(k.ss[:, :], k.ss[:, :], sq[:, kk % 2, :], ALU.add).then_inc(k.ss_done, 1)
                e.wait_ge(k.ss_done, kk + 1)

        @block.tensor
        def _(e):
            for s in range(2):
                e.sem_inc(k.acc_free[s], 1)
                e.sem_inc(k.acc_full[s], 1)
    k.sqs += KT


ADA_M = 3
ADA_LOADS = 48 // ADA_M


def adaln(k):
    nc, d = k.nc, k.d
    w = [k.at(f"ada_w{s}", END - 2 * KT * ADA_M * P + s * KT * ADA_M * P, [P, KT, ADA_M, P]) for s in range(2)]
    full = [k.sem(f"ada_landed{s}") for s in range(2)]
    used, sums, read, steps_sem = k.sem("ada_used"), k.sem("ada_sums"), k.sem("ada_read"), k.sem("ada_steps")
    with nc.Block() as block:
        @block.sync
        def _(e):
            for l in range(2):
                if l == 0:
                    for s in range(2):
                        e.dma_start(w[s][:, :, :, :], d["ada_w"][0, s]).then_inc(full[s], 16)
                with e.Fori(1 - l, ADA_LOADS // 2) as i:
                    for s in range(2):
                        e.wait_ge(used, i * 2 + (l * ADA_LOADS + s - 1))
                        e.dma_start(w[s][:, :, :, :], d["ada_w"][l, i * 2 + s]).then_inc(full[s], 16)

        @block.tensor
        def _(e):
            for l in range(2):
                with e.Fori(0, ADA_LOADS // 2) as i:
                    for s in range(2):
                        e.wait_ge(full[s], i * 16 + (l * ADA_LOADS // 2 * 16 + 16))
                        for m in range(ADA_M):
                            for kk in range(KT):
                                mm = e.matmul(k.bank[:, 6 + l, bass.ds(i * (4 * ADA_M) + (s * ADA_M + m) * 2, 2)],
                                              w[s][:, kk, m, :], k.silu_c[:, 2 * kk:2 * kk + 2],
                                              start=(kk == 0), stop=(kk == KT - 1))
                        mm.then_inc(used, 1)

        @block.vector
        def _(e):
            steps = Steps(e, steps_sem)
            for l in range(2):
                e.wait_ge(used, (l + 1) * ADA_LOADS)
                mods = k.mods[:, 96 * l:96 * l + 96].rearrange("p (m w) -> p m w", w=2)
                bias = k.ada_b[:, 48 * l:48 * l + 48].unsqueeze(2).to_broadcast([P, 48, 2])
                steps(e.tensor_tensor(mods, k.bank[:, 6 + l, 0:96].rearrange("p (m w) -> p m w", w=2), bias, ALU.add))
                for which in range(2):
                    n = 2 * l + which
                    gain = k.gains[:, n * KT:(n + 1) * KT]
                    for who in range(2):
                        shift = mods[:, 24 * which:24 * which + 8, who]
                        scale = mods[:, 24 * which + 8:24 * which + 16, who]
                        a = k.coef[:, (n * 2 + who) * 16:(n * 2 + who) * 16 + 8]
                        b = k.coef[:, (n * 2 + who) * 16 + 8:(n * 2 + who) * 16 + 16]
                        steps(e.scalar_tensor_tensor(out=a, in0=scale, scalar=1.0, in1=gain, op0=ALU.add, op1=ALU.mult))
                        steps(e.tensor_copy(b, shift))



def butterfly_lat(e, steps, x, y, t):
    def add(o, a, b):
        steps(e.tensor_tensor(o, a, b, ALU.add))

    def sub(o, a, b):
        steps(e.tensor_tensor(o, a, b, ALU.subtract))

    def fma(o, a, c, b, op=ALU.add):
        steps(e.scalar_tensor_tensor(out=o, in0=a, scalar=c, in1=b, op0=ALU.mult, op1=op))

    def scale(o, a, c):
        steps(e.tensor_scalar(o, a, c, None, ALU.mult))

    add(t[:, 0:2], x[:, 0:2], x[:, 6:8])
    sub(t[:, 2:4], x[:, 0:2], x[:, 6:8])
    add(t[:, 4:6], t[:, 0:2], x[:, 3:5])
    add(t[:, 6], x[:, 2], x[:, 5])
    sub(t[:, 7:9], t[:, 0:2], x[:, 3:5])
    sub(t[:, 9], x[:, 2], x[:, 5])
    add(t[:, 0], t[:, 5], t[:, 6])
    add(y[:, 0], t[:, 4], t[:, 0])
    fma(y[:, 8], t[:, 0], -0.5, t[:, 4])
    sub(t[:, 1], t[:, 5], t[:, 6])
    scale(y[:, 9], t[:, 1], -S3)
    sub(t[:, 0], t[:, 8], t[:, 9])
    sub(y[:, 1], t[:, 7], t[:, 0])
    fma(y[:, 4], t[:, 0], 0.5, t[:, 7])
    add(t[:, 1], t[:, 8], t[:, 9])
    scale(y[:, 5], t[:, 1], -S3)
    sub(t[:, 0], x[:, 2], x[:, 4])
    sub(y[:, 6], t[:, 2], t[:, 0])
    fma(t[:, 4], t[:, 0], 0.5, t[:, 2])
    add(t[:, 1], t[:, 3], x[:, 5])
    sub(y[:, 7], x[:, 3], t[:, 1])
    fma(t[:, 5], t[:, 1], 0.5, x[:, 3])
    sub(t[:, 6], t[:, 3], x[:, 5])
    fma(y[:, 2], t[:, 6], S3, t[:, 4])
    fma(y[:, 10], t[:, 6], -S3, t[:, 4])
    add(t[:, 7], x[:, 2], x[:, 4])
    fma(y[:, 3], t[:, 7], -S3, t[:, 5], ALU.subtract)
    fma(y[:, 11], t[:, 7], S3, t[:, 5], ALU.subtract)


def butterfly_ctx(e, steps, x, y):
    steps(e.tensor_tensor(y[:, 0], x[:, 0], x[:, 1], ALU.add))
    steps(e.scalar_tensor_tensor(out=y[:, 2], in0=x[:, 1], scalar=-0.5, in1=x[:, 0], op0=ALU.mult, op1=ALU.add))
    steps(e.tensor_scalar(y[:, 3], x[:, 1], -S3, None, ALU.mult))


SPREAD_LAT = {0: (0,), 6: (1,), 1: (2, 3), 2: (4, 5), 3: (6, 7), 4: (8, 9), 5: (10, 11)}
SPREAD_CTX = {0: (0,), 4: (2, 3)}


def forward(e, k, tab, xh, r, spread, re, im):
    c = TF[r]
    tile = [tab[:, (c + n) * P:(c + n + 1) * P] for n in range(2 if len(spread) == 1 else 3)]
    if len(spread) == 1:
        e.matmul(re, tile[0], xh[:, spread[0], :], start=True, stop=True)
        return e.matmul(im, tile[1], xh[:, spread[0], :], start=True, stop=True)
    a, b = (xh[:, n, :] for n in spread)
    e.matmul(re, tile[0], a, start=True, stop=False)
    e.matmul(re, tile[1], b, start=False, stop=True)
    e.matmul(im, tile[0], b, start=True, stop=False)
    return e.matmul(im, tile[2], a, start=False, stop=True)


def inverse(e, tab, ys, r, pos, ct, out):
    c = TI[r]
    re, im = (ys[:, 2 * pos + n, ct * P:(ct + 1) * P] for n in range(2))
    if r in (0, 6):
        e.matmul(out, re, tab[:, (c + 1) * P:(c + 2) * P], start=True, stop=False)
        return e.matmul(out, im, tab[:, c * P:(c + 1) * P], start=False, stop=True)
    e.matmul(out, re, tab[:, (c + 1) * P:(c + 3) * P], start=True, stop=False)
    return e.matmul(out, im, tab[:, c * P:(c + 2) * P], start=False, stop=True)


def filters(k):
    nc, d = k.nc, k.d
    Q = H0
    hw = k.at("hw", Q, [P, NT, D_HY])
    xh = k.at("f_xh", Q + 5120, [P, 12, D_HY])
    spec = k.at("f_spec", Q + 11264, [P, 14, D_HY])
    tab = k.at("f_tab", Q + 18432, [P, TAB])
    win = k.at("window", Q + 20864, [P, NT, D_HY])
    arg = k.at("f_arg", Q + 25984, [P, T])
    tmp = k.at("f_tmp", Q + 27264, [P, T])
    zin = k.at("f_z", Q + 28544, [P, T])
    w3 = k.at("f_w3", Q + 28544, [P, 2 * D_HY])
    w12 = k.at("f_w12", Q + 29824, [P, 2 * HID_F])
    TWO_PI = 2.0 * math.pi
    C1 = 6.28125
    C2 = float(np.float32(TWO_PI - C1))
    C3 = float(np.float32(TWO_PI - C1 - C2))
    MAGIC = 1.5 * 2.0 ** 23
    PI = float(np.nextafter(np.float32(math.pi), np.float32(0)))
    landed, w3_landed, mm_full, arg_ready = k.sem("f_landed"), k.sem("f_w3_landed"), k.sem("f_sums"), k.sem("f_arg")
    sin_ready, steps_sem, tile_full, hw_ready = k.sem("f_sin"), k.sem("f_steps"), k.sem("f_tile"), k.sem("f_hw")
    xh_ready, spec_full, spec_read, stored = k.sem("f_xh"), k.sem("f_spec"), k.sem("f_spec_read"), k.sem("f_stored")
    npos = {"lat": len(ORDER_LAT), "ctx": len(ORDER_CTX)}
    jobs = [("lat", 0), ("ctx", 0), ("lat", 1), ("ctx", 1)]
    before = [sum(npos[p] for p, _ in jobs[:j]) for j in range(5)]
    with nc.Block() as block:
        @block.sync
        def _(e):
            e.dma_start(zin[0:EMB, :], d["filter_z"]).then_inc(landed, 16)
            e.dma_start(w12[0:EMB, 0:HID_F], d["hy_w1"]).then_inc(landed, 16)
            e.dma_start(w12[0:HID_F, HID_F:2 * HID_F], d["hy_w2"]).then_inc(landed, 16)
            e.dma_start(win[:, :, :], d["window"]).then_inc(landed, 16)
            e.dma_start(tab[:, :], d["tab_f"]).then_inc(landed, 16)
            e.wait_ge(arg_ready, 1)
            e.dma_start(w3[0:HID_F, :], d["hy_w3"]).then_inc(w3_landed, 16)
            for j, (part, order) in enumerate(jobs):
                n = 2 * npos[part]
                e.wait_ge(spec_read, before[j + 1])
                e.dma_start(d["spec_" + part][order], spec[:, 0:n, :]).then_inc(stored, 16)
            e.wait_ge(stored, 64)

        @block.tensor
        def _(e):
            e.wait_ge(landed, 80)
            for c, n in CHUNKS[T]:
                mm = e.matmul(k.acc[0][0:HID_F, c:c + n], w12[0:EMB, 0:HID_F], zin[0:EMB, c:c + n], start=True, stop=True)
            mm.then_inc(mm_full, 1)
            e.wait_ge(sin_ready, 1)
            for c, n in CHUNKS[T]:
                mm = e.matmul(k.acc[1][0:HID_F, c:c + n], w12[0:HID_F, HID_F:2 * HID_F], tmp[0:HID_F, c:c + n],
                              start=True, stop=True)
            mm.then_inc(mm_full, 1)
            e.wait_ge(sin_ready, 2)
            e.wait_ge(w3_landed, 16)
            for order in range(2):
                for t in range(NT):
                    g = order * NT + t
                    if g >= 2:
                        e.wait_ge(hw_ready, g - 1)
                    e.matmul(k.bank[:, 6 + g % 2, :], tmp[0:HID_F, t * P:(t + 1) * P],
                             w3[0:HID_F, order * D_HY:(order + 1) * D_HY], start=True, stop=True).then_inc(tile_full, 1)
                for j in (2 * order, 2 * order + 1):
                    part = jobs[j][0]
                    e.wait_ge(xh_ready, j + 1)
                    residues, spread = (ORDER_LAT, SPREAD_LAT) if part == "lat" else (ORDER_CTX, SPREAD_CTX)
                    for pos, r in enumerate(residues):
                        g = before[j] + pos
                        if g >= 3:
                            e.wait_ge(spec_read, g - 2)
                        b = 2 * (g % 3)
                        forward(e, k, tab, xh, r, spread[r], k.bank[:, b, :], k.bank[:, b + 1, :]).then_inc(spec_full, 1)

        @block.vector
        def _(e):
            steps = Steps(e, steps_sem)

            def reduce_angle(sums, n):
                rows = slice(0, HID_F)
                e.wait_ge(mm_full, n + 1)
                steps(e.tensor_scalar(arg[rows, :], sums[rows, 0:T], k.mlp[rows, n:n + 1], k.mlp[rows, 2:3], ALU.add, ALU.mult))
                steps(e.tensor_scalar(tmp[rows, :], arg[rows, :], 1.0 / TWO_PI, MAGIC, ALU.mult, ALU.add))
                steps(e.tensor_scalar(tmp[rows, :], tmp[rows, :], MAGIC, None, ALU.subtract))
                for c in (C1, C2, C3):
                    steps(e.scalar_tensor_tensor(out=arg[rows, :], in0=tmp[rows, :], scalar=-c, in1=arg[rows, :],
                                                 op0=ALU.mult, op1=ALU.add))
                e.tensor_scalar(arg[rows, :], arg[rows, :], PI, -PI, ALU.min, ALU.max).then_inc(arg_ready, 1)

            reduce_angle(k.acc[0], 0)
            reduce_angle(k.acc[1], 1)
            for order in range(2):
                for t in range(NT):
                    g = order * NT + t
                    e.wait_ge(tile_full, g + 1)
                    e.tensor_tensor(hw[:, t, :], k.bank[:, 6 + g % 2, :], win[:, t, :], ALU.mult).then_inc(hw_ready, 1)
                e.wait_ge(hw_ready, (order + 1) * NT)
                j = 2 * order
                if j:
                    e.wait_ge(spec_full, before[j])
                    e.wait_ge(stored, 16 * j)
                butterfly_lat(e, steps, hw[:, 0:M_LAT], xh, spec[:, 0:10])
                e.sem_inc(xh_ready, 1)
                e.wait_ge(spec_full, before[j + 1])
                butterfly_ctx(e, steps, hw[:, M_LAT:NT], xh)
                e.sem_inc(xh_ready, 1)

        @block.scalar
        def _(e):
            for n in range(2):
                e.wait_ge(arg_ready, n + 1)
                e.activation(tmp[0:HID_F, :], arg[0:HID_F, :], ACT.Sin).then_inc(sin_ready, 1)
            for j, (part, order) in enumerate(jobs):
                if j:
                    e.wait_ge(stored, 16 * j)
                for pos in range(npos[part]):
                    g = before[j] + pos
                    e.wait_ge(spec_full, g + 1)
                    b = 2 * (g % 3)
                    e.activation(spec[:, 2 * pos:2 * pos + 2, :], k.bank[:, b:b + 2, :], ACT.Copy).then_inc(spec_read, 1)



def even_in(k):
    nc, d, ph = k.nc, k.d, PH["ev_in"]
    norm = Norm(k, 0)
    lat = k.at("lat", R0, [P, LT, T])
    rope = k.at("rope", R0 + 6400, [P, T])
    uc = k.at("uc", R0 + 7680, [P, 2, T])
    centre, done, steps_sem, stored = k.sem("tap1"), k.sem("conv3_done"), k.sem("conv3_steps"), k.sem("u_stored")
    uc_free = k.sem("uc_free")
    w0, a0 = ph.w0, ph.a0
    HP = 6
    taps = k.hy_w[:, :].rearrange("p (m t) -> p m t", t=3)
    with nc.Block() as block:
        @block.sync
        def _(e):
            load_weights(k, e, ph)

        @block.tensor
        def _(e):
            norm.tensor(k, e)
            with e.Fori(0, ph.pairs) as i:
                for s in range(2):
                    item(k, e, s, i + w0, i + a0, k.rhs_h, T, ready=k.h_ready, base=norm.h_base)

        @block.scalar
        def _(e):
            norm.scalar(k, e)
            split_hi(k, e, 0, w0, k.acc_full[0], 1)
            with e.Fori(0, HP) as i:
                for s in range(2):
                    split_hi(k, e, 1 - s, i + (w0 + s), k.acc_full[1 - s], i + (a0 + 1 + s))
                    e.wait_ge(k.acc_full[s], full(i + a0))
                    e.wait_ge(uc_free, i * 2 + (s + 1))
                    e.activation(uc[:, s, :], k.acc[s][:, 0:T], ACT.Identity, scale=taps[:, i * 2 + s, 1:2],
                                 bias=k.hy_b[:, bass.ds(i * 2 + s, 1)]).then_inc(centre, 1)
            for j in range(LT + 1):
                s, pair = j % 2, HP + j // 2
                if j < LT:
                    split_hi(k, e, 1 - s, w0 + pair + s, k.acc_full[1 - s], a0 + pair + 1 + s)
                e.wait_ge(k.acc_full[s], full(a0 + pair))
                if j < LT:
                    e.activation(lat[:, j, :], k.acc[s][:, 0:T], ACT.Copy).then_inc(k.acc_free[s], 1)
                else:
                    e.activation(rope[0:ROPE, :], k.acc[s][0:ROPE, 0:T], ACT.Copy).then_inc(k.acc_free[s], 1)

        @block.vector
        def _(e):
            steps = Steps(e, steps_sem)
            norm.vector(k, e, steps)
            split_lo(k, e, 0, w0)
            with steps.loop(HP, 6) as i:
                for s in range(2):
                    split_lo(k, e, 1 - s, i + (w0 + s))
                    e.wait_ge(centre, i * 2 + (s + 1))
                    n = 0
                    for a, b in ((0, LAT), (LAT, T)):
                        for tap, lo, hi, sh in ((0, a + 1, b, -1), (2, a, b - 1, 1)):
                            ins = e.scalar_tensor_tensor(
                                out=uc[:, s, lo:hi], in0=k.acc[s][:, lo + sh:hi + sh],
                                scalar=taps[:, i * 2 + s, tap:tap + 1], in1=uc[:, s, lo:hi], op0=ALU.mult, op1=ALU.add)
                            n += 1
                            if n < 4:
                                steps(ins)
                            else:
                                ins.then_inc(k.acc_free[s], 1)
                    e.wait_ge(k.acc_free[s], i + (a0 + 2))
                    e.sem_inc(done, 1)
            for j in range(LT):
                split_lo(k, e, 1 - j % 2, w0 + HP + j // 2 + j % 2)

        @block.gpsimd
        def _(e):
            e.sem_inc(uc_free, 2)
            with e.Fori(0, HP) as i:
                for s in range(2):
                    e.wait_ge(done, i * 2 + (s + 1))
                    e.dma_start(d["u"][i * 2 + s], uc[:, s, :]).then_inc(stored, 16)
                    e.wait_ge(stored, i * 32 + (16 * s + 16))
                    e.sem_inc(uc_free, 1)


def rotate(e, steps, x, out, cos, sin, t1, heads):
    shape = [P, heads, ROPE]
    steps(e.tensor_tensor(t1, x, cos.unsqueeze(1).to_broadcast(shape), ALU.mult))
    halves = lambda a: a.rearrange("p h (g c) -> p h g c", g=2)
    sb = halves(sin.unsqueeze(1).to_broadcast(shape))
    xv, ov = halves(x), halves(out)
    return t1, xv, sb


def latents(k):
    nc, d = k.nc, k.d
    lat = k.at("lat", R0, [P, LT, T])
    rope = k.at("rope", R0 + 6400, [P, T])
    kT = k.at("kT", X0, [P, HEADS, T])
    qT = k.at("qT", X0 + 10240, [P, HEADS, T])
    v = k.at("v", X0 + 20480, [P, NT, HEADS * VD])
    wq = k.at("wq", X0 + 25600, [P, 3, HEADS * QD])
    wkv = k.at("wkv", X0 + 27904, [P, 2, 1024])
    gq = k.at("gq", X0 + 29952, [P, QD])
    gk = k.at("gk", X0 + 30048, [P, QD])
    cos = k.at("cos", X0 + 30144, [P, NT, ROPE])
    sin = k.at("sin", R0 + 7680, [P, NT, ROPE])
    lcur = k.at("lcur", S0, [P, 2, LT, P])
    sqc = k.at("sqc", S0 + 1280, [P, 2, LT, P])
    at = R0 + 8000
    assert at + 5056 <= END
    qb = k.at("qb", at, [P, 2, HEADS, QD])
    kb = k.at("kb", at + 1536, [P, 2, HEADS, QD])
    sqq = k.at("sqq", at + 3072, [P, HEADS, QD])
    sqk = k.at("sqk", at + 3840, [P, HEADS, NOPE])
    sqr = k.at("sqr", at + 4352, [P, ROPE])
    krow = k.at("krow", at + 4384, [P, 1, ROPE])
    kout = k.at("kout", at + 4416, [P, 1, ROPE])
    st = k.at("st", at + 4448, [P, 8])
    ss = k.at("hs", at + 4456, [P, 32])
    rcur = k.at("rcur", at + 4488, [P, 2, P])
    t1 = k.at("rot1", S0 + 2560, [P, HEADS, ROPE])
    t2 = k.at("rot2", S0 + 2816, [P, HEADS, ROPE])
    landed, folded = k.sem("m_landed"), k.sem("m_folded")
    cur, sq_ready = [k.sem(f"m_cur{s}") for s in range(2)], k.sem("m_sq")
    sums, tr_full = k.sem("m_sums"), k.sem("m_tr")
    ms, sd, hsq, hss, hsd, vout, tok = (k.sem("m_" + n) for n in ("ms", "sd", "hsq", "hss", "hsd", "v", "tok"))
    freed = [k.sem(f"m_freed{s}") for s in range(2)]
    steps_sem = k.sem("m_steps")
    HH = HEADS // 2
    qps = lambda s: k.bank[:, 4 * s:4 * s + 2, 0:HH * QD].rearrange("p b (h c) -> p b h c", c=QD)
    kvps = lambda s: k.bank[:, 4 * s + 2:4 * s + 4, :].rearrange("p b (h c) -> p b h c", c=NOPE + VD)
    two = lambda a: a.rearrange("p (b h) c -> p b h c", b=2)

    with nc.Block() as block:
        @block.sync
        def _(e):
            for t, name in ((wq, "w_uq"), (wkv, "w_ukv"), (cos, "cos"), (sin, "sin")):
                e.dma_start(t[:, :, :], d[name]).then_inc(landed, 16)
            e.dma_start(gq[:, :], d["gq"]).then_inc(landed, 16)
            e.dma_start(gk[:, :], d["gk"]).then_inc(landed, 16)
            e.wait_ge(landed, 96)

        @block.gpsimd
        def _(e):
            with e.Fori(0, NT // 2) as i:
                for s in range(2):
                    e.wait_ge(freed[s], i * 2 + 2)
                    e.tensor_copy(lcur[:, s, :, :], lat[:, :, bass.ds(i * 256 + s * P, P)]).then_inc(cur[s], 1)
                    e.tensor_copy(rcur[0:ROPE, s, :], rope[0:ROPE, bass.ds(i * 256 + s * P, P)]).then_inc(cur[s], 1)

        @block.tensor
        def _(e):
            e.wait_ge(folded, 5)
            with e.Fori(0, NT // 2) as i:
                for s in range(2):
                    e.wait_ge(freed[s], i * 2 + 2)
                    e.wait_ge(cur[s], i * 2 + 2)
                    for half in range(2):
                        for kk in range(3):
                            e.matmul(k.bank[:, 4 * s + half, 0:HH * QD], lcur[:, s, kk, :],
                                     wq[:, kk, half * HH * QD:(half + 1) * HH * QD], start=(kk == 0), stop=(kk == 2))
                        for kk in range(2):
                            e.matmul(k.bank[:, 4 * s + 2 + half, :], lcur[:, s, 3 + kk, :],
                                     wkv[:, kk, half * 512:(half + 1) * 512], start=(kk == 0), stop=(kk == 1))
                    e.transpose(k.bank[:, 4 * s + 1, 384:384 + ROPE], rcur[0:ROPE, s, :], k.ident[0:ROPE, 0:ROPE])
                    e.wait_ge(sq_ready, i * 2 + (s + 1))
                    for kk in range(LT):
                        c = 384 if kk < 3 else 386
                        mm = e.matmul(k.bank[:, 4 * s, c:c + 1], sqc[:, s, kk, :], k.ones[:, 0:1],
                                      start=kk in (0, 3), stop=kk in (2, 4))
                    mm.then_inc(sums, 1)
                for s in range(2):
                    e.wait_ge(tok, i * 2 + (s + 1))
                    e.wait_ge(vout, i * 2 + (s + 1))
                    for h in range(HEADS):
                        e.transpose(k.bank[0:QD, 4 * s + h // 4, (h % 4) * P:(h % 4 + 1) * P], qb[:, s, h, :], k.ident[:, :])
                    for h in range(HEADS):
                        mm = e.transpose(k.bank[0:QD, 4 * s + 2 + h // 4, (h % 4) * P:(h % 4 + 1) * P], kb[:, s, h, :],
                                         k.ident[:, :])
                    mm.then_inc(tr_full, 1)

        @block.scalar
        def _(e):
            with e.Fori(0, NT // 2) as i:
                for s in range(2):
                    e.wait_ge(cur[s], i * 2 + 2)
                    e.activation(sqc[:, s, :, :], lcur[:, s, :, :], ACT.Square).then_inc(sq_ready, 1)
                for s in range(2):
                    e.wait_ge(ms, i * 2 + (s + 1))
                    e.activation(st[:, 2:4], st[:, 0:2], ACT.Sqrt).then_inc(sd, 1)
                    e.wait_ge(hss, i * 4 + (2 * s + 1))
                    e.activation(two(sqq[:, :, :]), qps(s), ACT.Square, scale=st[:, 4:5]).then_inc(hsq, 1)
                    e.activation(two(sqk[:, :, :]), kvps(s)[:, :, :, 0:NOPE], ACT.Square, scale=st[:, 5:6]).then_inc(hsq, 1)
                    e.activation(sqr[:, :], k.bank[:, 4 * s + 1, 384:384 + ROPE], ACT.Square).then_inc(hsq, 1)
                    e.activation(v[:, i * 2 + s, :].rearrange("p (b h c) -> p b h c", b=2, c=VD), kvps(s)[:, :, :, NOPE:],
                                 ACT.Copy, scale=st[:, 5:6]).then_inc(vout, 1)
                    e.wait_ge(hss, i * 4 + (2 * s + 2))
                    e.activation(ss[:, 0:25], ss[:, 0:25], ACT.Sqrt).then_inc(hsd, 1)
                for s in range(2):
                    e.wait_ge(tr_full, i * 2 + (s + 1))
                    e.activation(qT[0:QD, :, bass.ds(i * 256 + s * P, P)].rearrange("p (b h) c -> p b h c", b=2),
                                 k.bank[0:QD, 4 * s:4 * s + 2, :].rearrange("p b (h c) -> p b h c", c=P),
                                 ACT.Copy).then_inc(freed[s], 1)

        @block.vector
        def _(e):
            for s in range(2):
                e.sem_inc(freed[s], 2)
            steps = Steps(e, steps_sem)
            e.wait_ge(landed, 96)
            for kk in range(3):
                e.tensor_scalar(wq[:, kk, :], wq[:, kk, :], k.g_lat[:, kk:kk + 1], None, ALU.mult).then_inc(folded, 1)
            for kk in range(2):
                e.tensor_scalar(wkv[:, kk, :], wkv[:, kk, :], k.g_lat[:, 3 + kk:4 + kk], None, ALU.mult).then_inc(folded, 1)
            with steps.loop(NT // 2, 48) as i:
                for s in range(2):
                    q, kk_, kr = qb[:, s, :, :], kb[:, s, :, :], k.bank[:, 4 * s + 1, 384:384 + ROPE]
                    e.wait_ge(sums, i * 2 + (s + 1))
                    steps(e.tensor_scalar(st[:, 0:1], k.bank[:, 4 * s, 384:385], 1.0 / Q_RANK, EPS, ALU.mult, ALU.add))
                    e.tensor_scalar(st[:, 1:2], k.bank[:, 4 * s, 386:387], 1.0 / KV_RANK, EPS, ALU.mult, ALU.add).then_inc(ms, 1)
                    e.wait_ge(sd, i * 2 + (s + 1))
                    e.reciprocal(st[:, 4:6], st[:, 2:4]).then_inc(hss, 1)
                    e.wait_ge(hsq, i * 6 + (3 * s + 3))
                    e.wait_ge(hss, i * 4 + (2 * s + 1))
                    steps(e.tensor_reduce(ss[:, 0:8], sqq[:, :, 0:NOPE], AX_X, ALU.add))
                    steps(e.tensor_reduce(ss[:, 8:16], sqk[:, :, :], AX_X, ALU.add))
                    steps(e.tensor_reduce(ss[:, 16:24], sqq[:, :, NOPE:QD], AX_X, ALU.add))
                    steps(e.tensor_reduce(ss[:, 24:25], sqr[:, :], AX_X, ALU.add))
                    steps(e.tensor_scalar(ss[:, 0:16], ss[:, 0:16], 1.0 / NOPE, EPS, ALU.mult, ALU.add))
                    e.tensor_scalar(ss[:, 16:25], ss[:, 16:25], 1.0 / ROPE, EPS, ALU.mult, ALU.add).then_inc(hss, 1)
                    e.wait_ge(hsd, i * 2 + (s + 1))
                    steps(e.reciprocal(ss[:, 0:25], ss[:, 0:25]))
                    steps(e.tensor_scalar(ss[:, 0:8], ss[:, 0:8], st[:, 4:5], None, ALU.mult))
                    steps(e.tensor_scalar(ss[:, 16:24], ss[:, 16:24], st[:, 4:5], None, ALU.mult))
                    steps(e.tensor_scalar(ss[:, 8:16], ss[:, 8:16], st[:, 5:6], None, ALU.mult))
                    bc = lambda a, n: a.rearrange("p (b h) -> p b h", b=2).unsqueeze(3).to_broadcast([P, 2, HH, n])
                    steps(e.tensor_tensor(two(q[:, :, 0:NOPE]), qps(s)[:, :, :, 0:NOPE], bc(ss[:, 0:8], NOPE), ALU.mult))
                    steps(e.tensor_tensor(two(q[:, :, NOPE:QD]), qps(s)[:, :, :, NOPE:QD], bc(ss[:, 16:24], ROPE), ALU.mult))
                    steps(e.tensor_tensor(two(kk_[:, :, 0:NOPE]), kvps(s)[:, :, :, 0:NOPE], bc(ss[:, 8:16], NOPE), ALU.mult))
                    steps(e.scalar_tensor_tensor(out=krow[:, 0, :], in0=kr, scalar=ss[:, 24:25], in1=gk[:, NOPE:QD],
                                                 op0=ALU.mult, op1=ALU.mult))
                    steps(e.tensor_tensor(q, q, gq[:, :].unsqueeze(1).to_broadcast([P, HEADS, QD]), ALU.mult))
                    steps(e.tensor_tensor(kk_[:, :, 0:NOPE], kk_[:, :, 0:NOPE],
                                          gk[:, 0:NOPE].unsqueeze(1).to_broadcast([P, HEADS, NOPE]), ALU.mult))
                    for x, out, tmp1, tmp2, n in ((q[:, :, NOPE:QD], q[:, :, NOPE:QD], t1[:, :, :], t2[:, :, :], HEADS),
                                                  (krow[:, :, :], kout[:, :, :], t1[:, 0:1, :], t2[:, 0:1, :], 1)):
                        tile = i * 2 + s
                        co = cos[:, tile, :].unsqueeze(1).to_broadcast([P, n, ROPE])
                        steps(e.tensor_tensor(tmp1, x, co, ALU.mult))
                        for a in range(2):
                            pick = lambda y, b: y.rearrange("p h (g c) -> p h g c", g=2)[:, :, :, 8 * b:8 * b + 8]
                            si = sin[:, tile, :].rearrange("p (g c) -> p g c", g=2)[:, :, 8 * a:8 * a + 8]
                            steps(e.tensor_tensor(pick(tmp2, a), pick(x, 1 - a),
                                                  si.unsqueeze(1).to_broadcast([P, n, 2, 8]), ALU.mult))
                        steps(e.tensor_tensor(out, tmp1, tmp2, ALU.add))
                    e.tensor_copy(kk_[:, :, NOPE:QD], kout[:, :, :].to_broadcast([P, HEADS, ROPE])).then_inc(tok, 1)
                for s in range(2):
                    e.wait_ge(tr_full, i * 2 + (s + 1))
                    e.tensor_copy(kT[0:QD, :, bass.ds(i * 256 + s * P, P)].rearrange("p (b h) c -> p b h c", b=2),
                                  k.bank[0:QD, 4 * s + 2:4 * s + 4, :].rearrange("p b (h c) -> p b h c", c=P)
                                  ).then_inc(freed[s], 1)


def attention(k):
    nc = k.nc
    kT = k.at("kT", X0, [P, HEADS, T])
    qT = k.at("qT", X0 + 10240, [P, HEADS, T])
    v = k.at("v", X0 + 20480, [P, NT, HEADS * VD])
    att = k.at("att_tok", X0 + 25600, [P, NT, HEADS * VD])
    assert X0 + 30720 == R0 and R0 + 7712 <= ATT0
    p = k.at("probs", R0, [P, 2, T])
    pT = k.at("probsT", R0 + 2560, [P, 2, NT, P])
    qcur = k.at("qcur", R0 + 5120, [P, 2, T])
    mx = k.at("mx", R0 + 7680, [P, 2])
    ng = k.at("ng", R0 + 7688, [P, 2])
    rs = k.at("rs", R0 + 7696, [P, 2])
    ri = k.at("ri", R0 + 7704, [P, 2])
    attT = k.at("attT", ATT0, [P, 4, T])
    q_ready, s_full, mx_ready, p_ready = k.sem("a_q"), k.sem("a_scores"), k.sem("a_max"), k.sem("a_p")
    t_full, t_read, pv_full, pv_out = k.sem("a_t"), k.sem("a_t_read"), k.sem("a_pv"), k.sem("a_out")
    max_made, inverse_ready = k.sem("a_max_made"), k.sem("a_inverse")
    aT_full, aT_read = k.sem("a_aT"), k.sem("a_aT_read")
    N = 2 * NT
    TURNS = HEADS // 2
    kinds = [(hp, j, NT, 0) if j < LAT // P else (hp, j, CTX // P, LAT) for hp in range(2) for j in range(NT)]
    groups = lambda keys: [(g, min(4, keys - g)) for g in range(0, keys, 4)]
    G = [sum(len(groups(kind[2])) for kind in kinds[:n]) for n in range(N + 1)]
    assert N % 2 == 0 and G[N] % 2 == 0

    class Turn:

        def __init__(self, i):
            self.i = i

        def kind(self, n):
            return kinds[n % N]

        def head(self, n):
            return self.i * 2 + (kinds[n % N][0] + 2 * (n // N))

        def step(self, n):
            return self.i * N + n

        def group(self, n):
            return self.i * G[N] + (G[n % N] + n // N * G[N])

    def turns(e, body):
        with e.Fori(0, TURNS - 1) as i:
            body(Turn(i), False)
        body(Turn(TURNS - 1), True)

    flat = lambda n: k.acc[n % 2]

    with nc.Block() as block:
        @block.gpsimd
        def _(e):
            for h in range(2):
                e.tensor_copy(qcur[0:QD, h, :], qT[0:QD, h, :]).then_inc(q_ready, 1)
            with e.Fori(0, TURNS - 1) as i:
                for hp in range(2):
                    e.wait_ge(s_full, i * N + (hp * NT + NT))
                    e.tensor_copy(qcur[0:QD, hp, :], qT[0:QD, i * 2 + (hp + 2), :]).then_inc(q_ready, 1)

        @block.tensor
        def _(e):
            e.sem_inc(pv_out, 2)
            e.sem_inc(t_read, 2)

            def scores(t, n, chunks):
                hp, j, keys, k0 = t.kind(n)
                if j == 0 and chunks[0] == 0:
                    e.wait_ge(q_ready, t.head(n) + 1)
                for c in chunks:
                    m = min(BANK, keys * P - c * BANK)
                    if m <= 0:
                        continue
                    mm = e.matmul(k.bank[:, 3 * (n % 2) + c, 0:m], qcur[0:QD, hp, j * P:(j + 1) * P],
                                  kT[0:QD, t.head(n), k0 + c * BANK:k0 + c * BANK + m], start=True, stop=True)
                    last = c == (keys * P - 1) // BANK
                if last:
                    mm.then_inc(s_full, 1)

            def body(t, ends):
                for n in range(N):
                    hp, j, keys, k0 = t.kind(n)
                    ahead = n + 2 < N or not ends
                    e.wait_ge(p_ready, t.step(n) + 1)
                    for g, (g0, m) in enumerate(groups(keys)):
                        last = g == len(groups(keys)) - 1
                        if last and ahead:
                            scores(t, n + 2, [0])
                        e.wait_ge(t_read, t.group(n) + (g + 1))
                        if g < 2:
                            e.wait_ge(pv_out, t.step(n) + 2)
                        for kt in range(g0, g0 + m):
                            tr = e.transpose(k.bank[:, 6 + (G[n] + g) % 2, (kt - g0) * P:(kt - g0 + 1) * P],
                                             p[:, n % 2, kt * P:(kt + 1) * P], k.ident[:, :])
                        tr.then_inc(t_full, 1)
                    if ahead and t.kind(n + 2)[2] > CTX // P:
                        scores(t, n + 2, [1, 2])
                    e.wait_ge(t_read, t.group(n) + (len(groups(keys)) + 2))
                    for kt in range(keys):
                        mm = e.matmul(k.bank[:, 6 + (G[n + 1] - 1) % 2, 256:256 + VD], pT[:, n % 2, kt, :],
                                      v[:, k0 // P + kt, bass.ds(t.head(n) * VD, VD)],
                                      start=(kt == 0), stop=(kt == keys - 1))
                    mm.then_inc(pv_full, 1)

            scores(Turn(0), 0, [0, 1, 2])
            scores(Turn(0), 1, [0, 1, 2])
            turns(e, body)
            e.wait_ge(pv_out, 2 + N * TURNS)
            for t in range(NT):
                if t >= 8:
                    e.wait_ge(aT_read, t - 7)
                for f in range(4):
                    tr = e.transpose(k.bank[:, t % 8, f * P:(f + 1) * P], att[:, t, f * P:(f + 1) * P], k.ident[:, :])
                tr.then_inc(aT_full, 1)

        @block.vector
        def _(e):
            def maximum(t, n):
                keys = t.kind(n)[2]
                e.wait_ge(s_full, t.step(n) + 1)
                e.reduce_max(mx[:, n % 2:n % 2 + 1], flat(n)[:, 0:keys * P], AX_X).then_inc(max_made, 1)
                e.wait_ge(max_made, t.step(n) + 1)
                e.tensor_scalar(ng[:, n % 2:n % 2 + 1], mx[:, n % 2:n % 2 + 1], -MLA_SCALE, None,
                                ALU.mult).then_inc(mx_ready, 1)

            def body(t, ends):
                for n in range(N):
                    hp, j, keys, k0 = t.kind(n)
                    if n + 2 < N or not ends:
                        maximum(t, n + 2)
                    e.wait_ge(p_ready, t.step(n) + 1)
                    e.reciprocal(ri[:, n % 2:n % 2 + 1], rs[:, n % 2:n % 2 + 1]).then_inc(inverse_ready, 1)
                    e.wait_ge(inverse_ready, t.step(n) + 1)
                    e.wait_ge(pv_full, t.step(n) + 1)
                    e.tensor_scalar(att[:, j, bass.ds(t.head(n) * VD, VD)], k.bank[:, 6 + (G[n + 1] - 1) % 2, 256:256 + VD],
                                    ri[:, n % 2:n % 2 + 1], None, ALU.mult).then_inc(pv_out, 1)

            maximum(Turn(0), 0)
            maximum(Turn(0), 1)
            turns(e, body)

        @block.scalar
        def _(e):
            def exps(t, n):
                keys = t.kind(n)[2]
                e.wait_ge(mx_ready, t.step(n) + 1)
                e.wait_ge(pv_out, t.step(n) + 1)
                e.activation(p[:, n % 2, 0:keys * P], flat(n)[:, 0:keys * P], ACT.Exp, bias=ng[:, n % 2:n % 2 + 1],
                             scale=MLA_SCALE, accum_out=rs[:, n % 2:n % 2 + 1]).then_inc(p_ready, 1)

            def body(t, ends):
                for n in range(N):
                    keys = t.kind(n)[2]
                    e.wait_ge(pv_out, t.step(n) + 1)
                    for g, (g0, m) in enumerate(groups(keys)):
                        e.wait_ge(t_full, t.group(n) + (g + 1))
                        e.activation(pT[:, n % 2, g0:g0 + m, :].rearrange("p a b -> p (a b)"),
                                     k.bank[:, 6 + (G[n] + g) % 2, 0:m * P], ACT.Copy).then_inc(t_read, 1)
                    if n + 1 < N or not ends:
                        exps(t, n + 1)

            exps(Turn(0), 0)
            turns(e, body)
            for t in range(NT):
                e.wait_ge(aT_full, t + 1)
                e.activation(attT[:, :, t * P:(t + 1) * P], k.bank[:, t % 8, :].rearrange("p (f c) -> p f c", c=P),
                             ACT.Copy).then_inc(aT_read, 1)


def hyena(k):
    nc, d = k.nc, k.d
    at = X0
    xh = k.at("h_xh", at, [P, 14, D_HY])
    yr = k.at("h_yr", at, [P, CT, 1536])
    ys = k.at("h_ys", at + 7168, [P, 14, D_HY])
    spec = k.at("h_spec", at + 14336, [P, 14, D_HY])
    gate = k.at("h_gate", at + 21504, [P, CT, T])
    zt = k.at("h_zt", at + 26624, [P, M_LAT, D_HY])
    cv = k.at("h_cv", at + 26624, [P, CT, LAT])
    z = k.at("h_z", R0, [P, CT, T])
    ti = k.at("h_ti", R0 + 5120, [P, TAB])
    assert R0 + 5120 + TAB <= ATT0 and at + 30720 == R0
    tf = k.at("h_tf", S0, [P, TAB])
    t = [k.at(f"h_t{n}", S0 + TAB + n * D_HY, [P, D_HY]) for n in range(2)]
    g_tmp = k.at("h_bt", at + 7168, [P, 10, D_HY])
    i_tmp = k.at("h_it", at + 7168, [P, 7168])
    landed, spec_in, gate_in = k.sem("y_landed"), k.sem("y_spec_in"), k.sem("y_gate_in")
    zt_full, zt_read, xh_ready, sp_full, sp_read = (k.sem("y_" + n) for n in ("ztf", "ztr", "xh", "spf", "spr"))
    yr_full, yr_read, z_ready, steps_sem = (k.sem("y_" + n) for n in ("yrf", "yrr", "z", "steps"))
    blocks = {"lat": M_LAT, "ctx": M_CTX}
    resid = {"lat": ORDER_LAT, "ctx": ORDER_CTX}
    spread = {"lat": SPREAD_LAT, "ctx": SPREAD_CTX}
    yo = {"lat": YO_LAT, "ctx": YO_CTX}
    zb = [sum(blocks[p] for p, _ in JOBS[:j]) for j in range(5)]
    pb = [sum(len(resid[p]) for p, _ in JOBS[:j]) for j in range(5)]
    tok0 = {"lat": 0, "ctx": LAT}
    width = {"lat": 1536, "ctx": 384}
    with nc.Block() as block:
        @block.sync
        def _(e):
            e.dma_start(z[:, :, :], d["u"][0:CT].rearrange("m p t -> p m t")).then_inc(landed, 16)
            e.dma_start(tf[:, :], d["tab_f"]).then_inc(landed, 16)
            e.dma_start(ti[:, :], d["tab_i"]).then_inc(landed, 16)
            for j, (part, order) in enumerate(JOBS):
                if j:
                    e.wait_ge(sp_read, pb[j])
                e.dma_start(spec[:, 0:2 * len(resid[part]), :], d["spec_" + part][order]).then_inc(spec_in, 16)
                if j:
                    e.wait_ge(z_ready, j)
                e.dma_start(gate[:, :, :], d["u"][CT * (1 + order):CT * (2 + order)].rearrange("m p t -> p m t")
                            ).then_inc(gate_in, 16)
            e.wait_ge(gate_in, 64)

        @block.tensor
        def _(e):
            e.wait_ge(landed, 48)
            for j, (part, order) in enumerate(JOBS):
                if j:
                    e.wait_ge(z_ready, j)
                for m in range(blocks[part]):
                    for ct in range(CT):
                        c = tok0[part] + m * P
                        tr = e.transpose(k.bank[:, m, ct * P:(ct + 1) * P], z[:, ct, c:c + P], k.ident[:, :])
                    tr.then_inc(zt_full, 1)
                e.wait_ge(xh_ready, j + 1)
                for pos, r in enumerate(resid[part]):
                    b = 2 * (pos % 4)
                    if pos >= 4:
                        e.wait_ge(sp_read, pb[j] + pos - 3)
                    forward(e, k, tf, xh, r, spread[part][r], k.bank[:, b, :], k.bank[:, b + 1, :]).then_inc(sp_full, 1)
                e.wait_ge(sp_read, pb[j + 1])
                for ct in range(CT):
                    if ct >= 2:
                        e.wait_ge(yr_read, j * CT + ct - 1)
                    out = k.acc[ct % 2]
                    for pos, r in enumerate(resid[part]):
                        o = yo[part][r]
                        mm = inverse(e, ti, ys, r, pos, ct, out[:, o:o + (P if r in (0, 6) else 2 * P)])
                    mm.then_inc(yr_full, 1)

        @block.scalar
        def _(e):
            for j, (part, order) in enumerate(JOBS):
                for m in range(blocks[part]):
                    e.wait_ge(zt_full, zb[j] + m + 1)
                    e.activation(zt[:, m, :], k.bank[:, m, :], ACT.Copy).then_inc(zt_read, 1)
                for ct in range(CT):
                    e.wait_ge(yr_full, j * CT + ct + 1)
                    e.activation(yr[:, ct, 0:width[part]], k.acc[ct % 2][:, 0:width[part]], ACT.Copy).then_inc(yr_read, 1)

        @block.vector
        def _(e):
            steps = Steps(e, steps_sem)

            def tt(o, a, b, op):
                steps(e.tensor_tensor(o, a, b, op))

            def fma(o, a, c, b, op=ALU.add):
                steps(e.scalar_tensor_tensor(out=o, in0=a, scalar=c, in1=b, op0=ALU.mult, op1=op))

            def products(j, part):
                for pos in range(len(resid[part])):
                    e.wait_ge(sp_full, pb[j] + pos + 1)
                    b = 2 * (pos % 4)
                    zr, zi = k.bank[:, b, :], k.bank[:, b + 1, :]
                    hr, hi = spec[:, 2 * pos, :], spec[:, 2 * pos + 1, :]
                    tt(t[0][:, :], zr, hr, ALU.mult)
                    tt(t[1][:, :], zi, hi, ALU.mult)
                    tt(ys[:, 2 * pos, :], t[0][:, :], t[1][:, :], ALU.subtract)
                    tt(t[0][:, :], zr, hi, ALU.mult)
                    tt(t[1][:, :], zi, hr, ALU.mult)
                    e.tensor_tensor(ys[:, 2 * pos + 1, :], t[0][:, :], t[1][:, :], ALU.add).then_inc(sp_read, 1)
                    e.wait_ge(sp_read, pb[j] + pos + 1)

            def back_lat():
                y = lambda r, im=0, n=P: yr[:, :, YO_LAT[r] + im * P:YO_LAT[r] + im * P + n]
                buf = lambda n, w=P: i_tmp[:, n * 512:n * 512 + 4 * w].rearrange("p (c t) -> p c t", c=CT)
                ps, qw = buf(0, 2 * P), buf(2, 2 * P)
                u, v = [buf(4 + n) for n in range(3)], [buf(7 + n) for n in range(3)]
                ev, od, od2 = buf(10), buf(11), buf(12)
                out = lambda m: cv[:, :, m * P:(m + 1) * P]
                tt(ps, y(1, n=2 * P), y(5, n=2 * P), ALU.add)
                tt(qw, y(1, n=2 * P), y(5, n=2 * P), ALU.subtract)
                p_, s_, q_, w_ = ps[:, :, 0:P], ps[:, :, P:], qw[:, :, 0:P], qw[:, :, P:]
                tt(u[0], y(0), y(4), ALU.add)
                fma(ev, y(4), -0.5, y(0))
                fma(u[1], y(4, 1), -S3, ev)
                fma(u[2], y(4, 1), S3, ev)
                tt(v[0], y(6), y(2), ALU.add)
                fma(ev, y(2), -0.5, y(6))
                fma(v[1], y(2, 1), S3, ev)
                fma(v[2], y(2, 1), -S3, ev)

                def emit(m, o):
                    tt(ev, u[m % 3], v[m % 3], ALU.subtract if m % 2 else ALU.add)
                    tt(out(m + 2), ev, o, ALU.subtract)
                    if m >= 4:
                        tt(out(m - 4), ev, o, ALU.add)

                tt(od, p_, y(3), ALU.add)
                emit(0, od)
                fma(od2, s_, -0.5, y(3, 1), ALU.subtract)
                fma(od, q_, S3, od2)
                emit(1, od)
                fma(od, q_, -S3, od2)
                emit(5, od)
                fma(od2, p_, 0.5, y(3), ALU.subtract)
                fma(od, w_, -S3, od2)
                emit(2, od)
                tt(od, y(3, 1), s_, ALU.subtract)
                emit(3, od)
                fma(od2, p_, -0.5, y(3))
                fma(od, w_, -S3, od2)
                emit(4, od)

            def back_ctx():
                re, im, r0 = yr[:, :, 0:P], yr[:, :, P:2 * P], yr[:, :, 2 * P:3 * P]
                tmp = i_tmp[:, 0:512].rearrange("p (c t) -> p c t", c=CT)
                fma(tmp, re, -0.5, r0)
                fma(cv[:, :, 0:P], im, -S3, tmp)
                fma(cv[:, :, P:2 * P], im, S3, tmp)

            for j, (part, order) in enumerate(JOBS):
                c, n = tok0[part], blocks[part] * P
                e.wait_ge(zt_read, zb[j + 1])
                if part == "lat":
                    butterfly_lat(e, steps, zt, xh, g_tmp)
                else:
                    butterfly_ctx(e, steps, zt, xh)
                e.sem_inc(xh_ready, 1)
                e.wait_ge(spec_in, 16 * (j + 1))
                products(j, part)
                e.wait_ge(yr_read, CT * (j + 1))
                if part == "lat":
                    back_lat()
                else:
                    back_ctx()
                for ct in range(CT):
                    fma(cv[:, ct, 0:n], z[:, ct, c:c + n], k.hy_bias[:, order * CT + ct:order * CT + ct + 1], cv[:, ct, 0:n])
                e.wait_ge(gate_in, 16 * (j + 1))
                e.tensor_tensor(z[:, :, c:c + n], cv[:, :, 0:n], gate[:, :, c:c + n], ALU.mult).then_inc(z_ready, 1)
                e.wait_ge(z_ready, j + 1)



def gate_rows(k, layer, part):
    gates = k.mods[:, 96 * layer:96 * layer + 96].rearrange("p (m w) -> p m w", w=2)
    return gates[:, 8 * part:8 * part + 8, :]


def add_branch(k, e, s, m, gate, old, tokens):
    for n, (a, b) in enumerate(((0, LAT), (LAT, T))[:1 + (tokens > LAT)]):
        ins = e.scalar_tensor_tensor(out=k.x[:, m, a:b], in0=k.acc[s][:, a:b], scalar=gate(m, n),
                                     in1=old[:, m, a:b], op0=ALU.mult, op1=ALU.add)
    ins.then_inc(k.acc_free[s], 1)


def square_tile(k, e, s, m, use, base, sq, tokens):
    e.wait_ge(k.acc_free[s], use + 2)
    e.wait_ge(k.ss_done, base + m - 1)
    e.activation(sq[:, s, 0:tokens], k.x[:, m, 0:tokens], ACT.Square).then_inc(k.sq_ready, 1)


def sum_squares(k, e, cleared, base, sq, tokens):
    e.memset(k.ss[:, 0:tokens], 0.0).then_inc(cleared, 1)
    e.wait_ge(cleared, 1)
    with e.Fori(0, KT // 2) as i:
        for s in range(2):
            e.wait_ge(k.sq_ready, i * 2 + (base + s + 1))
            e.tensor_tensor(k.ss[:, 0:tokens], k.ss[:, 0:tokens], sq[:, s, 0:tokens],
                            ALU.add).then_inc(k.ss_done, 1)
            e.wait_ge(k.ss_done, i * 2 + (base + s + 1))


def even_out(k):
    nc, d, ph = k.nc, k.d, PH["ev_out"]
    w0, a0 = ph.w0, ph.a0
    base = k.sqs
    x_in, cleared, z_hi, z_ready = k.sem("ev_x_in"), k.sem("ev_cleared"), k.sem("ev_z_hi"), k.sem("ev_z_ready")
    z = k.at("h_z", R0, [P, CT, T])
    attT = k.at("attT", ATT0, [P, 4, T])
    sq = k.at("sq_ev", R0 + CT * T, [P, 2, T])
    source = lambda kk: z[:, kk, :] if kk < CT else attT[:, kk - CT, :]
    rows = gate_rows(k, 0, 2)
    with nc.Block() as block:
        @block.sync
        def _(e):
            e.dma_start(k.x[:, :, :], d["x"]).then_inc(x_in, 16)
            load_weights(k, e, ph)
            e.wait_ge(x_in, 16)

        @block.tensor
        def _(e):
            with e.Fori(0, ph.pairs) as i:
                for s in range(2):
                    item(k, e, s, i + w0, i + a0, k.rhs_h, T, ready=z_ready, base=0)

        @block.scalar
        def _(e):
            split_hi(k, e, 0, w0, k.acc_full[0], a0 + 1)
            for kk in range(KT):
                e.activation(k.h_hi[:, kk, :], source(kk), ACT.Copy).then_inc(z_hi, 1)
            with e.Fori(0, ph.pairs) as i:
                for s in range(2):
                    split_hi(k, e, 1 - s, i + (w0 + s), k.acc_full[1 - s], i + (a0 + 1 + s))
                    square_tile(k, e, s, i * 2 + s, i + a0, base, sq, T)

        @block.vector
        def _(e):
            split_lo(k, e, 0, w0)
            for kk in range(KT):
                e.wait_ge(z_hi, kk + 1)
                e.tensor_tensor(k.h_lo[:, kk, :], source(kk), k.h_hi[:, kk, :].bitcast(F32), ALU.subtract
                                ).then_inc(z_ready, 1)
            e.wait_ge(x_in, 16)
            with e.Fori(0, ph.pairs) as i:
                for s in range(2):
                    split_lo(k, e, 1 - s, i + (w0 + s))
                    e.wait_ge(k.acc_full[s], full(i + a0))
                    add_branch(k, e, s, i * 2 + s, lambda m, n: rows[:, m, n:n + 1], k.x, T)

        @block.gpsimd
        def _(e):
            sum_squares(k, e, cleared, base, sq, T)
    k.sqs += KT


def ffn(k, layer):
    nc, d, ph = k.nc, k.d, PH[f"ffn{layer}"]
    w0, a0, last = ph.w0, ph.a0, ph.last
    base = k.sqs
    tokens = T if layer == 0 else LAT
    norm = Norm(k, 2 * layer + 1)
    hid_hi = [k.at(f"hid_hi{n}", R0 + 2 * n * HG * T, [P, HG, T], F32R) for n in range(2)]
    hid_lo = [k.at(f"hid_lo{n}", R0 + (2 * n + 1) * HG * T, [P, HG, T], F32R) for n in range(2)]
    sg = k.at("silu_gate", R0 + 4 * HG * T, [P, T])
    hid = k.at("hid", R0 + 4 * HG * T + T, [P, T])
    sq = k.at("sq_ffn", R0 + 2 * HG * T, [P, 2, T])
    assert GROUPS % 2 == 1 and 4 * HG * T + 2 * T <= END - R0
    hid_ready, hi_done, lo_done = (k.sem(f"{n}{layer}") for n in ("ffn_hid", "ffn_hid_hi", "ffn_hid_lo"))
    cleared, stored, steps_sem = k.sem(f"ffn_cleared{layer}"), k.sem(f"ffn_stored{layer}"), k.sem(f"ffn_steps{layer}")
    rows = gate_rows(k, layer, 5)
    half = KT // 2
    in_at = lambda g: (g * 3 + (w0 - 1), g * 6 + (a0 - 4))
    out_at = lambda g: (g * 3 + (w0 + 4), g * 6 + (a0 + 4))
    end = GROUPS - 1
    end_at = (w0 + 3 * end + 2, a0 + 6 * end + 2)

    def schedule(e, take_in, take_out):
        take_in(0, 0, (w0, a0))
        with e.Fori(0, end // 2) as b:
            for n in range(2):
                g = b * 2 + n
                take_in(g + 1, (n + 1) % 2, in_at(g + 1))
                take_out(g, n, out_at(g), False)
        take_out(end, 0, end_at, True)

    with nc.Block() as block:
        @block.sync
        def _(e):
            load_weights(k, e, ph)

        @block.tensor
        def _(e):
            norm.tensor(k, e)

            def take_in(g, buf, at):
                for t in range(HG):
                    for s in range(2):
                        item(k, e, s, at[0] + t, at[1] + t, k.rhs_h, tokens, ready=k.h_ready, base=norm.h_base)

            def take_out(g, buf, at, ends):
                e.wait_ge(lo_done, g * HG + (HG + 1))
                rhs = lambda kk: (hid_hi[buf][:, kk, :], hid_lo[buf][:, kk, :])
                for m in range(KT):
                    s = m % 2
                    if m % half == 0:
                        e.wait_ge(k.split_lo[m // half], at[0] + 1)
                    e.wait_ge(k.acc_free[s], at[1] + (m // 2 + 1))
                    product(k, e, m // half, k.acc[s], HG, rhs, tokens, at=m % half * P, stride=half * P
                            ).then_inc(k.acc_full[s], 1)

            schedule(e, take_in, take_out)

        @block.scalar
        def _(e):
            norm.scalar(k, e)

            def take_in(g, buf, at):
                for t in range(HG):
                    split_hi(k, e, 1, at[0] + t, k.acc_full[1], at[1] + (t + 1))
                    e.wait_ge(k.acc_full[0], full(at[1] + t))
                    e.wait_ge(k.acc_free[1], at[1] + (t + 1))
                    e.activation(sg[:, 0:tokens], k.acc[0][:, 0:tokens], ACT.Silu).then_inc(k.acc_free[0], 1)
                    split_hi(k, e, 0, at[0] + (t + 1), k.acc_full[0], full(at[1] + t))
                    e.wait_ge(hid_ready, g * HG + (t + 1))
                    e.activation(hid_hi[buf][:, t, 0:tokens], hid[:, 0:tokens], ACT.Copy).then_inc(hi_done, 1)

            def take_out(g, buf, at, ends):
                split_hi(k, e, 1, at[0], k.acc_full[1], at[1] + 1)
                for m in range(KT):
                    s, use = m % 2, at[1] + m // 2
                    if m == half and not (ends and last):
                        split_hi(k, e, 0, at[0] + 1, k.acc_full[1], full(at[1] + (half // 2 - 1)))
                    if ends and not last:
                        square_tile(k, e, s, m, use, base, sq, tokens)
                    if ends and last:
                        e.wait_ge(k.acc_free[s], use + 2)
                        e.dma_start(d["out"][:, m, :], k.x[:, m, 0:LAT]).then_inc(stored, 16)
                if ends and last:
                    e.wait_ge(stored, 16 * KT)

            schedule(e, take_in, take_out)

        @block.vector
        def _(e):
            norm.vector(k, e, Steps(e, steps_sem))
            e.sem_inc(lo_done, 1)

            def take_in(g, buf, at):
                for t in range(HG):
                    split_lo(k, e, 1, at[0] + t)
                    split_lo(k, e, 0, at[0] + (t + 1))
                    e.wait_ge(k.acc_free[0], at[1] + (t + 2))
                    e.wait_ge(k.acc_full[1], full(at[1] + t))
                    e.wait_ge(lo_done, g * HG + (t + 1))
                    e.tensor_tensor(hid[:, 0:tokens], sg[:, 0:tokens], k.acc[1][:, 0:tokens],
                                    ALU.mult).then_inc(hid_ready, 1)
                    e.wait_ge(hid_ready, g * HG + (t + 1))
                    e.sem_inc(k.acc_free[1], 1)
                    e.wait_ge(hi_done, g * HG + (t + 1))
                    e.tensor_tensor(hid_lo[buf][:, t, 0:tokens], hid[:, 0:tokens],
                                    hid_hi[buf][:, t, 0:tokens].bitcast(F32), ALU.subtract).then_inc(lo_done, 1)

            def take_out(g, buf, at, ends):
                for s in range(2):
                    e.wait_ge(k.acc_free[s], at[1] + 1)
                split_lo(k, e, 1, at[0])
                for m in range(KT):
                    if m == half and not (ends and last):
                        split_lo(k, e, 0, at[0] + 1)
                    e.wait_ge(k.acc_full[m % 2], full(at[1] + m // 2))
                    add_branch(k, e, m % 2, m, lambda m, n: rows[:, m, n:n + 1], k.x, tokens)

            schedule(e, take_in, take_out)

        if not last:
            @block.gpsimd
            def _(e):
                e.wait_ge(k.stat_full, norm.n + 1)
                sum_squares(k, e, cleared, base, sq, tokens)
    if not last:
        k.sqs += KT



def rg_lru(k):
    nc, d, ph = k.nc, k.d, PH["rg_in"]
    w0, a0 = ph.w0, ph.a0
    norm = Norm(k, 2)
    y = k.at("y", X0, [P, RT, LAT])
    a = k.at("rg_a", R0, [P, 2, T])
    th = k.at("rg_th", R0 + 2 * T, [P, 2, T])
    rg = k.at("rg_g", R0 + 4 * T, [P, 4, T])
    xc = k.at("rg_xc", R0 + 8 * T, [P, T])
    gw = k.at("rg_gw", R0 + 9 * T, [P, 4, P])
    centre, conv, gw_in, steps_sem = k.sem("r_centre"), k.sem("r_conv"), k.sem("r_gw"), k.sem("r_steps")
    decay, root, v_ready, y_done, gelu_done = (k.sem("r_" + n) for n in ("decay", "root", "v", "y", "gelu"))
    acts, sig, gated, kept = k.sem("r_acts"), k.sem("r_sigmoids"), k.sem("r_gated"), k.sem("r_x_kept")
    taps = k.rg_w[:, :].rearrange("p (m t) -> p m t", t=4)
    bias = k.rg_ba[:, :].rearrange("p (n g) -> p n g", g=4)
    exp_scale = k.rg_sp[:, 0:20].rearrange("p (n g) -> p n g", g=2)
    tanh_scale = k.rg_sp[:, 60:80].rearrange("p (n g) -> p n g", g=2)
    with nc.Block() as block:
        @block.sync
        def _(e):
            e.dma_start(d["x_kept"], k.x[:, :, 0:LAT]).then_inc(kept, 16)
            e.dma_start(gw[:, :, :], d["rg_gw"][0]).then_inc(gw_in, 16)
            with e.Fori(0, RT - 1) as i:
                load_next(k, e, i + w0)
                e.wait_ge(k.acc_full[1], full(i * 3 + (a0 + 2)))
                e.dma_start(gw[:, :, :], d["rg_gw"][i + 1]).then_inc(gw_in, 16)
            load_next(k, e, w0 + RT - 1)
            e.wait_ge(kept, 16)

        @block.tensor
        def _(e):
            norm.tensor(k, e)
            with e.Fori(0, RT) as i:
                item(k, e, 0, i + w0, i * 3 + a0, k.rhs_h, T, ready=k.h_ready, base=norm.h_base)
                item(k, e, 1, i + w0, i * 3 + a0, k.rhs_h, LAT)
                e.wait_ge(gw_in, i * 16 + 16)
                e.wait_ge(conv, i + 1)
                for g in range(4):
                    s = g % 2
                    e.wait_ge(k.acc_free[s], i * 3 + (a0 + 2 + g // 2))
                    for c, n in CHUNKS[T]:
                        mm = e.matmul(k.acc[s][:, c:c + n], gw[:, g, :], xc[:, c:c + n], start=True, stop=True)
                    mm.then_inc(k.acc_full[s], 1)

        @block.scalar
        def _(e):
            norm.scalar(k, e)
            e.wait_ge(kept, 16)
            e.sem_inc(y_done, 1)

            def branches(i):
                e.wait_ge(k.acc_full[0], full(i * 3 + a0))
                e.activation(xc[:, :], k.acc[0][:, 0:T], ACT.Identity, scale=taps[:, i, 2:3],
                             bias=k.rg_b[:, bass.ds(i, 1)]).then_inc(centre, 1)
                split_hi(k, e, 0, i + (w0 + 1), k.acc_full[0], full(i * 3 + a0))
                e.wait_ge(k.acc_full[1], full(i * 3 + a0))
                e.activation(y[:, i, :], k.acc[1][:, 0:LAT], ACT.Gelu_apprx_tanh).then_inc(k.acc_free[1], 1)

            def gates(i, more):
                e.wait_ge(y_done, i + 1)
                for g in range(4):
                    s = g % 2
                    e.wait_ge(k.acc_full[s], full(i * 3 + (a0 + 1 + g // 2)))
                    e.activation(rg[:, g, :], k.acc[s][:, 0:T], ACT.Sigmoid, bias=bias[:, i, g:g + 1]
                                 ).then_inc(k.acc_free[s], 1)
                for s in range(2):
                    e.wait_ge(k.acc_free[s], i * 3 + (a0 + 4))
                e.sem_inc(sig, 1)
                for dr in range(2):
                    e.activation(a[:, dr, :], rg[:, 2 * dr, :], ACT.Exp, scale=exp_scale[:, i, dr:dr + 1]).then_inc(acts, 1)
                    e.activation(th[:, dr, :], rg[:, 2 * dr, :], ACT.Tanh, scale=tanh_scale[:, i, dr:dr + 1]).then_inc(acts, 1)
                e.wait_ge(acts, i * 4 + 4)
                for dr in range(2):
                    e.activation(rg[:, 2 * dr, :], a[:, dr, :], ACT.Square).then_inc(decay, 1)
                if more:
                    split_hi(k, e, 1, i + (w0 + 1), k.acc_full[1], i * 3 + (a0 + 4))
                for dr in range(2):
                    e.wait_ge(v_ready, i * 2 + (dr + 1))
                    e.activation(th[:, dr, :], th[:, dr, :], ACT.Sqrt).then_inc(root, 1)
                if more:
                    e.wait_ge(gated, i + 1)
                    branches(i + 1)

            split_hi(k, e, 1, w0, k.acc_full[1], a0 + 1)
            branches(0)
            with e.Fori(0, RT - 1) as i:
                gates(i, True)
            gates(RT - 1, False)

        @block.vector
        def _(e):
            steps = Steps(e, steps_sem)
            norm.vector(k, e, steps)

            def convolution(i):
                e.wait_ge(centre, i + 1)
                n = 0
                for tap, sh in ((0, -2), (1, -1), (3, 1)):
                    for lo0, hi0 in ((0, LAT), (LAT, T)):
                        lo, hi = lo0 + max(0, -sh), hi0 - max(0, sh)
                        ins = e.scalar_tensor_tensor(out=xc[:, lo:hi], in0=k.acc[0][:, lo + sh:hi + sh],
                                                     scalar=taps[:, i, tap:tap + 1], in1=xc[:, lo:hi],
                                                     op0=ALU.mult, op1=ALU.add)
                        n += 1
                        if n < 6:
                            steps(ins)
                        else:
                            ins.then_inc(k.acc_free[0], 1)
                e.wait_ge(k.acc_free[0], i * 3 + (a0 + 2))
                e.sem_inc(conv, 1)

            def block_of(i, more):
                e.wait_ge(sig, i + 1)
                for dr in range(2):
                    steps(e.tensor_tensor(rg[:, 2 * dr + 1, :], rg[:, 2 * dr + 1, :], xc[:, :], ALU.mult))
                e.sem_inc(gated, 1)
                for dr in range(2):
                    e.wait_ge(decay, i * 2 + (dr + 1))
                    e.scalar_tensor_tensor(out=th[:, dr, :], in0=rg[:, 2 * dr, :], scalar=1.0, in1=th[:, dr, :],
                                           op0=ALU.add, op1=ALU.mult).then_inc(v_ready, 1)
                if more:
                    split_lo(k, e, 1, i + (w0 + 1))
                for dr in range(2):
                    e.wait_ge(root, i * 2 + (dr + 1))
                    steps(e.tensor_tensor(th[:, dr, :], th[:, dr, :], rg[:, 2 * dr + 1, :], ALU.mult))
                if more:
                    convolution(i + 1)
                    split_lo(k, e, 0, i + (w0 + 2))
                steps(e.tensor_tensor_scan(rg[:, 0, LAT:T], a[:, 0, LAT:T], th[:, 0, LAT:T], 0.0, ALU.mult, ALU.add))
                steps(e.tensor_tensor_scan(rg[:, 0, 0:LAT], a[:, 0, 0:LAT], th[:, 0, 0:LAT], rg[:, 0, T - 1:T],
                                           ALU.mult, ALU.add))
                steps(e.tensor_tensor_scan(rg[:, 2, ::-1], a[:, 1, ::-1], th[:, 1, ::-1], 0.0, ALU.mult, ALU.add))
                steps(e.tensor_tensor(rg[:, 0, 0:LAT], rg[:, 0, 0:LAT], rg[:, 2, 0:LAT], ALU.add))
                steps(e.tensor_tensor(y[:, i, :], y[:, i, :], rg[:, 0, 0:LAT], ALU.mult))
                e.sem_inc(y_done, 1)

            split_lo(k, e, 1, w0)
            convolution(0)
            split_lo(k, e, 0, w0 + 1)
            with steps.loop(RT - 1, 14) as i:
                block_of(i, True)
            block_of(RT - 1, False)


def rg_out(k):
    nc, d, ph = k.nc, k.d, PH["rg_out"]
    w0, a0 = ph.w0, ph.a0
    base = k.sqs
    x_in, cleared, y_hi_done, y_ready = k.sem("ro_x_in"), k.sem("ro_cleared"), k.sem("ro_y_hi"), k.sem("ro_y_ready")
    y = k.at("y", X0, [P, RT, LAT])
    y_hi = k.at("y_hi", H0, [P, RT, LAT], F32R)
    y_lo = k.at("y_lo", H0 + RT * LAT, [P, RT, LAT], F32R)
    x_old = k.at("x_old", R0, [P, KT, LAT])
    sq = k.at("sq_rg", R0 + KT * LAT, [P, 2, LAT])
    rows = gate_rows(k, 1, 2)
    half = RT // 2
    with nc.Block() as block:
        @block.sync
        def _(e):
            e.dma_start(x_old[:, :, :], d["x_kept"]).then_inc(x_in, 16)
            load_weights(k, e, ph)
            e.wait_ge(x_in, 16)

        @block.tensor
        def _(e):
            with e.Fori(0, KT // 2) as i:
                for s in range(2):
                    for h in range(2):
                        e.wait_ge(k.split_lo[h], i * 2 + (w0 + s + 1))
                        if h == 0:
                            e.wait_ge(k.acc_free[s], i + (a0 + 1))
                        rhs = lambda kk: (y_hi[:, h * half + kk, :], y_lo[:, h * half + kk, :])
                        product(k, e, h, k.acc[s], half, rhs, LAT, first=(h == 0), last=(h == 1), ready=y_ready,
                                base=h * half).then_inc(k.acc_full[s] if h else k.half_done, 1)

        @block.scalar
        def _(e):
            for kk in range(RT):
                e.activation(y_hi[:, kk, :], y[:, kk, :], ACT.Copy).then_inc(y_hi_done, 1)
            with e.Fori(0, KT // 2) as i:
                for s in range(2):
                    split_hi(k, e, 1, i * 2 + (w0 + s), k.acc_full[1 - s], i + (a0 + 1 + s))
                    split_hi(k, e, 0, i * 2 + (w0 + s + 1), k.half_done, i * 2 + (s + 1))
                    square_tile(k, e, s, i * 2 + s, i + a0, base, sq, LAT)

        @block.vector
        def _(e):
            for kk in range(RT):
                e.wait_ge(y_hi_done, kk + 1)
                e.tensor_tensor(y_lo[:, kk, :], y[:, kk, :], y_hi[:, kk, :].bitcast(F32), ALU.subtract
                                ).then_inc(y_ready, 1)
            e.wait_ge(x_in, 16)
            e.wait_ge(y_ready, RT)
            with e.Fori(0, KT // 2) as i:
                for s in range(2):
                    split_lo(k, e, 1, i * 2 + (w0 + s))
                    split_lo(k, e, 0, i * 2 + (w0 + s + 1))
                    e.wait_ge(k.acc_full[s], full(i + a0))
                    add_branch(k, e, s, i * 2 + s, lambda m, n: rows[:, m, n:n + 1], x_old, LAT)

        @block.gpsimd
        def _(e):
            sum_squares(k, e, cleared, base, sq, LAT)
    k.sqs += KT



def program(nc, dram):
    with ExitStack() as ctx:
        k = Kernel(nc, ctx, dram)
        k.coef_a = lambda n, who, kk: k.coef[:, (n * 2 + who) * 16 + kk:(n * 2 + who) * 16 + kk + 1]
        k.coef_b = lambda n, who, kk: k.coef[:, (n * 2 + who) * 16 + 8 + kk:(n * 2 + who) * 16 + 9 + kk]
        k.rhs_h = lambda kk: (k.h_hi[:, kk, :], k.h_lo[:, kk, :])
        load_constants(k)
        filters(k)
        adaln(k)
        even_in(k)
        latents(k)
        attention(k)
        hyena(k)
        even_out(k)
        ffn(k, 0)
        rg_lru(k)
        rg_out(k)
        ffn(k, 1)



def _tables():
    t0, q = np.arange(P)[:, None], np.arange(P)[None, :]
    fwd, inv = [], []
    for r in ORDER_LAT:
        ang = 2.0 * np.pi * (t0 * q / P + r * t0 / N_LAT)
        c, s = np.cos(ang), np.sin(ang)
        two = 1.0 if r in (0, 6) else 2.0
        if r in (0, 6):
            fwd += [c, -s]
            inv += [-s.T, c.T]
        else:
            fwd += [c, s, -s]
            inv += [-two * s.T, two * c.T, two * s.T]
    return tuple(np.concatenate(x, axis=1).astype(np.float32) for x in (fwd, inv))


def _filter_constants():
    zs, wins = [], []
    for length, n in ((LAT, N_LAT), (CTX, N_CTX)):
        kk = np.arange(length, dtype=np.float32)
        t = (kk / np.float32(max(length - 1, 1)))[:, None]
        bands = (EMB - 1) // 2
        ang = np.float32(2.0 * math.pi / length) * kk[:, None] * np.linspace(1e-4, bands - 1, bands, dtype=np.float32)[None, :]
        zs.append(np.concatenate([t, np.cos(ang), -np.sin(ang)], axis=-1).T)
        half = length // 2
        dist = np.abs(kk - half) / np.float32(max(half, 1))
        deltas = np.abs(np.linspace(math.log(1e-2) / 1.5, math.log(1e-2) / 0.3, D_HY, dtype=np.float32))
        wins.append((np.exp(-dist[:, None] * deltas[None, :]) / n).reshape(length // P, P, D_HY).transpose(1, 0, 2))
    return (np.ascontiguousarray(np.concatenate(zs, axis=1), dtype=np.float32),
            np.ascontiguousarray(np.concatenate(wins, axis=1), dtype=np.float32))


def _rope_tables():
    row = np.repeat(np.arange(LAT // GRID_W, dtype=np.float32), GRID_W)
    col = np.tile(np.arange(GRID_W, dtype=np.float32), LAT // GRID_W)
    inv = (np.float32(10000.0) ** (-np.arange(0, 16, 2, dtype=np.float32) / np.float32(16))).astype(np.float32)
    cos, sin = np.ones((T, ROPE), np.float32), np.zeros((T, ROPE), np.float32)
    for g, pos in enumerate((row, col)):
        ang = pos[:, None] * inv[None, :]
        c, s = np.cos(ang), np.sin(ang)
        cos[:LAT, 16 * g:16 * g + 16] = np.concatenate([c, c], axis=1)
        sin[:LAT, 16 * g:16 * g + 16] = np.concatenate([-s, s], axis=1)
    lay = lambda a: np.ascontiguousarray(a.reshape(NT, P, ROPE).transpose(1, 0, 2))
    return lay(cos), lay(sin)


def _tiles(w, m=P):
    kk, mm = w.shape
    return np.ascontiguousarray(w.reshape(kk // P, P, mm // m, m).transpose(2, 1, 0, 3))


def _ffn(a, l):
    fi = a["ffn_w_in"][l].reshape(KT, P, 2, GROUPS, HG, P).transpose(3, 4, 2, 1, 0, 5).reshape(GROUPS, HG, 2, P, WS)
    fo = a["ffn_w_out"][l].reshape(GROUPS, HG, P, 2, D // 2).transpose(0, 3, 2, 1, 4).reshape(GROUPS, 1, 2, P, WS)
    parts = [fi[0]]
    for g in range(GROUPS):
        parts += ([fi[g + 1]] if g + 1 < GROUPS else []) + [fo[g]]
    return np.concatenate(parts)


def _columns(v):
    v = np.asarray(v)
    return np.ascontiguousarray(v.reshape(-1, P).T)


def layout(inp):
    a = {n: np.asarray(v) for n, v in inp.items()}
    o = {}
    x = np.concatenate([a["x"][0], a["ctx"][0]], axis=0)
    o["x"] = np.ascontiguousarray(x.T.reshape(KT, P, T).transpose(1, 0, 2))
    o["cc"] = np.ascontiguousarray(np.stack([a["c"][0], a["c_ctx"]], -1).reshape(KT, P, 2).transpose(1, 0, 2).reshape(P, 16))
    aw = a["ada_w"].reshape(2, KT, P, ADA_LOADS, ADA_M, P)
    o["ada_w"] = np.ascontiguousarray(aw.transpose(0, 3, 2, 1, 4, 5))
    o["ada_b"] = _columns(a["ada_b"])
    o["gains"] = _columns(np.stack([a["norm1_g"][0], a["norm2_g"][0], a["norm1_g"][1], a["norm2_g"][1]]))
    ev = np.zeros((D, 18 * P), np.float32)
    ev[:, :a["ev_w_in"].shape[2]] = a["ev_w_in"][0]
    ri = a["rg_w_in"][0].reshape(KT, P, 2, RT, P)
    ri = ri[:, :, ::-1].transpose(3, 2, 1, 0, 4).reshape(RT, 2, P, WS)
    ro = a["rg_w_out"][0].reshape(2, RT // 2, P, KT, P)
    ro = ro.transpose(3, 0, 2, 1, 4).reshape(KT, 2, P, RT // 2 * P)
    ro = np.concatenate([ro, np.zeros((KT, 2, P, WS - RT // 2 * P), np.float32)], axis=-1)
    o["weights"] = np.ascontiguousarray(np.concatenate([
        _tiles(ev).reshape(9, 2, P, WS), _tiles(a["ev_w_out"][0]).reshape(4, 2, P, WS), _ffn(a, 0), ri, ro, _ffn(a, 1)]))
    assert len(o["weights"]) == ALL_PAIRS
    o["hy_w"] = np.ascontiguousarray(a["hy_short_w"][0].T.reshape(12, P, 3).transpose(1, 0, 2).reshape(P, 36))
    o["hy_b"] = _columns(a["hy_short_b"][0])
    o["hy_bias"] = _columns(a["hy_bias"][0])
    o["mlp"] = np.ascontiguousarray(np.stack([a["hy_b1"][0], a["hy_b2"][0], a["hy_freq"][0]], -1))
    o["hy_w1"], o["hy_w2"], o["hy_w3"] = a["hy_w1"][0], a["hy_w2"][0], a["hy_w3"][0]
    o["g_lat"] = _columns(np.concatenate([a["mla_q_norm_g"][0], a["mla_kv_norm_g"][0]]))
    o["w_uq"] = np.ascontiguousarray(a["mla_w_uq"][0].reshape(3, P, -1).transpose(1, 0, 2))
    o["w_ukv"] = np.ascontiguousarray(a["mla_w_ukv"][0].reshape(2, P, -1).transpose(1, 0, 2))
    o["gq"] = np.ascontiguousarray(np.broadcast_to(a["mla_qk_g_q"][0], (P, QD)))
    o["gk"] = np.ascontiguousarray(np.broadcast_to(a["mla_qk_g_k"][0], (P, QD)))
    o["rg_w"] = np.ascontiguousarray(a["rg_conv_w"][0].T.reshape(RT, P, 4).transpose(1, 0, 2).reshape(P, 40))
    o["rg_b"] = _columns(a["rg_conv_b"][0])
    gw = np.stack([a["rg_w_a"][0], a["rg_w_x"][0]], axis=1)
    o["rg_gw"] = np.ascontiguousarray(gw.transpose(2, 3, 0, 1, 4)).reshape(RT, P, 4, P)
    gb = np.stack([a["rg_b_a"][0], a["rg_b_x"][0]], axis=1).reshape(2, 2, RT, P)
    o["rg_ba"] = np.ascontiguousarray(gb.transpose(3, 2, 0, 1)).reshape(P, 40)
    o["rg_lam"] = np.ascontiguousarray(a["rg_lambda"][0].reshape(2, RT, P).transpose(2, 1, 0)).reshape(P, 20)
    o["tab_f"], o["tab_i"] = _tables()
    o["filter_z"], o["window"] = _filter_constants()
    o["cos"], o["sin"] = _rope_tables()
    o["ident"] = np.eye(P, dtype=np.float32)
    o["ones"] = np.ones((P, P), np.float32)
    return o


def build(nc, arrays):
    dram = {n: nc.dram_tensor("in_" + n, v.shape, mybir.dt.from_np(v.dtype), kind="ExternalInput").ap()
            for n, v in arrays.items()}
    dram["u"] = nc.dram_tensor("u_scratch", (12, P, T), F32, kind="Internal").ap()
    dram["x_kept"] = nc.dram_tensor("x_kept", (P, KT, LAT), F32, kind="Internal").ap()
    dram["spec_lat"] = nc.dram_tensor("spec_lat", (2, P, 14, D_HY), F32, kind="Internal").ap()
    dram["spec_ctx"] = nc.dram_tensor("spec_ctx", (2, P, 4, D_HY), F32, kind="Internal").ap()
    dram["out"] = nc.dram_tensor("out_0", (P, KT, LAT), F32, kind="ExternalOutput").ap()
    program(nc, dram)


def kernel(**inputs):
    import concourse.bacc as bacc
    from concourse.bass_utils import run_bass_kernel_spmd

    nc = bacc.Bacc("TRN2", target_bir_lowering=False, num_devices=1)
    arrays = layout(inputs)
    build(nc, arrays)
    r = run_bass_kernel_spmd(nc, [{"in_" + n: v for n, v in arrays.items()}], core_ids=[0])
    out = r.results[0]["out_0"]
    return np.ascontiguousarray(out.transpose(1, 0, 2).reshape(D, LAT).T)[None]
```

```python
import math
from contextlib import ExitStack, contextmanager

import numpy as np

import concourse.bass as bass
from concourse import mybir

F32 = mybir.dt.float32
F32R = mybir.dt.float32r
ACT = mybir.ActivationFunctionType
ALU = mybir.AluOpType
AX_X = mybir.AxisListType.X

P = 128
D = 1024
KT = D // P
LAT, CTX = 1024, 256
T = LAT + CTX
NT = T // P
EPS = 1e-6
D_FF = 2816
HT = D_FF // P
HG = 2
GROUPS = HT // HG
D_HY = 512
CT = D_HY // P
Q_RANK, KV_RANK, ROPE = 384, 256, 32
NOPE, VD, HEADS = 64, 64, 8
QD = NOPE + ROPE
LT = (Q_RANK + KV_RANK) // P
MLA_SCALE = QD ** -0.5
D_RNN = 1280
RT = D_RNN // P
HID_F = 64
EMB = 33
GRID_W = 64
BANK = 512
CHUNKS = {T: [(0, 512), (512, 512), (1024, 256)], LAT: [(0, 512), (512, 512)]}

N_LAT, R_LAT, M_LAT = 1536, 12, 8
N_CTX, R_CTX, M_CTX = 384, 3, 2
ORDER_LAT = [0, 6, 1, 2, 3, 4, 5]
ORDER_CTX = [0, 4]
S3 = math.sqrt(3.0) / 2.0
TF = {}
TI = {}
_n = 0
for _r in ORDER_LAT:
    TF[_r] = TI[_r] = _n
    _n += 2 if _r in (0, 6) else 3
TAB = _n * P
YO_LAT = {1: 0, 2: 256, 3: 512, 4: 768, 5: 1024, 0: 1280, 6: 1408}
YO_CTX = {4: 0, 0: 256}
JOBS = [("lat", 0), ("lat", 1), ("ctx", 0), ("ctx", 1)]

BASE = 16512
C0 = 0
SS0 = 2000
WS = KT * P
W0 = SS0 + T
S0 = W0 + 2 * WS
X0 = S0 + 4 * WS
H0 = X0 + KT * T
R0 = H0 + 2 * KT * T
END = (229368 - BASE) // 32 * 8
ATT0 = END - 4 * T

CONSTS = {}
_at = C0
for _name, _len in (("ident", P), ("ones", P), ("mods", 2 * 96), ("coef", 4 * 32), ("gains", 4 * KT), ("ada_b", 2 * 48),
                    ("hy_w", 12 * 3), ("hy_b", 12), ("hy_bias", 8), ("mlp", 3), ("cc", 16), ("silu_c", 16),
                    ("g_lat", 5), ("rg_w", 40), ("rg_b", 10), ("rg_ba", 40), ("rg_lam", 20), ("rg_sp", 80),
                    ("stat", 16), ("rstd", 16)):
    CONSTS[_name] = (_at, _len)
    _at += -(-_len // 8) * 8
assert _at <= SS0


class Phase:

    def __init__(self, name, pairs, uses):
        self.name, self.pairs, self.uses = name, pairs, uses


FFN_PAIRS = GROUPS * 3
PHASES = [Phase("ev_in", 9, 9), Phase("ev_out", 4, 4), Phase("ffn0", FFN_PAIRS, GROUPS * 6),
          Phase("rg_in", RT, 3 * RT), Phase("rg_out", KT, KT // 2), Phase("ffn1", FFN_PAIRS, GROUPS * 6)]
PH = {}
_w = _a = 0
for _p in PHASES:
    _p.w0, _p.a0, _p.last = _w, _a, _p is PHASES[-1]
    _w += _p.pairs
    _a += _p.uses
    PH[_p.name] = _p
ALL_PAIRS = _w


class Steps:

    def __init__(self, eng, sem):
        self.eng, self.sem, self.n, self.extra = eng, sem, 0, 0

    def __call__(self, ins, lag=0):
        self.n += 1
        ins.then_inc(self.sem, 1)
        if self.n > lag:
            self.eng.wait_ge(self.sem, self.extra + (self.n - lag))

    def settle(self):
        self.eng.wait_ge(self.sem, self.extra + self.n)

    @contextmanager
    def loop(self, count, per):
        before = self.n
        with self.eng.Fori(0, count) as i:
            self.extra = i * per
            yield i
        assert self.n == before + per, (self.n - before, per)
        self.extra, self.n = 0, before + count * per


class Kernel:

    def __init__(self, nc, ctx, dram):
        self.nc, self.ctx, self.d, self.placed = nc, ctx, dram, {}
        self.bank = ctx.enter_context(nc.psum_tensor("bank", [P, 8, BANK], F32))
        self.acc = [self.bank[:, 3 * s:3 * s + 3, :].rearrange("p b n -> p (b n)") for s in range(2)]
        self.w = [self.at(f"w_raw{s}", W0 + s * WS, [P, WS]) for s in range(2)]
        self.w_hi = [self.at(f"w_hi{s}", S0 + 2 * s * WS, [P, WS], F32R) for s in range(2)]
        self.w_lo = [self.at(f"w_lo{s}", S0 + (2 * s + 1) * WS, [P, WS], F32R) for s in range(2)]
        self.x = self.at("x", X0, [P, KT, T])
        self.h_hi = self.at("h_hi", H0, [P, KT, T], F32R)
        self.h_lo = self.at("h_lo", H0 + KT * T, [P, KT, T], F32R)
        self.ss = self.at("ss", SS0, [P, T])
        self.c = c = {name: self.at("c_" + name, at, [P, n]) for name, (at, n) in CONSTS.items()}
        self.ident, self.ones, self.mods, self.coef = c["ident"], c["ones"], c["mods"], c["coef"]
        self.gains, self.ada_b, self.cc, self.silu_c = c["gains"], c["ada_b"], c["cc"], c["silu_c"]
        self.hy_w, self.hy_b, self.hy_bias, self.mlp = c["hy_w"], c["hy_b"], c["hy_bias"], c["mlp"]
        self.g_lat, self.stat, self.rstd = c["g_lat"], c["stat"], c["rstd"]
        self.rg_w, self.rg_b, self.rg_ba = c["rg_w"], c["rg_b"], c["rg_ba"]
        self.rg_lam, self.rg_sp = c["rg_lam"], c["rg_sp"]
        self.w_full = [self.sem(f"weights_landed{s}") for s in range(2)]
        self.split_hi = [self.sem(f"weights_hi{s}") for s in range(2)]
        self.split_lo = [self.sem(f"weights_lo{s}") for s in range(2)]
        self.half_done, self.hi_ready, self.h_mid = self.sem("half_done"), self.sem("hi_ready"), self.sem("h_mid")
        self.acc_full = [self.sem(f"sums_ready{s}") for s in range(2)]
        self.acc_free = [self.sem(f"sums_read{s}") for s in range(2)]
        self.stat_full, self.ms_ready, self.sd_ready = self.sem("stat_full"), self.sem("ms_ready"), self.sem("sd_ready")
        self.diag_ready, self.bc_full, self.rr_ready = self.sem("diag_ready"), self.sem("bc_full"), self.sem("rr_ready")
        self.xr_ready, self.h_ready = self.sem("xr_ready"), self.sem("h_ready")
        self.x_new, self.sq_ready, self.ss_done = self.sem("x_new"), self.sem("sq_ready"), self.sem("ss_done")
        self.sqs = 0

    def at(self, name, word, shape, dt=F32):
        key = (word, tuple(shape), str(dt))
        if key not in self.placed:
            self.placed[key] = self.nc.alloc_sbuf_tensor_at(name, shape, dt, offset=BASE + 4 * word)
        return self.placed[key]

    def sem(self, name):
        return self.ctx.enter_context(self.nc.semaphore(name))



def load_pair(k, e, p):
    for s in range(2):
        e.dma_start(k.w[s][:, :], k.d["weights"][p, s]).then_inc(k.w_full[s], 16)


def load_next(k, e, p):
    for s in range(2):
        e.wait_ge(k.split_lo[s], p + 1)
        e.dma_start(k.w[s][:, :], k.d["weights"][p + 1, s]).then_inc(k.w_full[s], 16)


def load_weights(k, e, ph):
    with e.Fori(0, ph.pairs - 1 if ph.last else ph.pairs) as i:
        load_next(k, e, i + ph.w0)


def full(use):
    return use + 2


def split_hi(k, e, s, pair, sem, count):
    e.wait_ge(k.w_full[s], pair * 16 + 16)
    e.wait_ge(sem, count)
    e.activation(k.w_hi[s][:, :], k.w[s][:, :], ACT.Copy).then_inc(k.split_hi[s], 1)


def split_lo(k, e, s, pair):
    e.wait_ge(k.split_hi[s], pair + 1)
    e.tensor_tensor(k.w_lo[s][:, :], k.w[s][:, :], k.w_hi[s][:, :].bitcast(F32), ALU.subtract
                    ).then_inc(k.split_lo[s], 1)


def product(k, e, s, out, kt, rhs, tokens, at=0, stride=P, first=True, last=True, ready=None, base=0):
    for kk in range(kt):
        if ready:
            e.wait_ge(ready, base + kk + 1)
        hi, lo = rhs(kk)
        c1 = at + kk * stride
        passes = ((k.w_hi[s], hi), (k.w_hi[s], lo), (k.w_lo[s], hi))
        for n, (w, x) in enumerate(passes):
            for c, m in CHUNKS[tokens]:
                mm = e.matmul(out[:, c:c + m], w[:, c1:c1 + P], x[:, c:c + m],
                              start=(first and kk == 0 and n == 0), stop=(last and kk == kt - 1 and n == 2))
    return mm


def item(k, e, s, pair, use, rhs, tokens, ready=None, base=0):
    e.wait_ge(k.split_lo[s], pair + 1)
    e.wait_ge(k.acc_free[s], use + 1)
    product(k, e, s, k.acc[s], KT, rhs, tokens, ready=ready, base=base).then_inc(k.acc_full[s], 1)



NORM_TILES = [NT, NT, NT, LAT // P]


class Norm:

    def __init__(self, k, n):
        self.n, self.tiles = n, NORM_TILES[n]
        self.tokens = self.tiles * P
        self.chunks = CHUNKS[self.tokens]
        self.diag = k.at(f"diag{n}", R0, [P, T])
        self.rr = k.at(f"rr{n}", R0 + T, [P, T])
        self.xr = k.at(f"xr{n}", R0 + 2 * T, [P, 2, T])
        self.diags = sum(NORM_TILES[:n])
        self.bcs = sum(len(CHUNKS[t * P]) for t in NORM_TILES[:n])
        self.h_base = n * KT

    def tensor(self, k, e):
        if k.sqs:
            e.wait_ge(k.ss_done, k.sqs)
        for j in range(self.tiles):
            mm = e.matmul(k.bank[:, 6, j:j + 1], k.ss[:, j * P:(j + 1) * P], k.ones[:, 0:1], start=True, stop=True)
        mm.then_inc(k.stat_full, 1)
        for c, (c0, n) in enumerate(self.chunks):
            e.wait_ge(k.diag_ready, self.diags + (c0 + n) // P)
            if c == 2:
                e.wait_ge(k.rr_ready, self.bcs + 1)
            e.matmul(k.bank[:, 7 - c % 2, 0:n], k.ones[:, :], self.diag[:, c0:c0 + n],
                     start=True, stop=True).then_inc(k.bc_full, 1)

    def vector(self, k, e, steps):
        t = self.tiles
        e.wait_ge(k.stat_full, self.n + 1)
        e.tensor_scalar(k.stat[:, 0:t], k.bank[:, 6, 0:t], 1.0 / D, EPS, ALU.mult, ALU.add).then_inc(k.ms_ready, 1)
        e.wait_ge(k.sd_ready, self.n + 1)
        steps(e.reciprocal(k.rstd[:, 0:t], k.stat[:, 0:t]))
        for j in range(t):
            e.tensor_scalar(self.diag[:, j * P:(j + 1) * P], k.ident[:, :], k.rstd[:, j:j + 1], None,
                            ALU.mult).then_inc(k.diag_ready, 1)
        e.wait_ge(k.rr_ready, self.bcs + len(self.chunks))
        def low(kk):
            e.wait_ge(k.hi_ready, self.h_base + kk + 1)
            e.tensor_tensor(k.h_lo[:, kk, 0:self.tokens], self.xr[:, kk % 2, 0:self.tokens],
                            k.h_hi[:, kk, 0:self.tokens].bitcast(F32), ALU.subtract).then_inc(k.h_ready, 1)

        for kk in range(KT):
            if kk >= 2:
                low(kk - 2)
                e.wait_ge(k.h_ready, self.h_base + kk - 1)
            e.tensor_tensor(self.xr[:, kk % 2, 0:self.tokens], k.x[:, kk, 0:self.tokens], self.rr[:, 0:self.tokens],
                            ALU.mult).then_inc(k.xr_ready, 1)
        low(KT - 2)
        low(KT - 1)

    def scalar(self, k, e):
        t, n = self.tiles, self.n
        e.wait_ge(k.ms_ready, n + 1)
        e.activation(k.stat[:, 0:t], k.stat[:, 0:t], ACT.Sqrt).then_inc(k.sd_ready, 1)
        for c, (c0, m) in enumerate(self.chunks):
            e.wait_ge(k.bc_full, self.bcs + c + 1)
            e.activation(self.rr[:, c0:c0 + m], k.bank[:, 7 - c % 2, 0:m], ACT.Copy).then_inc(k.rr_ready, 1)
        for kk in range(KT):
            e.wait_ge(k.xr_ready, self.h_base + kk + 1)
            for who, (c0, c1) in enumerate(((0, LAT), (LAT, T))[:1 + (self.tokens > LAT)]):
                at = (n * 2 + who) * 2 * KT + kk
                half = self.xr[:, kk % 2, c0:c1]
                ins = e.activation(half, half, ACT.Identity, scale=k.coef_a(n, who, kk), bias=k.coef_b(n, who, kk))
            ins.then_inc(k.h_mid, 1)
            e.wait_ge(k.h_mid, self.h_base + kk + 1)
            e.activation(k.h_hi[:, kk, 0:self.tokens], self.xr[:, kk % 2, 0:self.tokens], ACT.Copy
                         ).then_inc(k.hi_ready, 1)



ADA_M = 3
ADA_LOADS = 2 * 48 // ADA_M


class Stream:

    def __init__(self, k):
        words = KT * ADA_M * P
        assert H0 + 30080 + ADA_M * P <= END - words and words <= 4 * WS
        self.w = [k.at(f"ada_w{s}", at, [P, KT, ADA_M * P]) for s, at in enumerate((S0, END - words))]
        self.full = [k.sem(f"ada_landed{s}") for s in range(2)]
        self.sums = [k.sem(f"ada_sums{s}") for s in range(2)]
        self.read = [k.sem(f"ada_read{s}") for s in range(2)]
        self.stored = [k.sem(f"ada_stored{s}") for s in range(2)]
        self.columns = [k.sem(f"ada_columns{s}") for s in range(2)]
        self.row = [k.at(f"ada_row{s}", H0 + 28544 + s * ADA_M * P, [P, ADA_M * P]) for s in range(2)]
        self.out = [k.bank[0:2, 4 + s, 0:ADA_M * P] for s in range(2)]
        self.turned = [k.bank[:, 4 + s, ADA_M * P:ADA_M * (P + 2)] for s in range(2)]
        self.made = self.copied = 0

    def load(self, k, e):
        for s in range(2):
            e.dma_start(self.w[s][:, :, :], k.d["ada_w"][s]).then_inc(self.full[s], 16)
        with e.Fori(0, ADA_LOADS // 2 - 1) as i:
            for s in range(2):
                e.wait_ge(self.sums[s], i + 1)
                e.dma_start(self.w[s][:, :, :], k.d["ada_w"][i * 2 + (s + 2)]).then_inc(self.full[s], 16)

    def products(self, k, e, count):
        with e.Fori(0, count) as n:
            i = n + self.made
            for s in range(2):
                e.wait_ge(self.full[s], i * 16 + 16)
                e.wait_ge(self.stored[s], i + 1)
                for kk in range(KT):
                    mm = e.matmul(self.out[s], k.silu_c[:, 2 * kk:2 * kk + 2], self.w[s][:, kk, :],
                                  start=(kk == 0), stop=(kk == KT - 1))
                mm.then_inc(self.sums[s], 1)
            for s in range(2):
                e.wait_ge(self.read[s], i + 1)
                for m in range(ADA_M):
                    tr = e.matmul(self.turned[s][:, 2 * m:2 * m + 2], self.row[s][0:2, m * P:(m + 1) * P],
                                  k.ident[0:2, 0:2], start=True, stop=True)
                tr.then_inc(self.columns[s], 1)
        self.made += count

    def copy(self, k, e, count):
        with e.Fori(0, count) as n:
            i = n + self.copied
            for s in range(2):
                e.wait_ge(self.sums[s], i + 1)
                e.activation(self.row[s][0:2, :], self.out[s], ACT.Copy).then_inc(self.read[s], 1)
            for s in range(2):
                e.wait_ge(self.columns[s], i + 1)
                e.activation(k.mods[:, bass.ds(i * (4 * ADA_M) + 2 * ADA_M * s, 2 * ADA_M)], self.turned[s], ACT.Copy
                             ).then_inc(self.stored[s], 1)
        self.copied += count

    def coefficients(self, k, e, steps):
        for s in range(2):
            e.wait_ge(self.stored[s], ADA_LOADS // 2 + 1)
        mods = k.mods[:, :].rearrange("p (m w) -> p m w", w=2)
        bias = k.ada_b[:, :].unsqueeze(2).to_broadcast([P, 96, 2])
        steps(e.tensor_tensor(mods, mods, bias, ALU.add))
        for n in range(4):
            gain = k.gains[:, n * KT:(n + 1) * KT]
            for who in range(2):
                shift = mods[:, 24 * n:24 * n + 8, who]
                scale = mods[:, 24 * n + 8:24 * n + 16, who]
                a = k.coef[:, (n * 2 + who) * 16:(n * 2 + who) * 16 + 8]
                b = k.coef[:, (n * 2 + who) * 16 + 8:(n * 2 + who) * 16 + 16]
                steps(e.scalar_tensor_tensor(out=a, in0=scale, scalar=1.0, in1=gain, op0=ALU.add, op1=ALU.mult))
                steps(e.tensor_copy(b, shift))



def butterfly_lat(e, steps, x, y, t):
    def add(o, a, b, lag=0):
        steps(e.tensor_tensor(o, a, b, ALU.add), lag)

    def sub(o, a, b, lag=0):
        steps(e.tensor_tensor(o, a, b, ALU.subtract), lag)

    def fma(o, a, c, b, op=ALU.add, lag=0):
        steps(e.scalar_tensor_tensor(out=o, in0=a, scalar=c, in1=b, op0=ALU.mult, op1=op), lag)

    def scale(o, a, c, lag=0):
        steps(e.tensor_scalar(o, a, c, None, ALU.mult), lag)

    add(t[:, 0:2], x[:, 0:2], x[:, 6:8], 1)
    sub(t[:, 2:4], x[:, 0:2], x[:, 6:8], 1)
    add(t[:, 4:6], t[:, 0:2], x[:, 3:5], 2)
    add(t[:, 6], x[:, 2], x[:, 5], 2)
    sub(t[:, 7:9], t[:, 0:2], x[:, 3:5], 2)
    sub(t[:, 9], x[:, 2], x[:, 5], 1)
    add(t[:, 0], t[:, 5], t[:, 6], 1)
    sub(t[:, 1], t[:, 5], t[:, 6], 1)
    add(y[:, 0], t[:, 4], t[:, 0], 2)
    fma(y[:, 8], t[:, 0], -0.5, t[:, 4], lag=2)
    scale(y[:, 9], t[:, 1], -S3, 3)
    sub(t[:, 5], t[:, 8], t[:, 9], 4)
    add(t[:, 6], t[:, 8], t[:, 9], 1)
    sub(y[:, 1], t[:, 7], t[:, 5], 2)
    fma(y[:, 4], t[:, 5], 0.5, t[:, 7], lag=2)
    scale(y[:, 5], t[:, 6], -S3, 3)
    sub(t[:, 0], x[:, 2], x[:, 4], 1)
    add(t[:, 1], t[:, 3], x[:, 5], 1)
    sub(y[:, 6], t[:, 2], t[:, 0], 2)
    fma(t[:, 4], t[:, 0], 0.5, t[:, 2], lag=2)
    sub(y[:, 7], x[:, 3], t[:, 1], 2)
    fma(t[:, 5], t[:, 1], 0.5, x[:, 3], lag=2)
    sub(t[:, 6], t[:, 3], x[:, 5], 2)
    add(t[:, 7], x[:, 2], x[:, 4], 1)
    fma(y[:, 2], t[:, 6], S3, t[:, 4], lag=2)
    fma(y[:, 10], t[:, 6], -S3, t[:, 4], lag=2)
    fma(y[:, 3], t[:, 7], -S3, t[:, 5], ALU.subtract, 3)
    fma(y[:, 11], t[:, 7], S3, t[:, 5], ALU.subtract)


def butterfly_ctx(e, steps, x, y):
    steps(e.tensor_tensor(y[:, 0], x[:, 0], x[:, 1], ALU.add))
    steps(e.scalar_tensor_tensor(out=y[:, 2], in0=x[:, 1], scalar=-0.5, in1=x[:, 0], op0=ALU.mult, op1=ALU.add))
    steps(e.tensor_scalar(y[:, 3], x[:, 1], -S3, None, ALU.mult))


SPREAD_LAT = {0: (0,), 6: (1,), 1: (2, 3), 2: (4, 5), 3: (6, 7), 4: (8, 9), 5: (10, 11)}
SPREAD_CTX = {0: (0,), 4: (2, 3)}


def forward(e, k, tab, xh, r, spread, re, im):
    c = TF[r]
    tile = [tab[:, (c + n) * P:(c + n + 1) * P] for n in range(2 if len(spread) == 1 else 3)]
    if len(spread) == 1:
        e.matmul(re, tile[0], xh[:, spread[0], :], start=True, stop=True)
        return e.matmul(im, tile[1], xh[:, spread[0], :], start=True, stop=True)
    a, b = (xh[:, n, :] for n in spread)
    e.matmul(re, tile[0], a, start=True, stop=False)
    e.matmul(re, tile[1], b, start=False, stop=True)
    e.matmul(im, tile[0], b, start=True, stop=False)
    return e.matmul(im, tile[2], a, start=False, stop=True)


def inverse(e, tab, ys, r, pos, ct, out):
    c = TI[r]
    re, im = (ys[:, 2 * pos + n, ct * P:(ct + 1) * P] for n in range(2))
    if r in (0, 6):
        e.matmul(out, re, tab[:, (c + 1) * P:(c + 2) * P], start=True, stop=False)
        return e.matmul(out, im, tab[:, c * P:(c + 1) * P], start=False, stop=True)
    e.matmul(out, re, tab[:, (c + 1) * P:(c + 3) * P], start=True, stop=False)
    return e.matmul(out, im, tab[:, c * P:(c + 2) * P], start=False, stop=True)


def prologue(k):
    nc, d = k.nc, k.d
    Q = H0
    hw = k.at("hw", Q, [P, NT, D_HY])
    xh = k.at("f_xh", Q + 5120, [P, 12, D_HY])
    spec = k.at("f_spec", Q + 11264, [P, 14, D_HY])
    tab = k.at("f_tab", Q + 18432, [P, TAB])
    win = k.at("window", Q + 20864, [P, NT, D_HY])
    arg = k.at("f_arg", Q + 25984, [P, T])
    tmp = k.at("f_tmp", Q + 27264, [P, T])
    zin = k.at("f_z", Q + 28544, [P, T])
    w3 = k.at("f_w3", S0 + KT * ADA_M * P, [P, 2 * D_HY])
    sq = k.at("sq_first", Q + 5120, [P, 2, T])
    ada = Stream(k)
    names = ["gains", "ada_b", "hy_w", "hy_b", "hy_bias", "g_lat", "rg_w", "rg_b", "rg_ba", "ones"]
    lam, sp = k.rg_lam, k.rg_sp
    x_landed, vectors_landed, others, win_landed, tab_landed = (k.sem(n) for n in (
        "x_landed", "vectors_landed", "constants_landed", "window_landed", "table_landed"))
    decay_steps, acts, cleared = k.sem("decay_steps"), k.sem("setup_acts"), k.sem("x_cleared")
    w12 = k.at("f_w12", Q + 29824, [P, 2 * HID_F])
    TWO_PI = 2.0 * math.pi
    C1 = 6.28125
    C2 = float(np.float32(TWO_PI - C1))
    C3 = float(np.float32(TWO_PI - C1 - C2))
    MAGIC = 1.5 * 2.0 ** 23
    PI = float(np.nextafter(np.float32(math.pi), np.float32(0)))
    landed, w3_landed, mm_full, arg_ready = k.sem("f_landed"), k.sem("f_w3_landed"), k.sem("f_sums"), k.sem("f_arg")
    sin_ready, steps_sem, tile_full, hw_ready = k.sem("f_sin"), k.sem("f_steps"), k.sem("f_tile"), k.sem("f_hw")
    xh_ready, spec_full, spec_read, stored = k.sem("f_xh"), k.sem("f_spec"), k.sem("f_spec_read"), k.sem("f_stored")
    silu_ready, ident_landed = k.sem("silu_ready"), k.sem("ident_landed")
    npos = {"lat": len(ORDER_LAT), "ctx": len(ORDER_CTX)}
    jobs = [("lat", 0), ("ctx", 0), ("lat", 1), ("ctx", 1)]
    before = [sum(npos[p] for p, _ in jobs[:j]) for j in range(5)]
    with nc.Block() as block:
        @block.sync
        def _(e):
            e.dma_start(zin[0:EMB, :], d["filter_z"]).then_inc(landed, 16)
            e.dma_start(w12[0:EMB, 0:HID_F], d["hy_w1"]).then_inc(landed, 16)
            e.dma_start(w12[0:HID_F, HID_F:2 * HID_F], d["hy_w2"]).then_inc(landed, 16)
            e.dma_start(k.mlp[0:HID_F, :], d["mlp"]).then_inc(landed, 16)
            e.dma_start(k.cc[:, :], d["cc"]).then_inc(vectors_landed, 16)
            e.dma_start(lam[:, :], d["rg_lam"]).then_inc(vectors_landed, 16)
            e.dma_start(w3[0:HID_F, :], d["hy_w3"]).then_inc(w3_landed, 16)
            e.dma_start(k.ident[:, :], d["ident"]).then_inc(ident_landed, 16)
            e.dma_start(win[:, :, :], d["window"]).then_inc(win_landed, 16)
            e.dma_start(k.x[:, :, :], d["x"]).then_inc(x_landed, 16)
            e.dma_start(tab[:, :], d["tab_f"]).then_inc(tab_landed, 16)
            for name in names:
                e.dma_start(k.c[name][:, :], d[name]).then_inc(others, 16)
            ada.load(k, e)
            load_pair(k, e, 0)
            e.wait_ge(others, 16 * len(names))

        @block.tensor
        def _(e):
            for s in range(2):
                e.sem_inc(k.acc_free[s], 1)
                e.sem_inc(k.acc_full[s], 1)
            e.wait_ge(landed, 64)
            for c, n in CHUNKS[T]:
                mm = e.matmul(k.acc[0][0:HID_F, c:c + n], w12[0:EMB, 0:HID_F], zin[0:EMB, c:c + n], start=True, stop=True)
            mm.then_inc(mm_full, 1)
            e.wait_ge(silu_ready, 1)
            e.wait_ge(ident_landed, 16)
            e.wait_ge(sin_ready, 1)
            for c, n in CHUNKS[T]:
                mm = e.matmul(k.acc[0][0:HID_F, c:c + n], w12[0:HID_F, HID_F:2 * HID_F], tmp[0:HID_F, c:c + n],
                              start=True, stop=True)
            mm.then_inc(mm_full, 1)
            e.wait_ge(sin_ready, 2)
            e.wait_ge(w3_landed, 16)
            for order in range(2):
                for t in range(NT):
                    g = order * NT + t
                    if g >= 2:
                        e.wait_ge(hw_ready, g - 1)
                    e.matmul(k.bank[:, 6 + g % 2, :], tmp[0:HID_F, t * P:(t + 1) * P],
                             w3[0:HID_F, order * D_HY:(order + 1) * D_HY], start=True, stop=True).then_inc(tile_full, 1)
                ada.products(k, e, 4)
                if order == 0:
                    e.wait_ge(tab_landed, 16)
                for j in (2 * order, 2 * order + 1):
                    part = jobs[j][0]
                    e.wait_ge(xh_ready, j + 1)
                    residues, spread = (ORDER_LAT, SPREAD_LAT) if part == "lat" else (ORDER_CTX, SPREAD_CTX)
                    for pos, r in enumerate(residues):
                        g = before[j] + pos
                        if g >= 2:
                            e.wait_ge(spec_read, g - 1)
                        b = 2 * (g % 2)
                        forward(e, k, tab, xh, r, spread[r], k.bank[:, b, :], k.bank[:, b + 1, :]).then_inc(spec_full, 1)
                        if part == "lat" and pos in (2, 4):
                            ada.products(k, e, 1)
            ada.products(k, e, ADA_LOADS // 2 - ada.made)

        @block.vector
        def _(e):
            setup = Steps(e, decay_steps)
            e.wait_ge(acts, 2)
            setup(e.tensor_scalar(sp[:, 0:20], lam[:, :], -1.0, 0.0, ALU.mult, ALU.max))
            setup(e.tensor_scalar(sp[:, 40:60], sp[:, 20:40], 1.0, None, ALU.add))
            e.wait_ge(acts, 3)
            setup(e.tensor_tensor(sp[:, 20:40], sp[:, 0:20], sp[:, 60:80], ALU.add))
            setup(e.tensor_scalar(sp[:, 0:20], sp[:, 20:40], -8.0, None, ALU.mult))
            setup(e.tensor_scalar(sp[:, 60:80], sp[:, 20:40], 8.0, None, ALU.mult))
            steps = Steps(e, steps_sem)

            def reduce_angle(sums, n):
                rows = slice(0, HID_F)
                e.wait_ge(mm_full, n + 1)
                steps(e.tensor_scalar(arg[rows, :], sums[rows, 0:T], k.mlp[rows, n:n + 1], k.mlp[rows, 2:3], ALU.add, ALU.mult))
                steps(e.tensor_scalar(tmp[rows, :], arg[rows, :], 1.0 / TWO_PI, MAGIC, ALU.mult, ALU.add))
                steps(e.tensor_scalar(tmp[rows, :], tmp[rows, :], MAGIC, None, ALU.subtract))
                for c in (C1, C2, C3):
                    steps(e.scalar_tensor_tensor(out=arg[rows, :], in0=tmp[rows, :], scalar=-c, in1=arg[rows, :],
                                                 op0=ALU.mult, op1=ALU.add))
                e.tensor_scalar(arg[rows, :], arg[rows, :], PI, -PI, ALU.min, ALU.max).then_inc(arg_ready, 1)

            reduce_angle(k.acc[0], 0)
            reduce_angle(k.acc[0], 1)
            e.wait_ge(win_landed, 16)
            for order in range(2):
                for t in range(NT):
                    g = order * NT + t
                    e.wait_ge(tile_full, g + 1)
                    e.tensor_tensor(hw[:, t, :], k.bank[:, 6 + g % 2, :], win[:, t, :], ALU.mult).then_inc(hw_ready, 1)
                e.wait_ge(hw_ready, (order + 1) * NT)
                j = 2 * order
                if not j:
                    e.wait_ge(k.ss_done, KT)
                if j:
                    e.wait_ge(spec_full, before[j])
                    e.wait_ge(stored, 16 * j)
                butterfly_lat(e, steps, hw[:, 0:M_LAT], xh, spec[:, 0:10])
                e.sem_inc(xh_ready, 1)
                e.wait_ge(spec_full, before[j + 1])
                butterfly_ctx(e, steps, hw[:, M_LAT:NT], xh)
                e.sem_inc(xh_ready, 1)
            e.wait_ge(others, 16 * len(names))
            ada.coefficients(k, e, steps)

        @block.scalar
        def _(e):
            e.wait_ge(vectors_landed, 32)
            e.activation(k.silu_c[:, :], k.cc[:, :], ACT.Silu).then_inc(silu_ready, 1)
            e.activation(sp[:, 0:20], lam[:, :], ACT.Abs).then_inc(acts, 1)
            e.wait_ge(acts, 1)
            e.activation(sp[:, 20:40], sp[:, 0:20], ACT.Exp, scale=-1.0).then_inc(acts, 1)
            e.wait_ge(decay_steps, 2)
            e.activation(sp[:, 60:80], sp[:, 40:60], ACT.Ln).then_inc(acts, 1)
            for n in range(2):
                e.wait_ge(arg_ready, n + 1)
                e.activation(tmp[0:HID_F, :], arg[0:HID_F, :], ACT.Sin).then_inc(sin_ready, 1)
                e.wait_ge(x_landed, 16)
                for kk in range(n * KT // 2, (n + 1) * KT // 2):
                    if kk >= 2:
                        e.wait_ge(k.ss_done, kk - 1)
                    e.activation(sq[:, kk % 2, :], k.x[:, kk, :], ACT.Square).then_inc(k.sq_ready, 1)
            for j, (part, order) in enumerate(jobs):
                if part == "lat":
                    ada.copy(k, e, 4)
                if j:
                    e.wait_ge(stored, 16 * j)
                for pos in range(npos[part]):
                    g = before[j] + pos
                    e.wait_ge(spec_full, g + 1)
                    b = 2 * (g % 2)
                    e.activation(spec[:, 2 * pos:2 * pos + 2, :], k.bank[:, b:b + 2, :], ACT.Copy).then_inc(spec_read, 1)
                    if part == "lat" and pos in (2, 4):
                        ada.copy(k, e, 1)
                e.wait_ge(spec_read, before[j + 1])
                e.dma_start(d["spec_" + part][order], spec[:, 0:2 * npos[part], :]).then_inc(stored, 16)
            ada.copy(k, e, ADA_LOADS // 2 - ada.copied)
            e.wait_ge(stored, 64)

        @block.gpsimd
        def _(e):
            for s in range(2):
                e.sem_inc(ada.stored[s], 1)
            e.memset(k.ss[:, :], 0.0).then_inc(cleared, 1)
            e.wait_ge(cleared, 1)
            for kk in range(KT):
                e.wait_ge(k.sq_ready, kk + 1)
                e.tensor_tensor(k.ss[:, :], k.ss[:, :], sq[:, kk % 2, :], ALU.add).then_inc(k.ss_done, 1)
                e.wait_ge(k.ss_done, kk + 1)
    k.sqs += KT



def even_in(k):
    nc, d, ph = k.nc, k.d, PH["ev_in"]
    norm = Norm(k, 0)
    lat = k.at("lat", R0, [P, LT, T])
    rope = k.at("rope", R0 + 6400, [P, T])
    uc = k.at("uc", R0 + 7680, [P, 2, T])
    centre, done, steps_sem, stored = k.sem("tap1"), k.sem("conv3_done"), k.sem("conv3_steps"), k.sem("u_stored")
    uc_free = k.sem("uc_free")
    w0, a0 = ph.w0, ph.a0
    HP = 6
    taps = k.hy_w[:, :].rearrange("p (m t) -> p m t", t=3)
    with nc.Block() as block:
        @block.sync
        def _(e):
            load_weights(k, e, ph)

        @block.tensor
        def _(e):
            norm.tensor(k, e)
            with e.Fori(0, ph.pairs) as i:
                for s in range(2):
                    item(k, e, s, i + w0, i + a0, k.rhs_h, T, ready=k.h_ready, base=norm.h_base)

        @block.scalar
        def _(e):
            norm.scalar(k, e)
            split_hi(k, e, 0, w0, k.acc_full[0], 1)
            with e.Fori(0, HP) as i:
                for s in range(2):
                    split_hi(k, e, 1 - s, i + (w0 + s), k.acc_full[1 - s], i + (a0 + 1 + s))
                    e.wait_ge(k.acc_full[s], full(i + a0))
                    e.wait_ge(uc_free, i * 2 + (s + 1))
                    e.activation(uc[:, s, :], k.acc[s][:, 0:T], ACT.Identity, scale=taps[:, i * 2 + s, 1:2],
                                 bias=k.hy_b[:, bass.ds(i * 2 + s, 1)]).then_inc(centre, 1)
            for j in range(LT + 1):
                s, pair = j % 2, HP + j // 2
                if j < LT:
                    split_hi(k, e, 1 - s, w0 + pair + s, k.acc_full[1 - s], a0 + pair + 1 + s)
                e.wait_ge(k.acc_full[s], full(a0 + pair))
                if j < LT:
                    e.activation(lat[:, j, :], k.acc[s][:, 0:T], ACT.Copy).then_inc(k.acc_free[s], 1)
                else:
                    e.activation(rope[0:ROPE, :], k.acc[s][0:ROPE, 0:T], ACT.Copy).then_inc(k.acc_free[s], 1)

        @block.vector
        def _(e):
            steps = Steps(e, steps_sem)
            norm.vector(k, e, steps)
            split_lo(k, e, 0, w0)
            with steps.loop(HP, 6) as i:
                for s in range(2):
                    split_lo(k, e, 1 - s, i + (w0 + s))
                    e.wait_ge(centre, i * 2 + (s + 1))
                    n = 0
                    for a, b in ((0, LAT), (LAT, T)):
                        for tap, lo, hi, sh in ((0, a + 1, b, -1), (2, a, b - 1, 1)):
                            ins = e.scalar_tensor_tensor(
                                out=uc[:, s, lo:hi], in0=k.acc[s][:, lo + sh:hi + sh],
                                scalar=taps[:, i * 2 + s, tap:tap + 1], in1=uc[:, s, lo:hi], op0=ALU.mult, op1=ALU.add)
                            n += 1
                            if n < 4:
                                steps(ins)
                            else:
                                ins.then_inc(k.acc_free[s], 1)
                    e.wait_ge(k.acc_free[s], i + (a0 + 2))
                    e.sem_inc(done, 1)
            for j in range(LT):
                split_lo(k, e, 1 - j % 2, w0 + HP + j // 2 + j % 2)

        @block.gpsimd
        def _(e):
            e.sem_inc(uc_free, 2)
            with e.Fori(0, HP) as i:
                for s in range(2):
                    e.wait_ge(done, i * 2 + (s + 1))
                    e.dma_start(d["u"][i * 2 + s], uc[:, s, :]).then_inc(stored, 16)
                    e.wait_ge(stored, i * 32 + (16 * s + 16))
                    e.sem_inc(uc_free, 1)


def rotate(e, steps, x, out, cos, sin, t1, heads):
    shape = [P, heads, ROPE]
    steps(e.tensor_tensor(t1, x, cos.unsqueeze(1).to_broadcast(shape), ALU.mult))
    halves = lambda a: a.rearrange("p h (g c) -> p h g c", g=2)
    sb = halves(sin.unsqueeze(1).to_broadcast(shape))
    xv, ov = halves(x), halves(out)
    return t1, xv, sb


def latents(k):
    nc, d = k.nc, k.d
    lat = k.at("lat", R0, [P, LT, T])
    rope = k.at("rope", R0 + 6400, [P, T])
    kT = k.at("kT", X0, [P, HEADS, T])
    qT = k.at("qT", X0 + 10240, [P, HEADS, T])
    v = k.at("v", X0 + 20480, [P, NT, HEADS * VD])
    wq = k.at("wq", X0 + 25600, [P, 3, HEADS * QD])
    wkv = k.at("wkv", X0 + 27904, [P, 2, 1024])
    gq = k.at("gq", X0 + 29952, [P, QD])
    gk = k.at("gk", X0 + 30048, [P, QD])
    cos = k.at("cos", X0 + 30144, [P, NT, ROPE])
    sin = k.at("sin", R0 + 7680, [P, NT, ROPE])
    lcur = k.at("lcur", S0, [P, 2, LT, P])
    sqc = k.at("sqc", S0 + 1280, [P, 2, LT, P])
    at = R0 + 8000
    assert at + 5056 <= END
    qb = k.at("qb", at, [P, 2, HEADS, QD])
    kb = k.at("kb", at + 1536, [P, 2, HEADS, QD])
    sqq = k.at("sqq", at + 3072, [P, HEADS, QD])
    sqk = k.at("sqk", at + 3840, [P, HEADS, NOPE])
    sqr = k.at("sqr", at + 4352, [P, ROPE])
    krow = k.at("krow", at + 4384, [P, 1, ROPE])
    kout = k.at("kout", at + 4416, [P, 1, ROPE])
    st = k.at("st", at + 4448, [P, 8])
    ss = k.at("hs", at + 4456, [P, 32])
    rcur = k.at("rcur", at + 4488, [P, 2, P])
    t1 = k.at("rot1", S0 + 2560, [P, HEADS, ROPE])
    t2 = k.at("rot2", S0 + 2816, [P, HEADS, ROPE])
    landed, folded = k.sem("m_landed"), k.sem("m_folded")
    cur, sq_ready = [k.sem(f"m_cur{s}") for s in range(2)], k.sem("m_sq")
    sums, tr_full = k.sem("m_sums"), k.sem("m_tr")
    ms, sd, hsq, hss, hsd, vout, tok = (k.sem("m_" + n) for n in ("ms", "sd", "hsq", "hss", "hsd", "v", "tok"))
    freed = [k.sem(f"m_freed{s}") for s in range(2)]
    steps_sem = k.sem("m_steps")
    HH = HEADS // 2
    qps = lambda s: k.bank[:, 4 * s:4 * s + 2, 0:HH * QD].rearrange("p b (h c) -> p b h c", c=QD)
    kvps = lambda s: k.bank[:, 4 * s + 2:4 * s + 4, :].rearrange("p b (h c) -> p b h c", c=NOPE + VD)
    two = lambda a: a.rearrange("p (b h) c -> p b h c", b=2)

    with nc.Block() as block:
        @block.sync
        def _(e):
            for t, name in ((wq, "w_uq"), (wkv, "w_ukv"), (cos, "cos"), (sin, "sin")):
                e.dma_start(t[:, :, :], d[name]).then_inc(landed, 16)
            e.dma_start(gq[:, :], d["gq"]).then_inc(landed, 16)
            e.dma_start(gk[:, :], d["gk"]).then_inc(landed, 16)
            e.wait_ge(landed, 96)

        @block.gpsimd
        def _(e):
            with e.Fori(0, NT // 2) as i:
                for s in range(2):
                    e.wait_ge(freed[s], i * 2 + 2)
                    e.tensor_copy(lcur[:, s, :, :], lat[:, :, bass.ds(i * 256 + s * P, P)]).then_inc(cur[s], 1)
                    e.tensor_copy(rcur[0:ROPE, s, :], rope[0:ROPE, bass.ds(i * 256 + s * P, P)]).then_inc(cur[s], 1)

        @block.tensor
        def _(e):
            e.wait_ge(folded, 5)
            with e.Fori(0, NT // 2) as i:
                for s in range(2):
                    e.wait_ge(freed[s], i * 2 + 2)
                    e.wait_ge(cur[s], i * 2 + 2)
                    for half in range(2):
                        for kk in range(3):
                            e.matmul(k.bank[:, 4 * s + half, 0:HH * QD], lcur[:, s, kk, :],
                                     wq[:, kk, half * HH * QD:(half + 1) * HH * QD], start=(kk == 0), stop=(kk == 2))
                        for kk in range(2):
                            e.matmul(k.bank[:, 4 * s + 2 + half, :], lcur[:, s, 3 + kk, :],
                                     wkv[:, kk, half * 512:(half + 1) * 512], start=(kk == 0), stop=(kk == 1))
                    e.transpose(k.bank[:, 4 * s + 1, 384:384 + ROPE], rcur[0:ROPE, s, :], k.ident[0:ROPE, 0:ROPE])
                    e.wait_ge(sq_ready, i * 2 + (s + 1))
                    for kk in range(LT):
                        c = 384 if kk < 3 else 386
                        mm = e.matmul(k.bank[:, 4 * s, c:c + 1], sqc[:, s, kk, :], k.ones[:, 0:1],
                                      start=kk in (0, 3), stop=kk in (2, 4))
                    mm.then_inc(sums, 1)
                for s in range(2):
                    e.wait_ge(tok, i * 2 + (s + 1))
                    e.wait_ge(vout, i * 2 + (s + 1))
                    for h in range(HEADS):
                        e.transpose(k.bank[0:QD, 4 * s + h // 4, (h % 4) * P:(h % 4 + 1) * P], qb[:, s, h, :], k.ident[:, :])
                    for h in range(HEADS):
                        mm = e.transpose(k.bank[0:QD, 4 * s + 2 + h // 4, (h % 4) * P:(h % 4 + 1) * P], kb[:, s, h, :],
                                         k.ident[:, :])
                    mm.then_inc(tr_full, 1)

        @block.scalar
        def _(e):
            with e.Fori(0, NT // 2) as i:
                for s in range(2):
                    e.wait_ge(cur[s], i * 2 + 2)
                    e.activation(sqc[:, s, :, :], lcur[:, s, :, :], ACT.Square).then_inc(sq_ready, 1)
                for s in range(2):
                    e.wait_ge(ms, i * 2 + (s + 1))
                    e.activation(st[:, 2:4], st[:, 0:2], ACT.Sqrt).then_inc(sd, 1)
                    e.wait_ge(hss, i * 4 + (2 * s + 1))
                    e.activation(two(sqq[:, :, :]), qps(s), ACT.Square, scale=st[:, 4:5]).then_inc(hsq, 1)
                    e.activation(two(sqk[:, :, :]), kvps(s)[:, :, :, 0:NOPE], ACT.Square, scale=st[:, 5:6]).then_inc(hsq, 1)
                    e.activation(sqr[:, :], k.bank[:, 4 * s + 1, 384:384 + ROPE], ACT.Square).then_inc(hsq, 1)
                    e.activation(v[:, i * 2 + s, :].rearrange("p (b h c) -> p b h c", b=2, c=VD), kvps(s)[:, :, :, NOPE:],
                                 ACT.Copy, scale=st[:, 5:6]).then_inc(vout, 1)
                    e.wait_ge(hss, i * 4 + (2 * s + 2))
                    e.activation(ss[:, 0:25], ss[:, 0:25], ACT.Sqrt).then_inc(hsd, 1)
                for s in range(2):
                    e.wait_ge(tr_full, i * 2 + (s + 1))
                    e.activation(qT[0:QD, :, bass.ds(i * 256 + s * P, P)].rearrange("p (b h) c -> p b h c", b=2),
                                 k.bank[0:QD, 4 * s:4 * s + 2, :].rearrange("p b (h c) -> p b h c", c=P),
                                 ACT.Copy).then_inc(freed[s], 1)

        @block.vector
        def _(e):
            for s in range(2):
                e.sem_inc(freed[s], 2)
            steps = Steps(e, steps_sem)
            e.wait_ge(landed, 96)
            for kk in range(3):
                e.tensor_scalar(wq[:, kk, :], wq[:, kk, :], k.g_lat[:, kk:kk + 1], None, ALU.mult).then_inc(folded, 1)
            for kk in range(2):
                e.tensor_scalar(wkv[:, kk, :], wkv[:, kk, :], k.g_lat[:, 3 + kk:4 + kk], None, ALU.mult).then_inc(folded, 1)
            with steps.loop(NT // 2, 48) as i:
                for s in range(2):
                    q, kk_, kr = qb[:, s, :, :], kb[:, s, :, :], k.bank[:, 4 * s + 1, 384:384 + ROPE]
                    e.wait_ge(sums, i * 2 + (s + 1))
                    steps(e.tensor_scalar(st[:, 0:1], k.bank[:, 4 * s, 384:385], 1.0 / Q_RANK, EPS, ALU.mult, ALU.add))
                    e.tensor_scalar(st[:, 1:2], k.bank[:, 4 * s, 386:387], 1.0 / KV_RANK, EPS, ALU.mult, ALU.add).then_inc(ms, 1)
                    e.wait_ge(sd, i * 2 + (s + 1))
                    e.reciprocal(st[:, 4:6], st[:, 2:4]).then_inc(hss, 1)
                    e.wait_ge(hsq, i * 6 + (3 * s + 3))
                    e.wait_ge(hss, i * 4 + (2 * s + 1))
                    steps(e.tensor_reduce(ss[:, 0:8], sqq[:, :, 0:NOPE], AX_X, ALU.add), 1)
                    steps(e.tensor_reduce(ss[:, 8:16], sqk[:, :, :], AX_X, ALU.add), 2)
                    steps(e.tensor_reduce(ss[:, 16:24], sqq[:, :, NOPE:QD], AX_X, ALU.add), 3)
                    steps(e.tensor_reduce(ss[:, 24:25], sqr[:, :], AX_X, ALU.add), 2)
                    steps(e.tensor_scalar(ss[:, 0:16], ss[:, 0:16], 1.0 / NOPE, EPS, ALU.mult, ALU.add), 1)
                    e.tensor_scalar(ss[:, 16:25], ss[:, 16:25], 1.0 / ROPE, EPS, ALU.mult, ALU.add).then_inc(hss, 1)
                    e.wait_ge(hsd, i * 2 + (s + 1))
                    steps(e.reciprocal(ss[:, 0:25], ss[:, 0:25]))
                    steps(e.tensor_scalar(ss[:, 0:8], ss[:, 0:8], st[:, 4:5], None, ALU.mult), 1)
                    steps(e.tensor_scalar(ss[:, 16:24], ss[:, 16:24], st[:, 4:5], None, ALU.mult), 2)
                    steps(e.tensor_scalar(ss[:, 8:16], ss[:, 8:16], st[:, 5:6], None, ALU.mult), 2)
                    bc = lambda a, n: a.rearrange("p (b h) -> p b h", b=2).unsqueeze(3).to_broadcast([P, 2, HH, n])
                    steps(e.tensor_tensor(two(q[:, :, 0:NOPE]), qps(s)[:, :, :, 0:NOPE], bc(ss[:, 0:8], NOPE), ALU.mult), 2)
                    steps(e.tensor_tensor(two(q[:, :, NOPE:QD]), qps(s)[:, :, :, NOPE:QD], bc(ss[:, 16:24], ROPE), ALU.mult), 2)
                    steps(e.tensor_tensor(two(kk_[:, :, 0:NOPE]), kvps(s)[:, :, :, 0:NOPE], bc(ss[:, 8:16], NOPE), ALU.mult), 3)
                    steps(e.scalar_tensor_tensor(out=krow[:, 0, :], in0=kr, scalar=ss[:, 24:25], in1=gk[:, NOPE:QD],
                                                 op0=ALU.mult, op1=ALU.mult), 2)
                    steps(e.tensor_tensor(q, q, gq[:, :].unsqueeze(1).to_broadcast([P, HEADS, QD]), ALU.mult), 2)
                    steps(e.tensor_tensor(kk_[:, :, 0:NOPE], kk_[:, :, 0:NOPE],
                                          gk[:, 0:NOPE].unsqueeze(1).to_broadcast([P, HEADS, NOPE]), ALU.mult), 1)
                    for x, out, tmp1, tmp2, n in ((q[:, :, NOPE:QD], q[:, :, NOPE:QD], t1[:, :, :], t2[:, :, :], HEADS),
                                                  (krow[:, :, :], kout[:, :, :], t1[:, 0:1, :], t2[:, 0:1, :], 1)):
                        tile = i * 2 + s
                        co = cos[:, tile, :].unsqueeze(1).to_broadcast([P, n, ROPE])
                        steps(e.tensor_tensor(tmp1, x, co, ALU.mult), 1)
                        for a in range(2):
                            pick = lambda y, b: y.rearrange("p h (g c) -> p h g c", g=2)[:, :, :, 8 * b:8 * b + 8]
                            si = sin[:, tile, :].rearrange("p (g c) -> p g c", g=2)[:, :, 8 * a:8 * a + 8]
                            steps(e.tensor_tensor(pick(tmp2, a), pick(x, 1 - a),
                                                  si.unsqueeze(1).to_broadcast([P, n, 2, 8]), ALU.mult), 2 - 2 * a)
                        steps(e.tensor_tensor(out, tmp1, tmp2, ALU.add))
                    e.tensor_copy(kk_[:, :, NOPE:QD], kout[:, :, :].to_broadcast([P, HEADS, ROPE])).then_inc(tok, 1)
                for s in range(2):
                    e.wait_ge(tr_full, i * 2 + (s + 1))
                    e.tensor_copy(kT[0:QD, :, bass.ds(i * 256 + s * P, P)].rearrange("p (b h) c -> p b h c", b=2),
                                  k.bank[0:QD, 4 * s + 2:4 * s + 4, :].rearrange("p b (h c) -> p b h c", c=P)
                                  ).then_inc(freed[s], 1)


def attention(k):
    nc = k.nc
    kT = k.at("kT", X0, [P, HEADS, T])
    qT = k.at("qT", X0 + 10240, [P, HEADS, T])
    v = k.at("v", X0 + 20480, [P, NT, HEADS * VD])
    att = k.at("att_tok", X0 + 25600, [P, NT, HEADS * VD])
    assert X0 + 30720 == R0 and R0 + 7712 <= ATT0
    p = k.at("probs", R0, [P, 2, T])
    pT = k.at("probsT", R0 + 2560, [P, 2, NT, P])
    qcur = k.at("qcur", R0 + 5120, [P, 2, T])
    mx = k.at("mx", R0 + 7680, [P, 2])
    ng = k.at("ng", R0 + 7688, [P, 2])
    rs = k.at("rs", R0 + 7696, [P, 2])
    ri = k.at("ri", R0 + 7704, [P, 2])
    attT = k.at("attT", ATT0, [P, 4, T])
    q_ready, s_full, mx_ready, p_ready = k.sem("a_q"), k.sem("a_scores"), k.sem("a_max"), k.sem("a_p")
    t_full, t_read, pv_full, pv_out = k.sem("a_t"), k.sem("a_t_read"), k.sem("a_pv"), k.sem("a_out")
    max_made, inverse_ready = k.sem("a_max_made"), k.sem("a_inverse")
    aT_full, aT_read = k.sem("a_aT"), k.sem("a_aT_read")
    N = 2 * NT
    TURNS = HEADS // 2
    kinds = [(hp, j, NT, 0) if j < LAT // P else (hp, j, CTX // P, LAT) for hp in range(2) for j in range(NT)]
    groups = lambda keys: [(g, min(4, keys - g)) for g in range(0, keys, 4)]
    G = [sum(len(groups(kind[2])) for kind in kinds[:n]) for n in range(N + 1)]
    assert N % 2 == 0 and G[N] % 2 == 0

    class Turn:

        def __init__(self, i):
            self.i = i

        def kind(self, n):
            return kinds[n % N]

        def head(self, n):
            return self.i * 2 + (kinds[n % N][0] + 2 * (n // N))

        def step(self, n):
            return self.i * N + n

        def group(self, n):
            return self.i * G[N] + (G[n % N] + n // N * G[N])

    def turns(e, body):
        with e.Fori(0, TURNS - 1) as i:
            body(Turn(i), False)
        body(Turn(TURNS - 1), True)

    flat = lambda n: k.acc[n % 2]

    with nc.Block() as block:
        @block.gpsimd
        def _(e):
            for h in range(2):
                e.tensor_copy(qcur[0:QD, h, :], qT[0:QD, h, :]).then_inc(q_ready, 1)
            with e.Fori(0, TURNS - 1) as i:
                for hp in range(2):
                    e.wait_ge(s_full, i * N + (hp * NT + NT))
                    e.tensor_copy(qcur[0:QD, hp, :], qT[0:QD, i * 2 + (hp + 2), :]).then_inc(q_ready, 1)

        @block.tensor
        def _(e):
            e.sem_inc(pv_out, 2)
            e.sem_inc(t_read, 2)

            def scores(t, n, chunks):
                hp, j, keys, k0 = t.kind(n)
                if j == 0 and chunks[0] == 0:
                    e.wait_ge(q_ready, t.head(n) + 1)
                for c in chunks:
                    m = min(BANK, keys * P - c * BANK)
                    if m <= 0:
                        continue
                    mm = e.matmul(k.bank[:, 3 * (n % 2) + c, 0:m], qcur[0:QD, hp, j * P:(j + 1) * P],
                                  kT[0:QD, t.head(n), k0 + c * BANK:k0 + c * BANK + m], start=True, stop=True)
                    if c == (keys * P - 1) // BANK:
                        mm.then_inc(s_full, 1)

            def body(t, ends):
                for n in range(N):
                    hp, j, keys, k0 = t.kind(n)
                    ahead = n + 2 < N or not ends
                    e.wait_ge(p_ready, t.step(n) + 1)
                    for g, (g0, m) in enumerate(groups(keys)):
                        e.wait_ge(t_read, t.group(n) + (g + 1))
                        if g < 2:
                            e.wait_ge(pv_out, t.step(n) + (g + 1))
                        for kt in range(g0, g0 + m):
                            tr = e.transpose(k.bank[:, 6 + (G[n] + g) % 2, (kt - g0) * P:(kt - g0 + 1) * P],
                                             p[:, n % 2, kt * P:(kt + 1) * P], k.ident[:, :])
                        tr.then_inc(t_full, 1)
                        if ahead:
                            scores(t, n + 2, [g] if g < len(groups(keys)) - 1 else list(range(g, 3)))
                    e.wait_ge(t_read, t.group(n) + (len(groups(keys)) + 2))
                    for kt in range(keys):
                        mm = e.matmul(k.bank[:, 6 + (G[n + 1] - 1) % 2, 256:256 + VD], pT[:, n % 2, kt, :],
                                      v[:, k0 // P + kt, bass.ds(t.head(n) * VD, VD)],
                                      start=(kt == 0), stop=(kt == keys - 1))
                    mm.then_inc(pv_full, 1)

            scores(Turn(0), 0, [0, 1, 2])
            scores(Turn(0), 1, [0, 1, 2])
            turns(e, body)
            e.wait_ge(pv_out, 2 + N * TURNS)
            for t in range(NT):
                if t >= 8:
                    e.wait_ge(aT_read, t - 7)
                for f in range(4):
                    tr = e.transpose(k.bank[:, t % 8, f * P:(f + 1) * P], att[:, t, f * P:(f + 1) * P], k.ident[:, :])
                tr.then_inc(aT_full, 1)

        @block.vector
        def _(e):
            def maximum(t, n):
                keys = t.kind(n)[2]
                e.wait_ge(s_full, t.step(n) + 1)
                e.reduce_max(mx[:, n % 2:n % 2 + 1], flat(n)[:, 0:keys * P], AX_X).then_inc(max_made, 1)
                e.wait_ge(max_made, t.step(n) + 1)
                e.tensor_scalar(ng[:, n % 2:n % 2 + 1], mx[:, n % 2:n % 2 + 1], -MLA_SCALE, None,
                                ALU.mult).then_inc(mx_ready, 1)

            def body(t, ends):
                for n in range(N):
                    hp, j, keys, k0 = t.kind(n)
                    if n + 2 < N or not ends:
                        maximum(t, n + 2)
                    e.wait_ge(p_ready, t.step(n) + 1)
                    e.reciprocal(ri[:, n % 2:n % 2 + 1], rs[:, n % 2:n % 2 + 1]).then_inc(inverse_ready, 1)
                    e.wait_ge(inverse_ready, t.step(n) + 3)
                    e.wait_ge(pv_full, t.step(n) + 1)
                    e.tensor_scalar(att[:, j, bass.ds(t.head(n) * VD, VD)], k.bank[:, 6 + (G[n + 1] - 1) % 2, 256:256 + VD],
                                    ri[:, n % 2:n % 2 + 1], None, ALU.mult).then_inc(pv_out, 1)

            e.sem_inc(inverse_ready, 2)
            maximum(Turn(0), 0)
            maximum(Turn(0), 1)
            turns(e, body)

        @block.scalar
        def _(e):
            def exps(t, n):
                keys = t.kind(n)[2]
                e.wait_ge(mx_ready, t.step(n) + 1)
                e.wait_ge(inverse_ready, t.step(n) + 1)
                e.activation(p[:, n % 2, 0:keys * P], flat(n)[:, 0:keys * P], ACT.Exp, bias=ng[:, n % 2:n % 2 + 1],
                             scale=MLA_SCALE, accum_out=rs[:, n % 2:n % 2 + 1]).then_inc(p_ready, 1)

            def body(t, ends):
                for n in range(N):
                    keys = t.kind(n)[2]
                    if n + 1 < N or not ends:
                        exps(t, n + 1)
                    e.wait_ge(pv_out, t.step(n) + 1)
                    for g, (g0, m) in enumerate(groups(keys)):
                        e.wait_ge(t_full, t.group(n) + (g + 1))
                        e.activation(pT[:, n % 2, g0:g0 + m, :].rearrange("p a b -> p (a b)"),
                                     k.bank[:, 6 + (G[n] + g) % 2, 0:m * P], ACT.Copy).then_inc(t_read, 1)

            exps(Turn(0), 0)
            turns(e, body)
            for t in range(NT):
                e.wait_ge(aT_full, t + 1)
                e.activation(attT[:, :, t * P:(t + 1) * P], k.bank[:, t % 8, :].rearrange("p (f c) -> p f c", c=P),
                             ACT.Copy).then_inc(aT_read, 1)


def hyena(k):
    nc, d = k.nc, k.d
    at, CH = X0, D_HY // 2
    xh = [k.at(f"h_xh{h}", at + h * 14 * CH, [P, 14, CH]) for h in range(2)]
    yr = [k.at(f"h_yr{h}", at + h * 14 * CH, [P, 2, 1536]) for h in range(2)]
    ys = [k.at(f"h_ys{h}", at + 7168 + h * 14 * CH, [P, 14, CH]) for h in range(2)]
    spec = k.at("h_spec", at + 14336, [P, 14, D_HY])
    gate = k.at("h_gate", at + 21504, [P, CT, T])
    zt = [k.at(f"h_zt{h}", at + 26624 + h * M_LAT * CH, [P, M_LAT, CH]) for h in range(2)]
    cv = [k.at(f"h_cv{h}", at + 26624 + h * M_LAT * CH, [P, 2, LAT]) for h in range(2)]
    z = k.at("h_z", R0, [P, CT, T])
    ti = k.at("h_ti", R0 + 5120, [P, TAB])
    assert R0 + 5120 + TAB <= ATT0 and at + 30720 == R0
    tf = k.at("h_tf", S0, [P, TAB])
    t = [k.at(f"h_t{n}", S0 + TAB + n * CH, [P, CH]) for n in range(4)]
    g_tmp = [k.at(f"h_bt{h}", at + 7168 + h * 14 * CH, [P, 10, CH]) for h in range(2)]
    i_tmp = [k.at(f"h_it{h}", at + 7168 + h * 14 * CH, [P, 14 * CH]) for h in range(2)]
    landed, spec_in, gate_in = k.sem("y_landed"), k.sem("y_spec_in"), k.sem("y_gate_in")
    zt_full, zt_read, xh_ready, sp_full, sp_read = (k.sem("y_" + n) for n in ("ztf", "ztr", "xh", "spf", "spr"))
    yr_full, yr_read, z_ready, steps_sem = (k.sem("y_" + n) for n in ("yrf", "yrr", "z", "steps"))
    blocks = {"lat": M_LAT, "ctx": M_CTX}
    resid = {"lat": ORDER_LAT, "ctx": ORDER_CTX}
    spread = {"lat": SPREAD_LAT, "ctx": SPREAD_CTX}
    yo = {"lat": YO_LAT, "ctx": YO_CTX}
    jobs = [(part, order, h) for part, order in JOBS for h in range(2)]
    pairs = [[(j, *jobs[j]) for j in (2 * u, 2 * u + 1)] for u in range(len(JOBS))]
    zb = [sum(blocks[p] for p, _, _ in jobs[:j]) for j in range(9)]
    pb = [sum(len(resid[p]) for p, _, _ in jobs[:j]) for j in range(9)]
    tok0 = {"lat": 0, "ctx": LAT}
    width = {"lat": 1536, "ctx": 384}
    spare = k.at("h_spare", S0 + TAB + 4 * CH, [P, 2, 2, P])
    assert TAB + 4 * CH + 4 * P <= 4 * WS
    sums = lambda h: k.bank[:, 4 * h:4 * h + 3, :].rearrange("p b n -> p (b n)")
    with nc.Block() as block:
        @block.sync
        def _(e):
            e.dma_start(z[:, :, :], d["u"][0:CT].rearrange("m p t -> p m t")).then_inc(landed, 16)
            e.dma_start(tf[:, :], d["tab_f"]).then_inc(landed, 16)
            e.dma_start(ti[:, :], d["tab_i"]).then_inc(landed, 16)
            for j, (part, order) in enumerate(JOBS):
                if j:
                    e.wait_ge(sp_read, pb[2 * j])
                e.dma_start(spec[:, 0:2 * len(resid[part]), :], d["spec_" + part][order]).then_inc(spec_in, 16)
                if j:
                    e.wait_ge(z_ready, 2 * j)
                e.dma_start(gate[:, :, :], d["u"][CT * (1 + order):CT * (2 + order)].rearrange("m p t -> p m t")
                            ).then_inc(gate_in, 16)
            e.wait_ge(gate_in, 64)

        @block.tensor
        def _(e):
            e.wait_ge(landed, 48)
            for pair in pairs:
                for j, part, order, h in pair:
                    if j >= 2:
                        e.wait_ge(z_ready, j - 1)
                        e.wait_ge(yr_read, 2 * (j - h))
                    for m in range(blocks[part]):
                        for c in range(2):
                            tok = tok0[part] + m * P
                            tr = e.transpose(k.bank[:, 4 * h + m // 2, m % 2 * CH + c * P:m % 2 * CH + (c + 1) * P],
                                             z[:, 2 * h + c, tok:tok + P], k.ident[:, :])
                        if m % 2:
                            tr.then_inc(zt_full, 1)
                for j, part, order, h in pair:
                    e.wait_ge(xh_ready, j + 1)
                    for pos, r in enumerate(resid[part]):
                        b = 4 * h + pos % 4
                        if pos >= 4:
                            e.wait_ge(sp_read, pb[j] + pos - 3)
                        forward(e, k, tf, xh[h], r, spread[part][r], k.bank[:, b, 0:CH], k.bank[:, b, CH:]
                                ).then_inc(sp_full, 1)
                for j, part, order, h in pair:
                    e.wait_ge(sp_read, pb[j + 1])
                    for c in range(2):
                        if c:
                            e.wait_ge(yr_read, 2 * j + 1)
                        out = sums(h)
                        for pos, r in enumerate(resid[part]):
                            o = yo[part][r]
                            mm = inverse(e, ti, ys[h], r, pos, c, out[:, o:o + (P if r in (0, 6) else 2 * P)])
                        mm.then_inc(yr_full, 1)

        @block.scalar
        def _(e):
            for pair in pairs:
                for j, part, order, h in pair:
                    for m in range(0, blocks[part], 2):
                        e.wait_ge(zt_full, (zb[j] + m) // 2 + 1)
                        e.activation(zt[h][:, m:m + 2, :].rearrange("p m c -> p (m c)"), k.bank[:, 4 * h + m // 2, :],
                                     ACT.Copy).then_inc(zt_read, 1)
                for j, part, order, h in pair:
                    for c in range(2):
                        e.wait_ge(yr_full, 2 * j + c + 1)
                        e.activation(yr[h][:, c, 0:width[part]], sums(h)[:, 0:width[part]], ACT.Copy).then_inc(yr_read, 1)

        @block.vector
        def _(e):
            steps = Steps(e, steps_sem)

            def tt(o, a, b, op, lag=0):
                steps(e.tensor_tensor(o, a, b, op), lag)

            def fma(o, a, c, b, op=ALU.add, lag=0):
                steps(e.scalar_tensor_tensor(out=o, in0=a, scalar=c, in1=b, op0=ALU.mult, op1=op), lag)

            def products(j, part, h):
                for pos in range(len(resid[part])):
                    e.wait_ge(sp_full, pb[j] + pos + 1)
                    b = 4 * h + pos % 4
                    zr, zi = k.bank[:, b, 0:CH], k.bank[:, b, CH:]
                    hr, hi = (spec[:, 2 * pos + n, h * CH:(h + 1) * CH] for n in range(2))
                    tt(t[0][:, :], zr, hr, ALU.mult, 1)
                    tt(t[1][:, :], zi, hi, ALU.mult, 1)
                    if pos:
                        e.wait_ge(sp_read, pb[j] + pos)
                    tt(t[2][:, :], zr, hi, ALU.mult, 1)
                    tt(t[3][:, :], zi, hr, ALU.mult, 2)
                    tt(ys[h][:, 2 * pos, :], t[0][:, :], t[1][:, :], ALU.subtract, 1)
                    e.tensor_tensor(ys[h][:, 2 * pos + 1, :], t[2][:, :], t[3][:, :], ALU.add).then_inc(sp_read, 1)
                    steps.settle()
                e.wait_ge(sp_read, pb[j] + pos + 1)

            def back_lat(yr, cv, i_tmp):
                y = lambda r, im=0, n=P: yr[:, :, YO_LAT[r] + im * P:YO_LAT[r] + im * P + n]
                buf = lambda n, w=P: i_tmp[:, n * 256:n * 256 + 2 * w].rearrange("p (c t) -> p c t", c=2)
                ps, qw = buf(0, 2 * P), buf(2, 2 * P)
                u, v = [buf(4 + n) for n in range(3)], [buf(7 + n) for n in range(3)]
                ev, od, od2 = [buf(10), buf(11)], [buf(12), buf(13)], [spare[:, n] for n in range(2)]
                out = lambda m: cv[:, :, m * P:(m + 1) * P]
                tt(ps, y(1, n=2 * P), y(5, n=2 * P), ALU.add, 1)
                tt(qw, y(1, n=2 * P), y(5, n=2 * P), ALU.subtract, 2)
                p_, s_, q_, w_ = ps[:, :, 0:P], ps[:, :, P:], qw[:, :, 0:P], qw[:, :, P:]
                tt(u[0], y(0), y(4), ALU.add, 3)
                fma(ev[0], y(4), -0.5, y(0), lag=2)
                fma(ev[1], y(2), -0.5, y(6), lag=1)
                fma(u[1], y(4, 1), -S3, ev[0], lag=2)
                fma(u[2], y(4, 1), S3, ev[0], lag=2)
                fma(v[1], y(2, 1), S3, ev[1], lag=3)
                fma(v[2], y(2, 1), -S3, ev[1], lag=4)
                tt(v[0], y(6), y(2), ALU.add)

                def even(m, lag):
                    tt(ev[m % 2], u[m % 3], v[m % 3], ALU.subtract if m % 2 else ALU.add, lag)

                def emit(ms):
                    for m in ms:
                        tt(out(m + 2), ev[m % 2], od[m % 2], ALU.subtract, 1)
                    for m in ms:
                        if m >= 4:
                            tt(out(m - 4), ev[m % 2], od[m % 2], ALU.add, 1)
                    steps.settle()

                even(0, 1)
                even(3, 1)
                tt(od[0], p_, y(3), ALU.add, 1)
                tt(od[1], y(3, 1), s_, ALU.subtract, 1)
                emit((0, 3))
                even(1, 1)
                fma(od2[0], s_, -0.5, y(3, 1), ALU.subtract, 1)
                fma(od2[1], p_, -0.5, y(3), lag=1)
                fma(od[1], q_, S3, od2[0], lag=1)
                fma(od[0], w_, -S3, od2[1], lag=1)
                even(4, 1)
                emit((1, 4))
                even(5, 1)
                fma(od2[1], p_, 0.5, y(3), ALU.subtract, 1)
                fma(od[1], q_, -S3, od2[0], lag=1)
                even(2, 1)
                fma(od[0], w_, -S3, od2[1])
                emit((5, 2))

            def back_ctx(yr, cv, i_tmp):
                re, im, r0 = yr[:, :, 0:P], yr[:, :, P:2 * P], yr[:, :, 2 * P:3 * P]
                tmp = i_tmp[:, 0:256].rearrange("p (c t) -> p c t", c=2)
                fma(tmp, re, -0.5, r0)
                fma(cv[:, :, 0:P], im, -S3, tmp)
                fma(cv[:, :, P:2 * P], im, S3, tmp)

            for pair in pairs:
                for j, part, order, h in pair:
                    e.wait_ge(zt_read, zb[j + 1] // 2)
                    if part == "lat":
                        butterfly_lat(e, steps, zt[h], xh[h], g_tmp[h])
                    else:
                        butterfly_ctx(e, steps, zt[h], xh[h])
                    e.sem_inc(xh_ready, 1)
                e.wait_ge(spec_in, 16 * (j // 2 + 1))
                for j, part, order, h in pair:
                    products(j, part, h)
                for j, part, order, h in pair:
                    t0, n = tok0[part], blocks[part] * P
                    e.wait_ge(yr_read, 2 * (j + 1))
                    (back_lat if part == "lat" else back_ctx)(yr[h], cv[h], i_tmp[h])
                    for c in range(2):
                        ct = 2 * h + c
                        fma(cv[h][:, c, 0:n], z[:, ct, t0:t0 + n],
                            k.hy_bias[:, order * CT + ct:order * CT + ct + 1], cv[h][:, c, 0:n])
                    e.wait_ge(gate_in, 16 * (j // 2 + 1))
                    e.tensor_tensor(z[:, 2 * h:2 * h + 2, t0:t0 + n], cv[h][:, :, 0:n],
                                    gate[:, 2 * h:2 * h + 2, t0:t0 + n], ALU.mult).then_inc(z_ready, 1)
                    e.wait_ge(z_ready, j + 1)



def gate_rows(k, layer, part):
    gates = k.mods[:, 96 * layer:96 * layer + 96].rearrange("p (m w) -> p m w", w=2)
    return gates[:, 8 * part:8 * part + 8, :]


def add_branch(k, e, s, m, gate, old, tokens):
    for n, (a, b) in enumerate(((0, LAT), (LAT, T))[:1 + (tokens > LAT)]):
        ins = e.scalar_tensor_tensor(out=k.x[:, m, a:b], in0=k.acc[s][:, a:b], scalar=gate(m, n),
                                     in1=old[:, m, a:b], op0=ALU.mult, op1=ALU.add)
    ins.then_inc(k.acc_free[s], 1)


def square_tile(k, e, s, m, use, base, sq, tokens):
    e.wait_ge(k.acc_free[s], use + 2)
    e.wait_ge(k.ss_done, base + m - 1)
    e.activation(sq[:, s, 0:tokens], k.x[:, m, 0:tokens], ACT.Square).then_inc(k.sq_ready, 1)


def sum_squares(k, e, cleared, base, sq, tokens):
    e.memset(k.ss[:, 0:tokens], 0.0).then_inc(cleared, 1)
    e.wait_ge(cleared, 1)
    with e.Fori(0, KT // 2) as i:
        for s in range(2):
            e.wait_ge(k.sq_ready, i * 2 + (base + s + 1))
            e.tensor_tensor(k.ss[:, 0:tokens], k.ss[:, 0:tokens], sq[:, s, 0:tokens],
                            ALU.add).then_inc(k.ss_done, 1)
            e.wait_ge(k.ss_done, i * 2 + (base + s + 1))


def even_out(k):
    nc, d, ph = k.nc, k.d, PH["ev_out"]
    w0, a0 = ph.w0, ph.a0
    base = k.sqs
    x_in, cleared, z_hi, z_ready = k.sem("ev_x_in"), k.sem("ev_cleared"), k.sem("ev_z_hi"), k.sem("ev_z_ready")
    z = k.at("h_z", R0, [P, CT, T])
    attT = k.at("attT", ATT0, [P, 4, T])
    sq = k.at("sq_ev", R0 + CT * T, [P, 2, T])
    source = lambda kk: z[:, kk, :] if kk < CT else attT[:, kk - CT, :]
    rows = gate_rows(k, 0, 2)
    with nc.Block() as block:
        @block.sync
        def _(e):
            e.dma_start(k.x[:, :, :], d["x"]).then_inc(x_in, 16)
            load_weights(k, e, ph)
            e.wait_ge(x_in, 16)

        @block.tensor
        def _(e):
            with e.Fori(0, ph.pairs) as i:
                for s in range(2):
                    item(k, e, s, i + w0, i + a0, k.rhs_h, T, ready=z_ready, base=0)

        @block.scalar
        def _(e):
            split_hi(k, e, 0, w0, k.acc_full[0], a0 + 1)
            for kk in range(KT):
                e.activation(k.h_hi[:, kk, :], source(kk), ACT.Copy).then_inc(z_hi, 1)
            with e.Fori(0, ph.pairs) as i:
                for s in range(2):
                    split_hi(k, e, 1 - s, i + (w0 + s), k.acc_full[1 - s], i + (a0 + 1 + s))
                    square_tile(k, e, s, i * 2 + s, i + a0, base, sq, T)

        @block.vector
        def _(e):
            split_lo(k, e, 0, w0)
            for kk in range(KT):
                e.wait_ge(z_hi, kk + 1)
                e.tensor_tensor(k.h_lo[:, kk, :], source(kk), k.h_hi[:, kk, :].bitcast(F32), ALU.subtract
                                ).then_inc(z_ready, 1)
            e.wait_ge(x_in, 16)
            with e.Fori(0, ph.pairs) as i:
                for s in range(2):
                    split_lo(k, e, 1 - s, i + (w0 + s))
                    e.wait_ge(k.acc_full[s], full(i + a0))
                    add_branch(k, e, s, i * 2 + s, lambda m, n: rows[:, m, n:n + 1], k.x, T)

        @block.gpsimd
        def _(e):
            sum_squares(k, e, cleared, base, sq, T)
    k.sqs += KT


def ffn(k, layer):
    nc, d, ph = k.nc, k.d, PH[f"ffn{layer}"]
    w0, a0, last = ph.w0, ph.a0, ph.last
    base = k.sqs
    tokens = T if layer == 0 else LAT
    norm = Norm(k, 2 * layer + 1)
    hid_hi = [k.at(f"hid_hi{n}", R0 + 2 * n * HG * T, [P, HG, T], F32R) for n in range(2)]
    hid_lo = [k.at(f"hid_lo{n}", R0 + (2 * n + 1) * HG * T, [P, HG, T], F32R) for n in range(2)]
    sg = k.at("silu_gate", R0 + 4 * HG * T, [P, T])
    hid = k.at("hid", R0 + 4 * HG * T + T, [P, T])
    sq = k.at("sq_ffn", R0 + 2 * HG * T, [P, 2, T])
    assert GROUPS % 2 == 1 and 4 * HG * T + 2 * T <= END - R0
    hid_ready, hi_done, lo_done = (k.sem(f"{n}{layer}") for n in ("ffn_hid", "ffn_hid_hi", "ffn_hid_lo"))
    cleared, stored, steps_sem = k.sem(f"ffn_cleared{layer}"), k.sem(f"ffn_stored{layer}"), k.sem(f"ffn_steps{layer}")
    rows = gate_rows(k, layer, 5)
    half = KT // 2
    in_at = lambda g: (g * 3 + (w0 - 1), g * 6 + (a0 - 4))
    out_at = lambda g: (g * 3 + (w0 + 4), g * 6 + (a0 + 4))
    end = GROUPS - 1
    end_at = (w0 + 3 * end + 2, a0 + 6 * end + 2)

    def schedule(e, take_in, take_out):
        take_in(0, 0, (w0, a0))
        with e.Fori(0, end // 2) as b:
            for n in range(2):
                g = b * 2 + n
                take_in(g + 1, (n + 1) % 2, in_at(g + 1))
                take_out(g, n, out_at(g), False)
        take_out(end, 0, end_at, True)

    with nc.Block() as block:
        @block.sync
        def _(e):
            load_weights(k, e, ph)

        @block.tensor
        def _(e):
            norm.tensor(k, e)

            def take_in(g, buf, at):
                for t in range(HG):
                    for s in range(2):
                        item(k, e, s, at[0] + t, at[1] + t, k.rhs_h, tokens, ready=k.h_ready, base=norm.h_base)

            def take_out(g, buf, at, ends):
                e.wait_ge(lo_done, g * HG + (HG + 1))
                rhs = lambda kk: (hid_hi[buf][:, kk, :], hid_lo[buf][:, kk, :])
                for m in range(KT):
                    s = m % 2
                    if m % half == 0:
                        e.wait_ge(k.split_lo[m // half], at[0] + 1)
                    e.wait_ge(k.acc_free[s], at[1] + (m // 2 + 1))
                    product(k, e, m // half, k.acc[s], HG, rhs, tokens, at=m % half * P, stride=half * P
                            ).then_inc(k.acc_full[s], 1)

            schedule(e, take_in, take_out)

        @block.scalar
        def _(e):
            norm.scalar(k, e)

            def take_in(g, buf, at):
                for t in range(HG):
                    split_hi(k, e, 1, at[0] + t, k.acc_full[1], at[1] + (t + 1))
                    e.wait_ge(k.acc_full[0], full(at[1] + t))
                    e.wait_ge(k.acc_free[1], at[1] + (t + 1))
                    e.activation(sg[:, 0:tokens], k.acc[0][:, 0:tokens], ACT.Silu).then_inc(k.acc_free[0], 1)
                    split_hi(k, e, 0, at[0] + (t + 1), k.acc_full[0], full(at[1] + t))
                    e.wait_ge(hid_ready, g * HG + (t + 1))
                    e.activation(hid_hi[buf][:, t, 0:tokens], hid[:, 0:tokens], ACT.Copy).then_inc(hi_done, 1)

            def take_out(g, buf, at, ends):
                split_hi(k, e, 1, at[0], k.acc_full[1], at[1] + 1)
                for m in range(KT):
                    s, use = m % 2, at[1] + m // 2
                    if m == half and not (ends and last):
                        split_hi(k, e, 0, at[0] + 1, k.acc_full[1], full(at[1] + (half // 2 - 1)))
                    if ends and not last:
                        square_tile(k, e, s, m, use, base, sq, tokens)
                    if ends and last:
                        e.wait_ge(k.acc_free[s], use + 2)
                        e.dma_start(d["out"][:, m, :], k.x[:, m, 0:LAT]).then_inc(stored, 16)
                if ends and last:
                    e.wait_ge(stored, 16 * KT)

            schedule(e, take_in, take_out)

        @block.vector
        def _(e):
            norm.vector(k, e, Steps(e, steps_sem))
            e.sem_inc(lo_done, 1)

            def take_in(g, buf, at):
                for t in range(HG):
                    split_lo(k, e, 1, at[0] + t)
                    split_lo(k, e, 0, at[0] + (t + 1))
                    e.wait_ge(k.acc_free[0], at[1] + (t + 2))
                    e.wait_ge(k.acc_full[1], full(at[1] + t))
                    e.wait_ge(lo_done, g * HG + (t + 1))
                    e.tensor_tensor(hid[:, 0:tokens], sg[:, 0:tokens], k.acc[1][:, 0:tokens],
                                    ALU.mult).then_inc(hid_ready, 1)
                    e.wait_ge(hid_ready, g * HG + (t + 1))
                    e.sem_inc(k.acc_free[1], 1)
                    e.wait_ge(hi_done, g * HG + (t + 1))
                    e.tensor_tensor(hid_lo[buf][:, t, 0:tokens], hid[:, 0:tokens],
                                    hid_hi[buf][:, t, 0:tokens].bitcast(F32), ALU.subtract).then_inc(lo_done, 1)

            def take_out(g, buf, at, ends):
                for s in range(2):
                    e.wait_ge(k.acc_free[s], at[1] + 1)
                split_lo(k, e, 1, at[0])
                for m in range(KT):
                    if m == half and not (ends and last):
                        split_lo(k, e, 0, at[0] + 1)
                    e.wait_ge(k.acc_full[m % 2], full(at[1] + m // 2))
                    add_branch(k, e, m % 2, m, lambda m, n: rows[:, m, n:n + 1], k.x, tokens)

            schedule(e, take_in, take_out)

        if not last:
            @block.gpsimd
            def _(e):
                e.wait_ge(k.stat_full, norm.n + 1)
                sum_squares(k, e, cleared, base, sq, tokens)
    if not last:
        k.sqs += KT



def rg_lru(k):
    nc, d, ph = k.nc, k.d, PH["rg_in"]
    w0, a0 = ph.w0, ph.a0
    norm = Norm(k, 2)
    y = k.at("y", X0, [P, RT, LAT])
    a = k.at("rg_a", R0, [P, 2, T])
    th = k.at("rg_th", R0 + 2 * T, [P, 2, T])
    rg = k.at("rg_g", R0 + 4 * T, [P, 4, T])
    xc = k.at("rg_xc", R0 + 8 * T, [P, T])
    gw = k.at("rg_gw", R0 + 9 * T, [P, 4, P])
    centre, conv, gw_in, steps_sem = k.sem("r_centre"), k.sem("r_conv"), k.sem("r_gw"), k.sem("r_steps")
    decay, root, v_ready, y_done, gelu_done = (k.sem("r_" + n) for n in ("decay", "root", "v", "y", "gelu"))
    mixed = k.sem("r_mixed")
    acts, sig, gated, kept = k.sem("r_acts"), k.sem("r_sigmoids"), k.sem("r_gated"), k.sem("r_x_kept")
    taps = k.rg_w[:, :].rearrange("p (m t) -> p m t", t=4)
    bias = k.rg_ba[:, :].rearrange("p (n g) -> p n g", g=4)
    exp_scale = k.rg_sp[:, 0:20].rearrange("p (n g) -> p n g", g=2)
    tanh_scale = k.rg_sp[:, 60:80].rearrange("p (n g) -> p n g", g=2)
    with nc.Block() as block:
        @block.sync
        def _(e):
            e.dma_start(d["x_kept"], k.x[:, :, 0:LAT]).then_inc(kept, 16)
            e.dma_start(gw[:, :, :], d["rg_gw"][0]).then_inc(gw_in, 16)
            with e.Fori(0, RT - 1) as i:
                load_next(k, e, i + w0)
                e.wait_ge(k.acc_full[1], full(i * 3 + (a0 + 2)))
                e.dma_start(gw[:, :, :], d["rg_gw"][i + 1]).then_inc(gw_in, 16)
            load_next(k, e, w0 + RT - 1)
            e.wait_ge(kept, 16)

        @block.tensor
        def _(e):
            norm.tensor(k, e)
            with e.Fori(0, RT) as i:
                item(k, e, 0, i + w0, i * 3 + a0, k.rhs_h, T, ready=k.h_ready, base=norm.h_base)
                item(k, e, 1, i + w0, i * 3 + a0, k.rhs_h, LAT)
                e.wait_ge(gw_in, i * 16 + 16)
                e.wait_ge(conv, i + 1)
                for g in range(4):
                    s = g % 2
                    e.wait_ge(k.acc_free[s], i * 3 + (a0 + 2 + g // 2))
                    for c, n in CHUNKS[T]:
                        mm = e.matmul(k.acc[s][:, c:c + n], gw[:, g, :], xc[:, c:c + n], start=True, stop=True)
                    mm.then_inc(k.acc_full[s], 1)

        @block.scalar
        def _(e):
            norm.scalar(k, e)
            e.wait_ge(kept, 16)
            e.sem_inc(y_done, 1)
            e.sem_inc(mixed, 1)

            def branches(i):
                e.wait_ge(k.acc_full[0], full(i * 3 + a0))
                e.activation(xc[:, :], k.acc[0][:, 0:T], ACT.Identity, scale=taps[:, i, 2:3],
                             bias=k.rg_b[:, bass.ds(i, 1)]).then_inc(centre, 1)
                split_hi(k, e, 0, i + (w0 + 1), k.acc_full[0], full(i * 3 + a0))
                e.wait_ge(k.acc_full[1], full(i * 3 + a0))
                e.activation(y[:, i, :], k.acc[1][:, 0:LAT], ACT.Gelu_apprx_tanh).then_inc(k.acc_free[1], 1)

            def gates(i, more):
                e.wait_ge(mixed, i + 1)
                for g in range(4):
                    s = g % 2
                    e.wait_ge(k.acc_full[s], full(i * 3 + (a0 + 1 + g // 2)))
                    e.activation(rg[:, g, :], k.acc[s][:, 0:T], ACT.Sigmoid, bias=bias[:, i, g:g + 1]
                                 ).then_inc(k.acc_free[s], 1)
                for s in range(2):
                    e.wait_ge(k.acc_free[s], i * 3 + (a0 + 4))
                e.sem_inc(sig, 1)
                e.wait_ge(y_done, i + 1)
                for dr in range(2):
                    e.activation(a[:, dr, :], rg[:, 2 * dr, :], ACT.Exp, scale=exp_scale[:, i, dr:dr + 1]).then_inc(acts, 1)
                    e.activation(th[:, dr, :], rg[:, 2 * dr, :], ACT.Tanh, scale=tanh_scale[:, i, dr:dr + 1]).then_inc(acts, 1)
                e.wait_ge(acts, i * 4 + 4)
                for dr in range(2):
                    e.activation(rg[:, 2 * dr, :], a[:, dr, :], ACT.Square).then_inc(decay, 1)
                if more:
                    split_hi(k, e, 1, i + (w0 + 1), k.acc_full[1], i * 3 + (a0 + 4))
                for dr in range(2):
                    e.wait_ge(v_ready, i * 2 + (dr + 1))
                    e.activation(th[:, dr, :], th[:, dr, :], ACT.Sqrt).then_inc(root, 1)
                if more:
                    e.wait_ge(gated, i + 1)
                    branches(i + 1)

            split_hi(k, e, 1, w0, k.acc_full[1], a0 + 1)
            branches(0)
            with e.Fori(0, RT - 1) as i:
                gates(i, True)
            gates(RT - 1, False)

        @block.vector
        def _(e):
            steps = Steps(e, steps_sem)
            norm.vector(k, e, steps)

            def convolution(i):
                e.wait_ge(centre, i + 1)
                n = 0
                for tap, sh in ((0, -2), (1, -1), (3, 1)):
                    for lo0, hi0 in ((0, LAT), (LAT, T)):
                        lo, hi = lo0 + max(0, -sh), hi0 - max(0, sh)
                        ins = e.scalar_tensor_tensor(out=xc[:, lo:hi], in0=k.acc[0][:, lo + sh:hi + sh],
                                                     scalar=taps[:, i, tap:tap + 1], in1=xc[:, lo:hi],
                                                     op0=ALU.mult, op1=ALU.add)
                        n += 1
                        if n < 6:
                            steps(ins, 1)
                        else:
                            ins.then_inc(k.acc_free[0], 1)
                steps.settle()
                e.wait_ge(k.acc_free[0], i * 3 + (a0 + 2))
                e.sem_inc(conv, 1)

            def block_of(i, more):
                e.wait_ge(sig, i + 1)
                for dr in range(2):
                    steps(e.tensor_tensor(rg[:, 2 * dr + 1, :], rg[:, 2 * dr + 1, :], xc[:, :], ALU.mult), 1 - dr)
                e.sem_inc(gated, 1)
                for dr in range(2):
                    e.wait_ge(decay, i * 2 + (dr + 1))
                    e.scalar_tensor_tensor(out=th[:, dr, :], in0=rg[:, 2 * dr, :], scalar=1.0, in1=th[:, dr, :],
                                           op0=ALU.add, op1=ALU.mult).then_inc(v_ready, 1)
                if more:
                    split_lo(k, e, 1, i + (w0 + 1))
                for dr in range(2):
                    e.wait_ge(root, i * 2 + (dr + 1))
                    steps(e.tensor_tensor(th[:, dr, :], th[:, dr, :], rg[:, 2 * dr + 1, :], ALU.mult), 1 - dr)
                e.sem_inc(mixed, 1)
                if more:
                    convolution(i + 1)
                    split_lo(k, e, 0, i + (w0 + 2))
                steps(e.tensor_tensor_scan(th[:, 0, LAT:T], a[:, 0, LAT:T], th[:, 0, LAT:T], 0.0, ALU.mult, ALU.add), 1)
                steps(e.tensor_tensor_scan(th[:, 1, ::-1], a[:, 1, ::-1], th[:, 1, ::-1], 0.0, ALU.mult, ALU.add), 1)
                steps(e.tensor_tensor_scan(th[:, 0, 0:LAT], a[:, 0, 0:LAT], th[:, 0, 0:LAT], th[:, 0, T - 1:T],
                                           ALU.mult, ALU.add))
                steps(e.tensor_tensor(th[:, 0, 0:LAT], th[:, 0, 0:LAT], th[:, 1, 0:LAT], ALU.add))
                steps(e.tensor_tensor(y[:, i, :], y[:, i, :], th[:, 0, 0:LAT], ALU.mult))
                e.sem_inc(y_done, 1)

            split_lo(k, e, 1, w0)
            convolution(0)
            split_lo(k, e, 0, w0 + 1)
            with steps.loop(RT - 1, 14) as i:
                block_of(i, True)
            block_of(RT - 1, False)


def rg_out(k):
    nc, d, ph = k.nc, k.d, PH["rg_out"]
    w0, a0 = ph.w0, ph.a0
    base = k.sqs
    x_in, cleared, y_hi_done, y_ready = k.sem("ro_x_in"), k.sem("ro_cleared"), k.sem("ro_y_hi"), k.sem("ro_y_ready")
    y = k.at("y", X0, [P, RT, LAT])
    y_hi = k.at("y_hi", H0, [P, RT, LAT], F32R)
    y_lo = k.at("y_lo", H0 + RT * LAT, [P, RT, LAT], F32R)
    x_old = k.at("x_old", R0, [P, KT, LAT])
    sq = k.at("sq_rg", R0 + KT * LAT, [P, 2, LAT])
    rows = gate_rows(k, 1, 2)
    half = RT // 2
    with nc.Block() as block:
        @block.sync
        def _(e):
            e.dma_start(x_old[:, :, :], d["x_kept"]).then_inc(x_in, 16)
            load_weights(k, e, ph)
            e.wait_ge(x_in, 16)

        @block.tensor
        def _(e):
            with e.Fori(0, KT // 2) as i:
                for s in range(2):
                    for h in range(2):
                        e.wait_ge(k.split_lo[h], i * 2 + (w0 + s + 1))
                        if h == 0:
                            e.wait_ge(k.acc_free[s], i + (a0 + 1))
                        rhs = lambda kk: (y_hi[:, h * half + kk, :], y_lo[:, h * half + kk, :])
                        product(k, e, h, k.acc[s], half, rhs, LAT, first=(h == 0), last=(h == 1), ready=y_ready,
                                base=h * half).then_inc(k.acc_full[s] if h else k.half_done, 1)

        @block.scalar
        def _(e):
            for kk in range(RT):
                e.activation(y_hi[:, kk, :], y[:, kk, :], ACT.Copy).then_inc(y_hi_done, 1)
            with e.Fori(0, KT // 2) as i:
                for s in range(2):
                    split_hi(k, e, 1, i * 2 + (w0 + s), k.acc_full[1 - s], i + (a0 + 1 + s))
                    split_hi(k, e, 0, i * 2 + (w0 + s + 1), k.half_done, i * 2 + (s + 1))
                    square_tile(k, e, s, i * 2 + s, i + a0, base, sq, LAT)

        @block.vector
        def _(e):
            for kk in range(RT):
                e.wait_ge(y_hi_done, kk + 1)
                e.tensor_tensor(y_lo[:, kk, :], y[:, kk, :], y_hi[:, kk, :].bitcast(F32), ALU.subtract
                                ).then_inc(y_ready, 1)
            e.wait_ge(x_in, 16)
            e.wait_ge(y_ready, RT)
            with e.Fori(0, KT // 2) as i:
                for s in range(2):
                    split_lo(k, e, 1, i * 2 + (w0 + s))
                    split_lo(k, e, 0, i * 2 + (w0 + s + 1))
                    e.wait_ge(k.acc_full[s], full(i + a0))
                    add_branch(k, e, s, i * 2 + s, lambda m, n: rows[:, m, n:n + 1], x_old, LAT)

        @block.gpsimd
        def _(e):
            sum_squares(k, e, cleared, base, sq, LAT)
    k.sqs += KT



def program(nc, dram):
    with ExitStack() as ctx:
        k = Kernel(nc, ctx, dram)
        k.coef_a = lambda n, who, kk: k.coef[:, (n * 2 + who) * 16 + kk:(n * 2 + who) * 16 + kk + 1]
        k.coef_b = lambda n, who, kk: k.coef[:, (n * 2 + who) * 16 + 8 + kk:(n * 2 + who) * 16 + 9 + kk]
        k.rhs_h = lambda kk: (k.h_hi[:, kk, :], k.h_lo[:, kk, :])
        prologue(k)
        even_in(k)
        latents(k)
        attention(k)
        hyena(k)
        even_out(k)
        ffn(k, 0)
        rg_lru(k)
        rg_out(k)
        ffn(k, 1)



def _tables():
    t0, q = np.arange(P)[:, None], np.arange(P)[None, :]
    fwd, inv = [], []
    for r in ORDER_LAT:
        ang = 2.0 * np.pi * (t0 * q / P + r * t0 / N_LAT)
        c, s = np.cos(ang), np.sin(ang)
        two = 1.0 if r in (0, 6) else 2.0
        if r in (0, 6):
            fwd += [c, -s]
            inv += [-s.T, c.T]
        else:
            fwd += [c, s, -s]
            inv += [-two * s.T, two * c.T, two * s.T]
    return tuple(np.concatenate(x, axis=1).astype(np.float32) for x in (fwd, inv))


def _filter_constants():
    zs, wins = [], []
    for length, n in ((LAT, N_LAT), (CTX, N_CTX)):
        kk = np.arange(length, dtype=np.float32)
        t = (kk / np.float32(max(length - 1, 1)))[:, None]
        bands = (EMB - 1) // 2
        ang = np.float32(2.0 * math.pi / length) * kk[:, None] * np.linspace(1e-4, bands - 1, bands, dtype=np.float32)[None, :]
        zs.append(np.concatenate([t, np.cos(ang), -np.sin(ang)], axis=-1).T)
        half = length // 2
        dist = np.abs(kk - half) / np.float32(max(half, 1))
        deltas = np.abs(np.linspace(math.log(1e-2) / 1.5, math.log(1e-2) / 0.3, D_HY, dtype=np.float32))
        wins.append((np.exp(-dist[:, None] * deltas[None, :]) / n).reshape(length // P, P, D_HY).transpose(1, 0, 2))
    return (np.ascontiguousarray(np.concatenate(zs, axis=1), dtype=np.float32),
            np.ascontiguousarray(np.concatenate(wins, axis=1), dtype=np.float32))


def _rope_tables():
    row = np.repeat(np.arange(LAT // GRID_W, dtype=np.float32), GRID_W)
    col = np.tile(np.arange(GRID_W, dtype=np.float32), LAT // GRID_W)
    inv = (np.float32(10000.0) ** (-np.arange(0, 16, 2, dtype=np.float32) / np.float32(16))).astype(np.float32)
    cos, sin = np.ones((T, ROPE), np.float32), np.zeros((T, ROPE), np.float32)
    for g, pos in enumerate((row, col)):
        ang = pos[:, None] * inv[None, :]
        c, s = np.cos(ang), np.sin(ang)
        cos[:LAT, 16 * g:16 * g + 16] = np.concatenate([c, c], axis=1)
        sin[:LAT, 16 * g:16 * g + 16] = np.concatenate([-s, s], axis=1)
    lay = lambda a: np.ascontiguousarray(a.reshape(NT, P, ROPE).transpose(1, 0, 2))
    return lay(cos), lay(sin)


def _tiles(w, m=P):
    kk, mm = w.shape
    return np.ascontiguousarray(w.reshape(kk // P, P, mm // m, m).transpose(2, 1, 0, 3))


def _ffn(a, l):
    fi = a["ffn_w_in"][l].reshape(KT, P, 2, GROUPS, HG, P).transpose(3, 4, 2, 1, 0, 5).reshape(GROUPS, HG, 2, P, WS)
    fo = a["ffn_w_out"][l].reshape(GROUPS, HG, P, 2, D // 2).transpose(0, 3, 2, 1, 4).reshape(GROUPS, 1, 2, P, WS)
    parts = [fi[0]]
    for g in range(GROUPS):
        parts += ([fi[g + 1]] if g + 1 < GROUPS else []) + [fo[g]]
    return np.concatenate(parts)


def _columns(v):
    v = np.asarray(v)
    return np.ascontiguousarray(v.reshape(-1, P).T)


def layout(inp):
    a = {n: np.asarray(v) for n, v in inp.items()}
    o = {}
    x = np.concatenate([a["x"][0], a["ctx"][0]], axis=0)
    o["x"] = np.ascontiguousarray(x.T.reshape(KT, P, T).transpose(1, 0, 2))
    o["cc"] = np.ascontiguousarray(np.stack([a["c"][0], a["c_ctx"]], -1).reshape(KT, P, 2).transpose(1, 0, 2).reshape(P, 16))
    aw = a["ada_w"].reshape(2, KT, P, ADA_LOADS // 2, ADA_M, P)
    o["ada_w"] = np.ascontiguousarray(aw.transpose(0, 3, 2, 1, 4, 5)).reshape(ADA_LOADS, P, KT, ADA_M * P)
    o["ada_b"] = _columns(a["ada_b"])
    o["gains"] = _columns(np.stack([a["norm1_g"][0], a["norm2_g"][0], a["norm1_g"][1], a["norm2_g"][1]]))
    ev = np.zeros((D, 18 * P), np.float32)
    ev[:, :a["ev_w_in"].shape[2]] = a["ev_w_in"][0]
    ri = a["rg_w_in"][0].reshape(KT, P, 2, RT, P)
    ri = ri[:, :, ::-1].transpose(3, 2, 1, 0, 4).reshape(RT, 2, P, WS)
    ro = a["rg_w_out"][0].reshape(2, RT // 2, P, KT, P)
    ro = ro.transpose(3, 0, 2, 1, 4).reshape(KT, 2, P, RT // 2 * P)
    ro = np.concatenate([ro, np.zeros((KT, 2, P, WS - RT // 2 * P), np.float32)], axis=-1)
    o["weights"] = np.ascontiguousarray(np.concatenate([
        _tiles(ev).reshape(9, 2, P, WS), _tiles(a["ev_w_out"][0]).reshape(4, 2, P, WS), _ffn(a, 0), ri, ro, _ffn(a, 1)]))
    assert len(o["weights"]) == ALL_PAIRS
    o["hy_w"] = np.ascontiguousarray(a["hy_short_w"][0].T.reshape(12, P, 3).transpose(1, 0, 2).reshape(P, 36))
    o["hy_b"] = _columns(a["hy_short_b"][0])
    o["hy_bias"] = _columns(a["hy_bias"][0])
    o["mlp"] = np.ascontiguousarray(np.stack([a["hy_b1"][0], a["hy_b2"][0], a["hy_freq"][0]], -1))
    o["hy_w1"], o["hy_w2"], o["hy_w3"] = a["hy_w1"][0], a["hy_w2"][0], a["hy_w3"][0]
    o["g_lat"] = _columns(np.concatenate([a["mla_q_norm_g"][0], a["mla_kv_norm_g"][0]]))
    o["w_uq"] = np.ascontiguousarray(a["mla_w_uq"][0].reshape(3, P, -1).transpose(1, 0, 2))
    o["w_ukv"] = np.ascontiguousarray(a["mla_w_ukv"][0].reshape(2, P, -1).transpose(1, 0, 2))
    o["gq"] = np.ascontiguousarray(np.broadcast_to(a["mla_qk_g_q"][0], (P, QD)))
    o["gk"] = np.ascontiguousarray(np.broadcast_to(a["mla_qk_g_k"][0], (P, QD)))
    o["rg_w"] = np.ascontiguousarray(a["rg_conv_w"][0].T.reshape(RT, P, 4).transpose(1, 0, 2).reshape(P, 40))
    o["rg_b"] = _columns(a["rg_conv_b"][0])
    gw = np.stack([a["rg_w_a"][0], a["rg_w_x"][0]], axis=1)
    o["rg_gw"] = np.ascontiguousarray(gw.transpose(2, 3, 0, 1, 4)).reshape(RT, P, 4, P)
    gb = np.stack([a["rg_b_a"][0], a["rg_b_x"][0]], axis=1).reshape(2, 2, RT, P)
    o["rg_ba"] = np.ascontiguousarray(gb.transpose(3, 2, 0, 1)).reshape(P, 40)
    o["rg_lam"] = np.ascontiguousarray(a["rg_lambda"][0].reshape(2, RT, P).transpose(2, 1, 0)).reshape(P, 20)
    o["tab_f"], o["tab_i"] = _tables()
    o["filter_z"], o["window"] = _filter_constants()
    o["cos"], o["sin"] = _rope_tables()
    o["ident"] = np.eye(P, dtype=np.float32)
    o["ones"] = np.ones((P, P), np.float32)
    return o


def build(nc, arrays):
    dram = {n: nc.dram_tensor("in_" + n, v.shape, mybir.dt.from_np(v.dtype), kind="ExternalInput").ap()
            for n, v in arrays.items()}
    dram["u"] = nc.dram_tensor("u_scratch", (12, P, T), F32, kind="Internal").ap()
    dram["x_kept"] = nc.dram_tensor("x_kept", (P, KT, LAT), F32, kind="Internal").ap()
    dram["spec_lat"] = nc.dram_tensor("spec_lat", (2, P, 14, D_HY), F32, kind="Internal").ap()
    dram["spec_ctx"] = nc.dram_tensor("spec_ctx", (2, P, 4, D_HY), F32, kind="Internal").ap()
    dram["out"] = nc.dram_tensor("out_0", (P, KT, LAT), F32, kind="ExternalOutput").ap()
    program(nc, dram)


def kernel(**inputs):
    import concourse.bacc as bacc
    from concourse.bass_utils import run_bass_kernel_spmd

    nc = bacc.Bacc("TRN2", target_bir_lowering=False, num_devices=1)
    arrays = layout(inputs)
    build(nc, arrays)
    r = run_bass_kernel_spmd(nc, [{"in_" + n: v for n, v in arrays.items()}], core_ids=[0])
    out = r.results[0]["out_0"]
    return np.ascontiguousarray(out.transpose(1, 0, 2).reshape(D, LAT).T)[None]
```
